# Optimizing a Trainium2 kernel written in Bass

```python
import jax, jax.numpy as jnp
from jax import lax
import numpy as np

D_MODEL = 1024
BATCH = 1
SEQ = 1024
DEPTH = 1
DEC_BATCH = 8
DEC_SEQ = 16
PAST_LEN = 512

CHUNK = 64
RET_HEADS = 4
RET_DK = D_MODEL // RET_HEADS
RET_DV = D_MODEL // RET_HEADS
HG_DK = 128
HG_HEADS = D_MODEL // HG_DK
HG_DV = D_MODEL // HG_HEADS
HG_BLOCK = 16
D_FF = 4 * D_MODEL
ROPE_BASE = 10000.0
EPS = 1e-6

RET_QK = RET_HEADS * RET_DK
RET_V = RET_HEADS * RET_DV
HG_QK = HG_HEADS * HG_DK
HG_V = HG_HEADS * HG_DV
IN_SIZES = (RET_QK, RET_QK, RET_V, RET_V, HG_QK, HG_QK, HG_V, HG_V, D_MODEL, D_MODEL)
D_IN = RET_QK * 2 + RET_V * 2 + HG_QK * 2 + HG_V * 2 + D_MODEL * 2

kernel_name = 'retnet_hgrn2_gated_parallel_stream'

def _rms_norm(x, g):
    xf = x.astype(jnp.float32)
    y = xf * lax.rsqrt(jnp.mean(xf * xf, axis=-1, keepdims=True) + EPS)
    return (y * g.astype(jnp.float32)).astype(x.dtype)

def _head_rms(x):
    return x * lax.rsqrt(jnp.mean(x * x, axis=-1, keepdims=True) + EPS)

def _split_cols(z):
    offs = np.cumsum(IN_SIZES)[:-1].tolist()
    return jnp.split(z, offs, axis=-1)

def _ret_log_gamma():
    g = 1.0 - np.exp(np.linspace(np.log(1.0 / 32), np.log(1.0 / 512), RET_HEADS))
    return jnp.asarray(np.log(g), dtype=jnp.float32)

def _rope(x, pos):
    d = x.shape[-1]
    inv = ROPE_BASE ** (-jnp.arange(0, d, 2, dtype=jnp.float32) / d)
    ang = pos.astype(jnp.float32)[:, None] * inv[None, :]
    cos = jnp.cos(ang)[None, :, None, :]
    sin = jnp.sin(ang)[None, :, None, :]
    x1, x2 = x[..., : d // 2], x[..., d // 2:]
    return jnp.concatenate([x1 * cos - x2 * sin, x1 * sin + x2 * cos], axis=-1)

def _retention(q, k, v, s0, chunk):
    B, T, H, dk = q.shape
    dv = v.shape[-1]
    n = T // chunk
    lg = _ret_log_gamma()
    idx = jnp.arange(chunk, dtype=jnp.float32)
    dmat = jnp.exp(jnp.abs(idx[:, None] - idx[None, :])[None] * lg[:, None, None])
    xi = jnp.exp((idx + 1.0)[:, None] * lg[None, :])
    zeta = jnp.exp((chunk - 1.0 - idx)[:, None] * lg[None, :])
    dec_c = jnp.exp(chunk * lg)
    qc = q.reshape(B, n, chunk, H, dk)
    kc = k.reshape(B, n, chunk, H, dk)
    vc = v.reshape(B, n, chunk, H, dv)
    scores = jnp.einsum('bnqhd,bnkhd->bnhqk', qc, kc) * dmat[None, None]
    intra = jnp.einsum('bnhqk,bnkhe->bnqhe', scores, vc)
    qx = jnp.moveaxis(qc * xi[None, None, :, :, None], 1, 0)
    kz = jnp.moveaxis(kc * zeta[None, None, :, :, None], 1, 0)
    vs = jnp.moveaxis(vc, 1, 0)

    def step(s, inp):
        q_i, k_i, v_i = inp
        cross = jnp.einsum('bchd,bhde->bche', q_i, s)
        s_new = dec_c[None, :, None, None] * s + jnp.einsum('bchd,bche->bhde', k_i, v_i)
        return s_new, cross

    s_last, cross = lax.scan(step, s0, (qx, kz, vs))
    out = intra + jnp.moveaxis(cross, 0, 1)
    return out.reshape(B, T, H, dv), s_last

def _hgrn2(q, k, v, logf, s0, block):
    B, T, H, dk = q.shape
    dv = v.shape[-1]
    n = T // block
    to_blocks = lambda a: jnp.moveaxis(a.reshape(B, n, block, H, a.shape[-1]), 1, 0)
    tri = jnp.tril(jnp.ones((block, block), dtype=bool))

    def step(s, inp):
        q_i, k_i, v_i, lf_i = inp
        b = jnp.cumsum(lf_i, axis=1)
        inter = jnp.einsum('bthd,bhde->bthe', q_i * jnp.exp(b), s)
        diff = b[:, :, None] - b[:, None, :]
        diff = jnp.where(tri[None, :, :, None, None], diff, -jnp.inf)
        att = jnp.einsum('bthd,btshd->bhts', q_i, jnp.exp(diff) * k_i[:, None])
        intra = jnp.einsum('bhts,bshe->bthe', att, v_i)
        b_last = b[:, -1]
        k_dec = k_i * jnp.exp(b_last[:, None] - b)
        s_new = jnp.exp(b_last)[..., None] * s + jnp.einsum('bshd,bshe->bhde', k_dec, v_i)
        return s_new, inter + intra

    s_last, out = lax.scan(step, s0, (to_blocks(q), to_blocks(k), to_blocks(v), to_blocks(logf)))
    return jnp.moveaxis(out, 0, 1).reshape(B, T, H, dv), s_last

def _layer(x, pos, s_ret, s_hg, lb, w_in, w_a, w_b, w_out, w_up, w_down,
           g_pre_mix, g_post_mix, g_pre_ffn, g_post_ffn, ret_chunk, hg_block):
    B, T, _ = x.shape
    f32 = jnp.float32
    h = _rms_norm(x, g_pre_mix)
    z = h @ w_in
    q_a, k_a, v_a, g_a, q_b, f_b, i_b, g_b, m_a, m_b = _split_cols(z)

    qa = _rope(q_a.astype(f32).reshape(B, T, RET_HEADS, RET_DK), pos)
    ka = _rope(k_a.astype(f32).reshape(B, T, RET_HEADS, RET_DK), pos) * (RET_DK ** -0.5)
    va = v_a.astype(f32).reshape(B, T, RET_HEADS, RET_DV)
    o_a, s_ret_new = _retention(qa, ka, va, s_ret, ret_chunk)
    o_a = _head_rms(o_a).reshape(B, T, RET_V)
    y_a = (jax.nn.silu(g_a.astype(f32)) * o_a).astype(x.dtype) @ w_a

    lbh = lb.reshape(HG_HEADS, HG_DK)
    f = lbh + (1.0 - lbh) * jax.nn.sigmoid(f_b.astype(f32).reshape(B, T, HG_HEADS, HG_DK))
    qb = q_b.astype(f32).reshape(B, T, HG_HEADS, HG_DK)
    vb = i_b.astype(f32).reshape(B, T, HG_HEADS, HG_DV)
    o_b, s_hg_new = _hgrn2(qb, 1.0 - f, vb, jnp.log(f), s_hg, hg_block)
    o_b = _head_rms(o_b).reshape(B, T, HG_V)
    y_b = (jax.nn.silu(g_b.astype(f32)) * o_b).astype(x.dtype) @ w_b

    mix = jax.nn.sigmoid(m_a) * y_a + jax.nn.sigmoid(m_b) * y_b
    x = x + _rms_norm(mix @ w_out, g_post_mix)

    u = jnp.square(jax.nn.relu(_rms_norm(x, g_pre_ffn) @ w_up))
    x = x + _rms_norm(u @ w_down, g_post_ffn)
    return x, s_ret_new, s_hg_new

def setup_inputs(seed: int = 0) -> dict:
    key = jax.random.key(seed)
    ks = jax.random.split(key, 16)
    f32 = jnp.float32
    nrm = lambda k, shape, s: jax.random.normal(k, shape, f32) * s
    return {
        'x_prompt': nrm(ks[0], (BATCH, SEQ, D_MODEL), 1.0),
        'x_sample': nrm(ks[1], (DEC_BATCH, DEC_SEQ, D_MODEL), 1.0),
        'state_ret': nrm(ks[2], (DEPTH, DEC_BATCH, RET_HEADS, RET_DK, RET_DV), 0.5),
        'state_hgrn': nrm(ks[3], (DEPTH, DEC_BATCH, HG_HEADS, HG_DK, HG_DV), 0.5),
        'lb_logits': nrm(ks[4], (DEPTH + 1, HG_QK), 0.5),
        'w_in': nrm(ks[5], (DEPTH, D_MODEL, D_IN), D_MODEL ** -0.5),
        'w_a': nrm(ks[6], (DEPTH, RET_V, D_MODEL), RET_V ** -0.5),
        'w_b': nrm(ks[7], (DEPTH, HG_V, D_MODEL), HG_V ** -0.5),
        'w_out': nrm(ks[8], (DEPTH, D_MODEL, D_MODEL), D_MODEL ** -0.5),
        'w_up': nrm(ks[9], (DEPTH, D_MODEL, D_FF), D_MODEL ** -0.5),
        'w_down': nrm(ks[10], (DEPTH, D_FF, D_MODEL), D_FF ** -0.5),
        'g_pre_mix': 1.0 + nrm(ks[11], (DEPTH, D_MODEL), 0.05),
        'g_post_mix': 1.0 + nrm(ks[12], (DEPTH, D_MODEL), 0.05),
        'g_pre_ffn': 1.0 + nrm(ks[13], (DEPTH, D_MODEL), 0.05),
        'g_post_ffn': 1.0 + nrm(ks[14], (DEPTH, D_MODEL), 0.05),
    }

def reference(x_prompt, x_sample, state_ret, state_hgrn, lb_logits, w_in, w_a, w_b, w_out,
              w_up, w_down, g_pre_mix, g_post_mix, g_pre_ffn, g_post_ffn):
    f32 = jnp.float32
    lb_all = jnp.cumsum(jax.nn.softmax(lb_logits.astype(f32), axis=0), axis=0)
    B, T, _ = x_prompt.shape
    Bs, Ts, _ = x_sample.shape
    pos_p = jnp.arange(T, dtype=jnp.int32)
    pos_s = PAST_LEN + jnp.arange(Ts, dtype=jnp.int32)
    xp, xs = x_prompt, x_sample
    ret_p, hg_p, ret_s, hg_s = [], [], [], []
    for l in range(DEPTH):
        weights = (lb_all[l], w_in[l], w_a[l], w_b[l], w_out[l], w_up[l], w_down[l],
                   g_pre_mix[l], g_post_mix[l], g_pre_ffn[l], g_post_ffn[l])
        zr = jnp.zeros((B, RET_HEADS, RET_DK, RET_DV), f32)
        zh = jnp.zeros((B, HG_HEADS, HG_DK, HG_DV), f32)
        xp, sr, sh = _layer(xp, pos_p, zr, zh, *weights, CHUNK, HG_BLOCK)
        ret_p.append(sr)
        hg_p.append(sh)
        xs, sr2, sh2 = _layer(xs, pos_s, state_ret[l].astype(f32), state_hgrn[l].astype(f32),
                              *weights, Ts, Ts)
        ret_s.append(sr2)
        hg_s.append(sh2)
    return (xp, xs,
            jnp.stack(ret_p).astype(x_prompt.dtype), jnp.stack(hg_p).astype(x_prompt.dtype),
            jnp.stack(ret_s).astype(state_ret.dtype), jnp.stack(hg_s).astype(state_hgrn.dtype))


_drawn_inputs = setup_inputs


def setup_inputs(seed=0):
    import zlib

    import numpy as np

    out = dict(_drawn_inputs(seed))
    spreads = {}
    factors = {}
    for name, (base, spread) in spreads.items():
        noise = np.random.default_rng([zlib.crc32(name.encode()), seed]).standard_normal(out[name].shape)
        drawn = base * np.exp(spread * noise) if base else spread * noise
        out[name] = __import__('jax').numpy.asarray(drawn.astype(out[name].dtype))
    for name, factor in factors.items():
        out[name] = (out[name] * factor).astype(out[name].dtype)
    return out
```

```python
import concourse.bass as bass
from concourse import mybir
from contextlib import ExitStack

F32 = mybir.dt.float32
F32R = mybir.dt.float32r
U32 = mybir.dt.uint32
ALU = mybir.AluOpType
ACT = mybir.ActivationFunctionType

P = 128
D = 1024
KT = D // P
TP = 1024
NS, TS = 8, 16
T = TP + NS * TS
NT = T // P
NTP = TP // P
CH = T // 3
NC = 3
TPC = NT // NC
RH, RD = 4, 256
HH, HD = 8, 128
FF = 4 * D
DIN = 10 * D
LEV = 7
LEVS = 4
PAST = 512
EPS = 1e-6

RET_SLOTS = 8 * NC
HG_BLOCKS = 5
HG_SLOTS = HG_BLOCKS * NC
RA, RB_ = 4, 5
R_NORM = (11, 17, 22)
H_NORM = (8, 11, 13)


class Chain:

    def __init__(self, eng, sem):
        self.eng, self.sem, self.n = eng, sem, 0

    def __call__(self, ins):
        self.n += 1
        ins.then_inc(self.sem, 1)
        self.eng.wait_ge(self.sem, self.n)

    def reset(self):
        self.eng.sem_clear(self.sem)
        self.n = 0


def program(nc, a, o, scr):
    ctx = ExitStack()
    with ctx:
        def sem(name):
            return ctx.enter_context(nc.semaphore(name))

        def sb(name, shape, dt=F32, stack=ctx):
            return stack.enter_context(nc.sbuf_tensor(name, shape, dt))

        XH, XL = sb("XH", [P, KT, T], F32R), sb("XL", [P, KT, T], F32R)
        WRAW = [sb(f"WRAW{i}", [P, 1024]) for i in range(2)]
        WHI = [sb(f"WHI{i}", [P, KT, P], F32R) for i in range(2)]
        WLO = [sb(f"WLO{i}", [P, KT, P], F32R) for i in range(2)]
        ident = sb("ident", [P, P])
        gcol = sb("gcol", [P, 2, KT])
        mhalf = sb("mhalf", [P, 1])
        LB = sb("LB", [P, 2, HH])
        LBM = sb("LBM", [P, HH])
        LBC = sb("LBC", [P, 2, HH])
        ssc = sb("ssc", [P, 2 * NT])
        msc = sb("msc", [P, 2 * NT])
        rsc = sb("rsc", [P, 2 * NT])
        dss, dms, drs = sb("dss", [P, 2 * NT]), sb("dms", [P, NT]), sb("drs", [P, NT])
        yss, yms, yrs = (sb(n, [P, NT]) for n in ("yss", "yms", "yrs"))
        psum = [ctx.enter_context(nc.psum_tensor(f"bank{i}", [P, 512], F32)) for i in range(8)]
        PT, PSC, PRB, PO, PST = psum[3], psum[4], psum[5], psum[6], psum[7]

        p0 = ExitStack()
        XR = [sb(f"XR{i}", [P, D], F32, p0) for i in range(2)]
        HR = [sb(f"HR{i}", [P, D], F32, p0) for i in range(2)]
        TM = [sb(f"TM{i}", [P, 4, P], F32, p0) for i in range(2)]
        SQJ = sb("SQJ", [P, D], F32, p0)
        p0.close()

        pa = ExitStack()
        ZST = [sb(f"ZST{i}", [P, T], F32, pa) for i in range(2)]
        KVT = [sb(f"KVT{i}", [P, 2, 256], F32, pa) for i in range(2)]
        ATT = [sb(f"ATT{i}", [P, P], F32, pa) for i in range(2)]
        SQ = sb("SQ", [P, 2, CH], F32, pa)
        SG = sb("SG", [P, 2, CH], F32, pa)
        MS = sb("MS", [P, TPC], F32, pa)
        RST = sb("RST", [P, TPC], F32, pa)
        DG = sb("DG", [P, TPC, P], F32, pa)
        UB = sb("UB", [P, 2, CH], F32, pa)
        ones = sb("ones", [P, P], F32, pa)
        MK = sb("MK", [P, LEV, 64], U32, pa)
        RM = sb("RM", [P, NS], F32, pa)

        pr = ExitStack()
        ZQ = sb("ZQ", [P, 2, T], F32, pr)
        ZK = sb("ZK", [P, 2, T], F32, pr)
        ZV = sb("ZV", [P, 2, T], F32, pr)
        ZG = [sb(f"ZG{i}", [P, 2, CH], F32, pr) for i in range(2)]
        QR = sb("QR", [P, 2, T], F32, pr)
        KR = sb("KR", [P, 2, T], F32, pr)
        QX = ZQ
        RTMP = sb("RTMP", [P, 2, CH], F32, pr)
        PTMP = sb("PTMP", [P, 2, CH], F32, pr)
        CS = sb("CS", [P, 2, T], F32, pr)
        HC = sb("HC", [P, 4 * P + 12], F32, pr)
        XI = HC[:, 0:2 * P].rearrange("p (a n) -> p a n", a=2)
        DM = HC[:, 2 * P:4 * P].rearrange("p (a n) -> p a n", a=2)
        ZETA, G128, G16 = (HC[:, 4 * P + i:4 * P + i + 1] for i in range(3))
        SR = sb("SR", [P, 2, RD], F32, pr)
        S8B = sb("S8B", [P, 4, 2, RD], F32, pr)
        S8A = ZK[:, :, :].rearrange("p a t -> p (a t)")[:, 0:4 * 2 * RD].rearrange("p (b d e) -> p b d e", b=4, d=2)
        KZ8 = [sb(f"KZ8{i}", [P, RD], F32, pr) for i in range(2)]
        pr.close()

        ph = ExitStack()
        HZ = [sb(f"HZ{i}", [P, T], F32, ph) for i in range(4)]
        FG = HZ[1]
        KK, PP, RR = (sb(n, [P, T], F32, ph) for n in ("KK", "PP", "RR"))
        QP, KRH = (sb(n, [P, T], F32, ph) for n in ("QP", "KRH"))
        OH = QP
        QE = [sb(f"QE{i}", [P, LEV, CH // 2], F32, ph) for i in range(2)]
        KE = [sb(f"KE{i}", [P, LEV, CH], F32, ph) for i in range(2)]
        FT = sb("FT", [P, CH], F32, ph)
        SH = sb("SH", [P, HD], F32, ph)
        SH8 = sb("SH8", [P, NS, HD], F32, ph)
        KM8 = [sb(f"KM8{i}", [P, HD], F32, ph) for i in range(2)]
        ph.close()
        pa.close()

        pb = ExitStack()
        MIX = sb("MIX", [P, KT, T], F32, pb)
        MG = [sb(f"MG{i}", [P, T], F32, pb) for i in range(2)]
        pb1 = ExitStack()
        URAW = [sb(f"URAW{i}", [P, T], F32, pb1) for i in range(2)]
        pb1.close()
        pb.close()

        pd = ExitStack()
        sb("hold_mix", [P, KT, T], F32, pd)
        sb("hold_mg", [P, 2, T], F32, pd)
        WOH, WOL = sb("WOH", [P, KT, D], F32R, pd), sb("WOL", [P, KT, D], F32R, pd)
        pd.close()
        pd2 = ExitStack()
        XI2 = [sb(f"XI2{i}", [P, D], F32, pd2) for i in range(2)]
        X1R = [sb(f"X1R{i}", [P, D], F32, pd2) for i in range(2)]
        HR2 = [sb(f"HR2{i}", [P, D], F32, pd2) for i in range(2)]
        TM2 = [sb(f"TM2{i}", [P, 4, P], F32, pd2) for i in range(2)]
        SQJ2 = sb("SQJ2", [P, D], F32, pd2)
        GB = sb("GB", [P, D], F32, pd2)
        pd2.close()
        pe_ = ExitStack()
        UH, UL = sb("UH", [P, 4, T], F32R, pe_), sb("UL", [P, 4, T], F32R, pe_)
        ACC = sb("ACC", [P, NT, D], F32, pe_)
        WDH, WDL = sb("WDH", [P, 4, D], F32R, pe_), sb("WDL", [P, 4, D], F32R, pe_)
        T1 = [sb(f"T1{i}", [P, CH], F32, pe_) for i in range(2)]
        T2 = [sb(f"T2{i}", [P, CH], F32, pe_) for i in range(2)]
        pe_.close()
        pf = ExitStack()
        GF, SQJ3 = sb("GF", [P, D], F32, pf), sb("SQJ3", [P, D], F32, pf)
        X1F = [sb(f"X1F{i}", [P, D], F32, pf) for i in range(2)]
        OF = [sb(f"OF{i}", [P, D], F32, pf) for i in range(2)]
        pf.close()

        w_raw = [sem("w_raw0"), sem("w_raw1")]
        w_hi, w_lo = sem("w_hi"), sem("w_lo")
        mm = sem("mm")
        ev = sem("ev")
        z_st = [sem("z_st0"), sem("z_st1")]
        c_in = sem("c_in")
        c_in2 = sem("c_in2")
        lb_ch, lb_e = sem("lb_ch"), sem("lb_e")
        act_ch, dve_ch, pool_ch = sem("act_ch"), sem("dve_ch"), sem("pool_ch")
        x_in = [sem("x_in0"), sem("x_in1")]
        n_ss, n_ms, n_rs, n_hr = sem("n_ss"), sem("n_ms"), sem("n_rs"), sem("n_hr")
        n_tp, n_tm, n_xh, n_xl = sem("n_tp"), sem("n_tm"), sem("n_xh"), sem("n_xl")

        class Heads:

            def __init__(self, k):
                self.in_ = [sem(f"{k}_in{i}") for i in range(4)]
                self.g_in = [sem(f"{k}_g_in0"), sem(f"{k}_g_in1")]
                self.s8_in = [sem(f"{k}_s8_in0"), sem(f"{k}_s8_in1")]
                self.q_ok, self.k_ok = sem(f"{k}_q_ok"), sem(f"{k}_k_ok")
                self.f_ok, self.fk = sem(f"{k}_f_ok"), sem(f"{k}_fk")
                self.t_full, self.kv = sem(f"{k}_t_full"), sem(f"{k}_kv")
                self.sc, self.att = sem(f"{k}_sc"), sem(f"{k}_att")
                self.o_full, self.o_ev = sem(f"{k}_o_full"), sem(f"{k}_o_ev")
                self.st_full, self.st_ev = sem(f"{k}_st_full"), sem(f"{k}_st_ev")
                self.kz8 = sem(f"{k}_kz8")
                self.sq, self.rb, self.ms = sem(f"{k}_sq"), sem(f"{k}_rb"), sem(f"{k}_ms")
                self.sg, self.w_ok, self.u_ok = sem(f"{k}_sg"), sem(f"{k}_w_ok"), sem(f"{k}_u_ok")
                self.rs, self.dg, self.rbb, self.gt = (sem(f"{k}_{x}") for x in ("rs", "dg", "rbb", "gt"))
                self.u_st, self.sr_st = sem(f"{k}_u_st"), sem(f"{k}_sr_st")
                self.s8_st = [sem(f"{k}_s8_st0"), sem(f"{k}_s8_st1")]

        R, H = Heads("r"), Heads("h")
        ur_in = [sem("ur_in0"), sem("ur_in1")]
        mg_in = [sem("mg_in0"), sem("mg_in1")]
        sp_hi, sp_lo = sem("sp_hi"), sem("sp_lo")
        mg_ok = sem("mg_ok")
        mtm_ok = sem("mtm_ok")
        gb_in, xi_in = sem("gb_in"), [sem("xi_in0"), sem("xi_in1")]
        d_mm, d_ss, d_ms, d_rs, d_x1 = sem("d_mm"), sem("d_ss"), sem("d_ms"), sem("d_rs"), sem("d_x1")
        x1_st = [sem("x1_st0"), sem("x1_st1")]
        f_t1, f_t2, f_uh, f_ul = sem("f_t1"), sem("f_t2"), sem("f_uh"), sem("f_ul")
        dn, dn_ev = sem("dn"), sem("dn_ev")
        acc0 = sem("acc0")
        x1_in = [sem("x1_in0"), sem("x1_in1")]
        y_ss, y_ms, y_rs, y_ok = sem("y_ss"), sem("y_ms"), sem("y_rs"), sem("y_ok")
        y_st = [sem("y_st0"), sem("y_st1")]

        zs, us, x1s = scr["z"], scr["u"], scr["x1"]
        NRB = 10 * KT
        NB1 = NRB + 2 * KT
        W_OUT = NB1
        W_FFN = W_OUT + KT

        def half(n):
            return n // 2, n % 2

        def z_block(n):
            if n < 32:
                h, j = divmod(n, 8)
                return (j // 2) * D + h * RD + (j % 2) * P, n
            if n < 40:
                h, j = divmod(n - 32, 4)
                return (4 + j) * D + h * HD, n
            i, j = divmod(n - 40, HG_BLOCKS)
            if i < 6 and j < 4:
                return (4 + j) * D + (i + 2) * HD, 40 + 4 * i + j
            mi = i if i < 6 else 6 + (n - 70)
            return 8 * D + mi * P, 64 + mi

        def w_src(w):
            if w < NRB:
                c = z_block(w)[0]
                return a["w_in"][0, :, c:c + P].rearrange("(k p) n -> p k n", p=P)
            name = "w_a" if w < NRB + KT else "w_b"
            c = ((w - NRB) % KT) * P
            return a[name][0, :, c:c + P].rearrange("(k p) n -> p k n", p=P)

        def as_block(t):
            return t[:, :].rearrange("p (k n) -> p k n", k=KT)

        def plain(x):
            return x.bitcast(F32)

        def y_store(sp, t):
            sp.wait_ge(y_ok, t + 1)
            dst = o["y_p"][0, t * P:(t + 1) * P, :] if t < NTP else o["y_s"].rearrange("b t d -> (b t) d")
            sp.dma_start(dst, OF[t % 2][:, :]).then_inc(y_st[t % 2], 16)

        def ret_done(e):
            e.wait_ge(R.u_st, 16 * 3 * RH + 16)
            e.wait_ge(R.sr_st, 16 * RH + 16)
            for s in R.s8_st:
                e.wait_ge(s, 32 * RH + 16)

        def hg_done(e):
            e.wait_ge(H.u_st, 16 * 3 * HH + 16)
            e.wait_ge(H.sr_st, 16 * HH + 16)
            e.wait_ge(H.s8_st[0], 16 * HH + 16)
            for q in range(2):
                e.wait_ge(z_st[q], 16 * NRB // 2)

        block = ctx.enter_context(nc.Block())

        @block.sync
        def _(sp):
            def load_w(w):
                m, p = half(w)
                if w >= 2:
                    sp.wait_ge(w_lo, w - 1)
                sp.dma_start(as_block(WRAW[p]), w_src(w)).then_inc(w_raw[p], 16)

            def store_z(n):
                m, p = half(n)
                sp.wait_ge(ev, NC * n + NC)
                sp.dma_start(zs[z_block(n)[1]], ZST[p][:, :]).then_inc(z_st[p], 16)

            def z_stored(n):
                for q in (n, n - 1):
                    if q >= 0:
                        sp.wait_ge(z_st[q % 2], 16 * (q // 2 + 1))

            def rows(tt, dst, s):
                src = a["x_prompt"][0, tt * P:(tt + 1) * P, :] if tt < NTP else \
                    a["x_sample"].rearrange("b t d -> (b t) d")
                sp.dma_start(dst[:, :], src).then_inc(s, 16)

            rows(0, XR[0], x_in[0])
            rows(1, XR[1], x_in[1])
            sp.dma_start(ident[:, :], a["c_ident"]).then_inc(c_in, 16)
            sp.dma_start(gcol[:, :, :], a["g_pre_cols"]).then_inc(c_in, 16)
            sp.dma_start(LB[:, :, :], a["lb_cols"]).then_inc(c_in, 16)
            load_w(0)
            load_w(1)
            for tt in range(2, NT):
                sp.wait_ge(n_hr, tt - 1)
                rows(tt, XR[tt % 2], x_in[tt % 2])
            sp.wait_ge(n_xl, 2 * NT)
            sp.wait_ge(n_xh, 2 * NT)
            sp.dma_start(CS[:, :, :], a["c_rope"]).then_inc(c_in2, 16)
            sp.dma_start(MK[:, :, :], a["c_mask"]).then_inc(c_in2, 16)
            sp.dma_start(RM[:, :], a["c_rows"]).then_inc(c_in2, 16)
            for s in (R.u_st, R.sr_st, *R.s8_st, H.u_st, H.sr_st, *H.s8_st):
                sp.sem_inc(s, 16)

            for n in range(8):
                load_w(n + 2)
                if n:
                    store_z(n - 1)

            for h in range(RH):
                for j in range(8):
                    n = 8 + 8 * h + j
                    load_w(n + 2)
                    store_z(n - 1)
                    if j == 0:
                        z_stored(n - 1)
                        if h:
                            sp.wait_ge(R.o_ev, 9 * h + 1)
                            sp.wait_ge(R.u_ok, 3 * h + 1)
                            sp.wait_ge(R.st_ev, 16 * h + 1)
                        z = zs[8 * h:8 * h + 8].rearrange("(g e) p t -> g p e t", e=2)
                        sp.dma_start(HC[:, :], a["c_ret"][h]).then_inc(R.in_[3], 16)
                        sp.dma_start(ZQ[:, :, :], z[0]).then_inc(R.in_[0], 16)
                        if h:
                            sp.wait_ge(R.s8_st[0], 32 * h + 16)
                        sp.dma_start(ZK[:, :, :], z[1]).then_inc(R.in_[1], 16)
                        sp.dma_start(ZV[:, :, :], z[2]).then_inc(R.in_[2], 16)
                        if h:
                            sp.wait_ge(R.s8_st[1], 32 * h + 16)
                        for d in range(2):
                            sp.dma_start(S8B[:, :, d, :], a["state_ret"][0, 4:8, h, d * P:(d + 1) * P, :]
                                         .rearrange("b p e -> p b e")).then_inc(R.s8_in[1], 16)
                        for c in range(2):
                            sp.dma_start(ZG[c][:, :, :], z[3][:, :, c * CH:(c + 1) * CH]).then_inc(R.g_in[c], 16)
                    if j == 2:
                        sp.wait_ge(R.k_ok, h + 1)
                        sp.wait_ge(R.q_ok, h + 1)
                        for d in range(2):
                            sp.dma_start(S8A[:, :, d, :], a["state_ret"][0, 0:4, h, d * P:(d + 1) * P, :]
                                         .rearrange("b p e -> p b e")).then_inc(R.s8_in[0], 16)
                    for c in range(NC):
                        if j == (5, 7, 7)[c]:
                            if c == 0:
                                sp.wait_ge(R.gt, 3 * h + 1)
                                sp.dma_start(ZG[0][:, :, :], z[3][:, :, 2 * CH:]).then_inc(R.g_in[0], 16)
                            sp.wait_ge(R.u_ok, 3 * h + c + 2)
                            sp.dma_start(us[2 * h:2 * h + 2, :, c * CH:(c + 1) * CH].rearrange("e p t -> p e t"),
                                         UB[:, :, :]).then_inc(R.u_st, 16)
                sp.wait_ge(R.st_ev, 16 * h + 9)
                sp.dma_start(o["ret_p"][0, 0, h].rearrange("(d p) e -> p d e", p=P), SR[:, :, :]).then_inc(R.sr_st, 16)
                sp.wait_ge(R.st_ev, 16 * h + 17)
                for g, t8 in enumerate((S8A, S8B[:, :, :, :])):
                    for d in range(2):
                        sp.dma_start(o["ret_s"][0, 4 * g:4 * g + 4, h, d * P:(d + 1) * P, :]
                                     .rearrange("b p e -> p b e"), t8[:, :, d, :]).then_inc(R.s8_st[g], 16)

            ret_done(sp)
            for h in range(HH):
                for j in range(HG_BLOCKS):
                    n = 40 + HG_BLOCKS * h + j
                    load_w(n + 2)
                    store_z(n - 1)
                    if j == 0:
                        z_stored(n - 1)
                        if h:
                            sp.wait_ge(H.att, 9 * h + 1)
                            sp.wait_ge(H.u_ok, 3 * h + 1)
                            sp.wait_ge(H.s8_st[0], 16 * h + 16)
                        for i in (1, 0, 2, 3):
                            sp.dma_start(HZ[i][:, :], zs[32 + 4 * h + i]).then_inc(H.in_[i], 16)
                        sp.dma_start(SH8[:, :, :], a["state_hgrn"][0, :, h].rearrange("b p e -> p b e"))\
                            .then_inc(H.s8_in[0], 16)
                    for c in range(NC):
                        if j == (3, 4, 4)[c]:
                            sp.wait_ge(H.u_ok, 3 * h + c + 2)
                            sp.dma_start(us[KT + h, :, c * CH:(c + 1) * CH], UB[:, 0, :]).then_inc(H.u_st, 16)
                sp.wait_ge(H.st_ev, 16 * h + 9)
                sp.dma_start(o["hg_p"][0, 0, h], SH[:, :]).then_inc(H.sr_st, 16)
                sp.wait_ge(H.st_ev, 16 * h + 17)
                sp.dma_start(o["hg_s"][0, :, h].rearrange("b p e -> p b e"), SH8[:, :, :]).then_inc(H.s8_st[0], 16)

            store_z(NRB - 1)
            z_stored(NRB - 1)
            hg_done(sp)
            for br in range(2):
                for k in range(KT):
                    i = KT * br + k
                    if i >= 2:
                        sp.wait_ge(sp_lo, i - 1)
                    sp.dma_start(URAW[i % 2][:, :], us[i]).then_inc(ur_in[i % 2], 16)
                for k in range(KT):
                    i = KT * br + k
                    if i >= 2:
                        sp.wait_ge(ev, NC * (NRB + i - 2) + NC)
                    sp.dma_start(MG[i % 2][:, :], zs[64 + i]).then_inc(mg_in[i % 2], 16)
                    if NRB + i + 2 < NB1:
                        load_w(NRB + i + 2)
            for k in range(KT):
                w = W_OUT + k
                sp.wait_ge(w_lo, w - 1)
                sp.dma_start(WRAW[w % 2][:, :], a["w_out"][0, k * P:(k + 1) * P, :]).then_inc(w_raw[w % 2], 16)
            sp.wait_ge(w_lo, W_FFN - 1)
            sp.dma_start(as_block(WRAW[0]), a["w_up"][0, :, 0:P].rearrange("(k p) n -> p k n", p=P)).then_inc(w_raw[0], 16)
            sp.wait_ge(sp_lo, 3 * KT)
            sp.wait_ge(sp_hi, 3 * KT)
            sp.dma_start(GB[:, :], a["g_post_mix"].to_broadcast([P, D])).then_inc(gb_in, 16)
            for t in range(NT):
                if t >= 2:
                    sp.wait_ge(d_x1, t - 1)
                rows(t, XI2[t % 2], xi_in[t % 2])
                if t >= 1:
                    sp.wait_ge(d_x1, t)
                    sp.dma_start(x1s[(t - 1) * P:t * P, :], X1R[(t - 1) % 2][:, :]).then_inc(x1_st[(t - 1) % 2], 16)
            sp.wait_ge(d_x1, NT)
            sp.dma_start(x1s[(NT - 1) * P:, :], X1R[(NT - 1) % 2][:, :]).then_inc(x1_st[(NT - 1) % 2], 16)
            def mlp_w(g, last):
                for i in range(7):
                    w = W_FFN + 1 + 8 * g + i
                    sp.wait_ge(w_lo, w - 1)
                    s = w_raw[(W_FFN + 1 + i) % 2]
                    dst = WRAW[(W_FFN + 1 + i) % 2]
                    if i % 2 == 0:
                        sp.dma_start(dst[:, :], a["w_down"][0, bass.ds(g * 512 + (i // 2) * P, P), :]).then_inc(s, 16)
                    else:
                        sp.dma_start(as_block(dst), a["w_up"][0, :, bass.ds(g * 512 + (i // 2 + 1) * P, P)]
                                     .rearrange("(k p) n -> p k n", p=P)).then_inc(s, 16)
                if not last:
                    w = W_FFN + 8 + 8 * g
                    sp.wait_ge(w_lo, w - 1)
                    sp.dma_start(as_block(WRAW[W_FFN % 2]), a["w_up"][0, :, bass.ds(g * 512 + 512, P)]
                                 .rearrange("(k p) n -> p k n", p=P)).then_inc(w_raw[W_FFN % 2], 16)

            with sp.Fori(0, FF // 512 - 1) as g:
                mlp_w(g, False)
            mlp_w(FF // 512 - 1, True)
            sp.wait_ge(dn, 18 * (FF // 512) + 1)
            for i in range(2):
                sp.wait_ge(x1_st[i], 16 * ((NT + 1 - i) // 2))
            sp.dma_start(GF[:, :], a["g_post_ffn"].to_broadcast([P, D])).then_inc(gb_in, 16)
            for t in range(NT):
                if t >= 2:
                    sp.wait_ge(y_ok, t - 1)
                sp.dma_start(X1F[t % 2][:, :], x1s[t * P:(t + 1) * P, :]).then_inc(x1_in[t % 2], 16)
                if t >= 1:
                    y_store(sp, t - 1)
            y_store(sp, NT - 1)
            for i in range(2):
                sp.wait_ge(y_st[i], 16 * ((NT + 1 - i) // 2))
            sp.wait_ge(H.sr_st, 16 * HH + 16)
            sp.wait_ge(H.s8_st[0], 16 * HH + 16)


        @block.tensor
        def _(pe):
            def norm_transpose(tt, src):
                b = 3 + 2 * (tt % 2)
                pe.wait_ge(n_hr, tt + 1)
                for g in range(2):
                    if tt >= 2:
                        pe.wait_ge(n_tm, 2 * (tt - 2) + g + 1)
                    for i in range(4):
                        k = 4 * g + i
                        last = pe.transpose(psum[b + g][:, i * P:(i + 1) * P], src[:, k * P:(k + 1) * P], ident[:, :])
                    last.then_inc(n_tp, 1)

            def gemm(n, m, p, c, first=False):
                if c == 0:
                    pe.wait_ge(w_lo, n + 1)
                if not first:
                    pe.wait_ge(ev, NC * (n - 1) + c + 1)
                s = slice(c * CH, (c + 1) * CH)
                for k in range(KT):
                    pe.matmul(psum[c][:, 0:CH], WHI[p][:, k, :], XH[:, k, s], start=(k == 0), stop=False)
                    pe.matmul(psum[c][:, 0:CH], WHI[p][:, k, :], XL[:, k, s], start=False, stop=False)
                    last = pe.matmul(psum[c][:, 0:CH], WLO[p][:, k, :], XH[:, k, s], start=False, stop=(k == KT - 1))
                last.then_inc(mm, 1)

            for s in (R.rb, H.rb, R.st_full, H.st_full):
                pe.sem_inc(s, 1)
            pe.wait_ge(c_in, 48)
            for tt in range(NT):
                norm_transpose(tt, HR[tt % 2])
            pe.wait_ge(n_xh, 2 * NT)
            pe.wait_ge(n_xl, 2 * NT)
            for p in range(2):
                for c in range(NC):
                    gemm(p, 0, p, c, first=(p == 0))
            with pe.Fori(1, 4) as m:
                for p in range(2):
                    for c in range(NC):
                        gemm(2 * m + p, m, p, c)

            def ret_a(h, t):
                s = slice(t * P, (t + 1) * P)
                if t == 0:
                    pe.wait_ge(R.in_[2], 16 * h + 16)
                    pe.wait_ge(R.q_ok, h + 1)
                    pe.wait_ge(R.k_ok, h + 1)
                    pe.wait_ge(R.kz8, 8 * h + 1)
                pe.wait_ge(R.kv, 9 * h + t + 1)
                for e in range(2):
                    pe.transpose(PT[:, e * P:(e + 1) * P], ZV[:, e, s], ident[:, :])
                for e in range(2):
                    last = pe.transpose(PT[:, (2 + e) * P:(3 + e) * P], KR[:, e, s], ident[:, :])
                last.then_inc(R.t_full, 1)
                pe.wait_ge(R.att, 9 * h + t + 1)
                pe.matmul(PSC[:, 0:P], KR[:, 0, s], QR[:, 0, s], start=True, stop=False)
                pe.matmul(PSC[:, 0:P], KR[:, 1, s], QR[:, 1, s], start=False, stop=True).then_inc(R.sc, 1)

            def ret_b(h, t):
                s = slice(t * P, (t + 1) * P)
                kv, at = KVT[t % 2], ATT[t % 2]
                pe.wait_ge(R.kv, 9 * h + t + 2)
                pe.wait_ge(R.att, 9 * h + t + 2)
                pe.wait_ge(R.o_ev, 9 * h + t + 1)
                pe.wait_ge(R.st_ev, 16 * h + t + 1)
                if t == NT - 1:
                    pe.wait_ge(R.s8_in[0], 32 * h + 32)
                    pe.wait_ge(R.s8_in[1], 32 * h + 32)
                for e in range(2):
                    es = slice(e * P, (e + 1) * P)
                    last = pe.matmul(PO[:, es], kv[:, 0, es], at[:, :], start=(e == 0), stop=(t == 0), skip_group_check=True)
                    if 0 < t < NT - 1:
                        for d in range(2):
                            last = pe.matmul(PO[:, es], SR[:, d, es], QX[:, d, s], start=False, stop=(d == 1), skip_group_check=True)
                    if t == NT - 1:
                        for b in range(NS):
                            st = S8A[:, b, :, :] if b < 4 else S8B[:, b - 4, :, :]
                            for d in range(2):
                                last = pe.matmul(PO[:, e * P + b * TS:e * P + (b + 1) * TS], st[:, d, es],
                                                 QX[:, d, TP + b * TS:TP + (b + 1) * TS],
                                                 start=False, stop=(b == NS - 1 and d == 1), skip_group_check=True)
                last.then_inc(R.o_full, 1)
                if t < NT - 1:
                    for d in range(2):
                        last = pe.matmul(PST[:, d * RD:(d + 1) * RD], kv[:, 1, d * P:(d + 1) * P], kv[:, 0, :],
                                         start=(d == 0), stop=(d == 1), skip_group_check=True)
                    last.then_inc(R.st_full, 1)
                    return
                for b in range(NS):
                    bank = (PST, PRB)[b % 2]
                    pe.wait_ge(R.kz8, 8 * h + b + 2)
                    if b == 1:
                        pe.wait_ge(R.w_ok, 3 * h + 3)
                    if b >= 2:
                        pe.wait_ge(R.st_ev, 16 * h + 8 + b)
                    for d in range(2):
                        last = pe.matmul(bank[:, d * RD:(d + 1) * RD], KZ8[b % 2][:, d * P:(d + 1) * P], kv[:, 0, :],
                                         start=(d == 0), stop=(d == 1), skip_group_check=True)
                    last.then_inc(R.st_full, 1)

            def head_sum(K, h, c, ne):
                pe.wait_ge(K.sq, 3 * h + c + 1)
                pe.wait_ge(K.w_ok, 3 * h + c + 1)
                if c == 2:
                    pe.wait_ge(K.st_ev, 16 * h + 17)
                for r in range(TPC):
                    for e in range(ne):
                        last = pe.matmul(PRB[:, r:r + 1], SQ[:, e, r * P:(r + 1) * P], ones[:, 0:1],
                                         start=(e == 0), stop=(e == ne - 1))
                last.then_inc(K.rb, 1)

            def head_spread(K, h, c):
                pe.wait_ge(K.dg, 3 * h + c + 1)
                pe.matmul(PRB[:, 0:CH], ones[:, :], DG[:, :, :].rearrange("p r t -> p (r t)"),
                          start=True, stop=True).then_inc(K.rbb, 1)

            with pe.Fori(0, RH) as h:
                for s in range(RET_SLOTS):
                    j, c = divmod(s, NC)
                    gemm(8 + 8 * h + j, 4 + 4 * h + j // 2, j % 2, c)
                    for i in range(NC):
                        if s == R_NORM[i]:
                            head_sum(R, h, i, 2)
                        if s == R_NORM[i] + 1:
                            head_spread(R, h, i)
                    for t in range(NT):
                        if s == RA + 2 * t:
                            ret_a(h, t)
                        if s == RB_ + 2 * t:
                            ret_b(h, t)

            def hg_a(h, t):
                s = slice(t * P, (t + 1) * P)
                c, r = divmod(t, TPC)
                if t == 0:
                    pe.wait_ge(H.in_[2], 16 * h + 16)
                    pe.wait_ge(H.fk, h + 1)
                    pe.wait_ge(H.kz8, 8 * h + 1)
                if r == 0:
                    pe.wait_ge(H.q_ok, 3 * h + c + 1)
                    pe.wait_ge(H.k_ok, 3 * h + c + 1)
                pe.wait_ge(H.kv, 9 * h + t + 1)
                pe.wait_ge(H.att, 9 * h + t + 1)
                pe.transpose(PT[:, 0:P], HZ[2][:, s], ident[:, :])
                tr = pe.transpose(PT[:, P:2 * P], KRH[:, s], ident[:, :])
                if t == NT - 1:
                    tr.then_inc(H.t_full, 1)
                last = pe.matmul(PSC[:, 0:P], KK[:, s], HZ[0][:, s], start=True, stop=True, skip_group_check=True)
                kt = slice(r * P, (r + 1) * P)
                qt = slice(r * 64, (r + 1) * 64)
                for l in range(min(6, LEV if t < NT - 1 else LEVS)):
                    last = pe.matmul(PSC[:, P + 64 * l:P + 64 * (l + 1)], KE[c % 2][:, l, kt], QE[c % 2][:, l, qt],
                                     start=True, stop=True, skip_group_check=True)
                last.then_inc(H.sc, 1)
                if t < NT - 1:
                    last = pe.matmul(PT[:, 2 * P:2 * P + 64], KE[c % 2][:, 6, kt], QE[c % 2][:, 6, qt], start=True, stop=True)
                    last.then_inc(H.t_full, 1)

            def hg_b(h, t):
                s = slice(t * P, (t + 1) * P)
                kv, at = KVT[t % 2], ATT[t % 2]
                pe.wait_ge(H.kv, 9 * h + t + 2)
                pe.wait_ge(H.att, 9 * h + t + 2)
                pe.wait_ge(H.o_ev, 9 * h + t + 1)
                pe.wait_ge(H.st_ev, 16 * h + t + 1)
                if t == NT - 1:
                    pe.wait_ge(H.s8_in[0], 16 * h + 16)
                last = pe.matmul(PO[:, 0:P], kv[:, 0, 0:P], at[:, :], start=True, stop=(t == 0), skip_group_check=True)
                if 0 < t < NT - 1:
                    last = pe.matmul(PO[:, 0:P], SH[:, :], QP[:, s], start=False, stop=True, skip_group_check=True)
                if t == NT - 1:
                    for b in range(NS):
                        last = pe.matmul(PO[:, b * TS:(b + 1) * TS], SH8[:, b, :], QP[:, TP + b * TS:TP + (b + 1) * TS],
                                         start=False, stop=(b == NS - 1), skip_group_check=True)
                last.then_inc(H.o_full, 1)
                if t < NT - 1:
                    pe.matmul(PST[:, 0:P], kv[:, 1, 0:P], kv[:, 0, 0:P], start=True, stop=True).then_inc(H.st_full, 1)
                    return
                for b in range(NS):
                    pe.wait_ge(H.kz8, 8 * h + b + 2)
                    if b == 1:
                        pe.wait_ge(H.w_ok, 3 * h + 3)
                    if b >= 2:
                        pe.wait_ge(H.st_ev, 16 * h + 8 + b)
                    pe.matmul((PST, PRB)[b % 2][:, 0:P], KM8[b % 2][:, :], kv[:, 0, 0:P],
                              start=True, stop=True).then_inc(H.st_full, 1)

            pe.wait_ge(R.kv, 9 * RH + 1)
            pe.wait_ge(R.kz8, 8 * RH + 1)
            pe.wait_ge(R.att, 9 * RH + 1)
            pe.wait_ge(R.o_ev, 9 * RH + 1)
            pe.wait_ge(R.st_ev, 16 * RH + 1)
            pe.wait_ge(R.w_ok, 3 * RH + 1)
            with pe.Fori(0, HH // 2) as i:
                for u in range(2):
                    h = 2 * i + u
                    for s in range(HG_SLOTS):
                        j, c = divmod(s, NC)
                        jj = HG_BLOCKS * u + j
                        gemm(40 + 10 * i + jj, 20 + 5 * i + jj // 2, jj % 2, c)
                        for x in range(NC):
                            if s == H_NORM[x]:
                                head_sum(H, h, x, 1)
                            if s == H_NORM[x] + 1:
                                head_spread(H, h, x)
                        if s >= 3 and s - 3 < NT:
                            hg_a(h, s - 3)
                        if s >= 4 and s - 4 < NT:
                            hg_b(h, s - 4)

            for br in range(2):
                pe.wait_ge(sp_hi, KT * (br + 1))
                pe.wait_ge(sp_lo, KT * (br + 1))
                with pe.Fori(0, KT // 2) as i:
                    for p in range(2):
                        for c in range(NC):
                            gemm(NRB + KT * br + 2 * i + p, None, p, c)

            pe.wait_ge(w_lo, W_OUT + KT)
            pe.wait_ge(sp_hi, 3 * KT)
            pe.wait_ge(sp_lo, 3 * KT)
            pe.wait_ge(ev, NC * NB1)
            pe.wait_ge(H.kv, 9 * HH + 1)
            pe.wait_ge(H.kz8, 8 * HH + 1)
            pe.wait_ge(H.att, 9 * HH + 1)
            pe.wait_ge(H.o_ev, 9 * HH + 1)
            pe.wait_ge(H.st_ev, 16 * HH + 1)
            pe.wait_ge(H.w_ok, 3 * HH + 1)
            DB = ((0, 1), (2, 7))
            for t in range(NT + 1):
                if t < NT:
                    s = slice(t * P, (t + 1) * P)
                    if t >= 2:
                        pe.wait_ge(d_x1, t - 1)
                    for q in range(2):
                        bank = psum[DB[t % 2][q]]
                        ns = slice(512 * q, 512 * (q + 1))
                        for k in range(KT):
                            pe.matmul(bank[:, :], XH[:, k, s], WOH[:, k, ns], start=(k == 0), stop=False)
                            pe.matmul(bank[:, :], XH[:, k, s], WOL[:, k, ns], start=False, stop=False)
                            last = pe.matmul(bank[:, :], XL[:, k, s], WOH[:, k, ns], start=False, stop=(k == KT - 1))
                    last.then_inc(d_mm, 1)
                if t >= 1:
                    norm_transpose(NT + t - 1, HR2[(NT + t - 1) % 2])

            pe.wait_ge(n_xh, 4 * NT)
            pe.wait_ge(n_xl, 4 * NT)
            pe.wait_ge(d_x1, NT)
            NG = FF // 512
            with pe.Fori(0, NG) as g:
                for b in range(4):
                    pe.wait_ge(w_lo, W_FFN + 8 * g + 2 * b + 1)
                    for c in range(NC):
                        if b:
                            pe.wait_ge(f_t1, NC * (4 * g + b - 1) + c + 1)
                        s = slice(c * CH, (c + 1) * CH)
                        for k in range(KT):
                            pe.matmul(psum[c][:, 0:CH], WHI[b % 2][:, k, :], XH[:, k, s], start=(k == 0), stop=False)
                            pe.matmul(psum[c][:, 0:CH], WHI[b % 2][:, k, :], XL[:, k, s], start=False, stop=False)
                            last = pe.matmul(psum[c][:, 0:CH], WLO[b % 2][:, k, :], XH[:, k, s], start=False, stop=(k == KT - 1))
                        last.then_inc(mm, 1)
                pe.wait_ge(w_lo, W_FFN + 8 * g + 8)
                pe.wait_ge(f_ul, 12 * g + 12)
                for t in range(NT):
                    s = slice(t * P, (t + 1) * P)
                    for q in range(2):
                        x = 2 * t + q
                        bank = psum[3 + x % 5]
                        ns = slice(512 * q, 512 * (q + 1))
                        if x >= 5:
                            pe.wait_ge(dn_ev, 18 * g + x - 5 + 2)
                        else:
                            pe.wait_ge(dn_ev, 18 * g + 1)
                        for k in range(4):
                            pe.matmul(bank[:, :], UH[:, k, s], WDH[:, k, ns], start=(k == 0), stop=False)
                            pe.matmul(bank[:, :], UH[:, k, s], WDL[:, k, ns], start=False, stop=False)
                            last = pe.matmul(bank[:, :], UL[:, k, s], WDH[:, k, ns], start=False, stop=(k == 3))
                        last.then_inc(dn, 1)

        @block.scalar
        def _(act):
            ch = Chain(act, act_ch)

            def copy(dst, src):
                return act.activation(dst, src, ACT.Copy)

            def whi(w, p, m, src, dst, free=None):
                act.wait_ge(w_raw[p], 16 * m + 16)
                if free is not None:
                    act.wait_ge(mm, free)
                copy(dst, src).then_inc(w_hi, 1)

            def whi_block(n, m, p, free=True):
                whi(n, p, m, as_block(WRAW[p]), WHI[p][:, :, :], 3 * n - 3 if free else None)

            def evac(n, m, p, c, first=False):
                act.wait_ge(mm, NC * n + c + 1)
                if c == 0 and not first:
                    act.wait_ge(z_st[p], 16 * m)
                copy(ZST[p][:, c * CH:(c + 1) * CH], psum[c][:, 0:CH]).then_inc(ev, 1)

            def norm_sq(tt, src, junk):
                if tt:
                    act.wait_ge(n_ss, tt)
                act.activation(junk[:, :], src[:, :], ACT.Square, accum_out=ssc[:, tt:tt + 1]).then_inc(n_ss, 1)

            def norm_xh(tt, tm, t):
                for g in range(2):
                    act.wait_ge(n_tm, 2 * tt + g + 1)
                    copy(XH[:, 4 * g:4 * g + 4, t * P:(t + 1) * P], tm[g][:, :, :]).then_inc(n_xh, 1)

            for tt in range(NT + 1):
                if tt < NT:
                    act.wait_ge(x_in[tt % 2], 16 * (tt // 2 + 1))
                    norm_sq(tt, XR[tt % 2], SQJ)
                if tt == 3:
                    whi_block(0, 0, 0, free=False)
                if tt == 4:
                    whi_block(1, 0, 1, free=False)
                if tt:
                    norm_xh(tt - 1, TM, tt - 1)
            act.wait_ge(lb_ch, 2)
            act.activation(LB[:, :, :], LB[:, :, :], ACT.Exp).then_inc(lb_e, 1)
            for s in (R.kv, R.o_ev, R.kz8, H.kv, H.o_ev, H.kz8):
                act.sem_inc(s, 1)

            def block_slot(n, m, p, c):
                if c == 0:
                    mn, pn = (m, 1) if p == 0 else (m + 1, 0)
                    whi_block(n + 1, mn, pn)
                evac(n, m, p, c)

            act.wait_ge(n_xl, 2 * NT)
            for n in range(2):
                for c in range(NC):
                    if c == 0 and n == 1:
                        whi_block(2, 1, 0)
                    evac(n, 0, n, c, first=True)
            with act.Fori(1, 4) as m:
                for p in range(2):
                    for c in range(NC):
                        block_slot(2 * m + p, m, p, c)

            def kv_ret(h, t):
                act.wait_ge(R.t_full, 9 * h + t + 1)
                act.wait_ge(R.st_full, 16 * h + (t if t >= 2 else 1))
                if t == 0:
                    act.wait_ge(R.in_[3], 16 * h + 16)
                if t < NT - 1:
                    copy(KVT[t % 2][:, 0, :], PT[:, 0:RD])
                    act.activation(KVT[t % 2][:, 1, :], PT[:, RD:2 * RD], ACT.Copy, scale=ZETA).then_inc(R.kv, 1)
                else:
                    copy(KVT[t % 2][:, 0, :], PT[:, 0:RD]).then_inc(R.kv, 1)

            def kz_ret(h):
                for b in range(NS):
                    if b >= 2:
                        act.wait_ge(R.st_full, 16 * h + 8 + b)
                    act.activation(KZ8[b % 2][:, :], PT[:, RD:2 * RD], ACT.Copy,
                                   scale=HC[:, 4 * P + 3 + b:4 * P + 4 + b]).then_inc(R.kz8, 1)

            def head_sq(K, h, c, ne, src, gate, g_in, g_v):
                act.wait_ge(K.o_ev, 9 * h + TPC * c + TPC + 1)
                act.wait_ge(K.rb, 3 * h + c + 1)
                act.activation(SQ[:, 0:ne, :], src, ACT.Square).then_inc(K.sq, 1)
                act.wait_ge(g_in, g_v)
                act.wait_ge(K.u_ok, 3 * h + c + 1)
                act.activation(SG[:, 0:ne, :], gate, ACT.Sigmoid).then_inc(K.sg, 1)

            with act.Fori(0, RH) as h:
                for s in range(RET_SLOTS):
                    j, c = divmod(s, NC)
                    block_slot(8 + 8 * h + j, 4 + 4 * h + j // 2, j % 2, c)
                    for t in range(NT):
                        if s == RA + 2 * t:
                            kv_ret(h, t)
                        if s == RB_ + 2 * t:
                            act.wait_ge(R.o_full, 9 * h + t + 1)
                            copy(QX[:, :, t * P:(t + 1) * P],
                                 PO[:, 0:RD].rearrange("p (e t) -> p e t", e=2)).then_inc(R.o_ev, 1)
                            if t == NT - 1:
                                kz_ret(h)
                    for i in range(NC):
                        if s == R_NORM[i] - 1:
                            g_v = 32 * h + (16, 16, 32)[i]
                            if i == 1:
                                g_v = 16 * h + 16
                            head_sq(R, h, i, 2, QX[:, :, i * CH:(i + 1) * CH], ZG[i % 2][:, :, :], R.g_in[i % 2], g_v)

            ret_done(act)

            def kv_hg(h, t):
                act.wait_ge(H.t_full, 9 * h + t + 1)
                act.wait_ge(H.st_full, 16 * h + (t if t >= 2 else 1))
                if t < NT - 1:
                    copy(KVT[t % 2][:, :, 0:P], PT[:, 0:2 * P].rearrange("p (a d) -> p a d", a=2)).then_inc(H.kv, 1)
                else:
                    copy(KVT[t % 2][:, 0, 0:P], PT[:, 0:P]).then_inc(H.kv, 1)

            def kz_hg(h):
                for b in range(NS):
                    if b >= 2:
                        act.wait_ge(H.st_full, 16 * h + 8 + b)
                    act.activation(KM8[b % 2][:, :], PT[:, P:2 * P], ACT.Copy, scale=RM[:, b:b + 1]).then_inc(H.kz8, 1)

            act.wait_ge(c_in2, 48)
            with act.Fori(0, HH // 2) as i:
                for u in range(2):
                    h = 2 * i + u
                    for s in range(HG_SLOTS):
                        j, c = divmod(s, NC)
                        jj = HG_BLOCKS * u + j
                        if s == 0:
                            act.wait_ge(H.in_[1], 16 * h + 16)
                            act.activation(FG[:, :], HZ[1][:, :], ACT.Sigmoid).then_inc(H.f_ok, 1)
                        block_slot(40 + 10 * i + jj, 20 + 5 * i + jj // 2, jj % 2, c)
                        if s >= 3 and s - 3 < NT:
                            kv_hg(h, s - 3)
                        if s >= 4 and s - 4 < NT:
                            t = s - 4
                            act.wait_ge(H.o_full, 9 * h + t + 1)
                            copy(OH[:, t * P:(t + 1) * P], PO[:, 0:P]).then_inc(H.o_ev, 1)
                            if t == NT - 1:
                                kz_hg(h)
                        for x in range(NC):
                            if s == H_NORM[x] - 1:
                                head_sq(H, h, x, 1, OH[:, x * CH:(x + 1) * CH].unsqueeze(1),
                                        HZ[3][:, x * CH:(x + 1) * CH].unsqueeze(1), H.in_[3], 16 * h + 16)

            hg_done(act)
            for br in range(2):
                for k in range(KT):
                    i = KT * br + k
                    act.wait_ge(ur_in[i % 2], 16 * (i // 2 + 1))
                    if k == 0:
                        act.wait_ge(mm, NC * (NRB + KT * br))
                    copy(XH[:, k, :], URAW[i % 2][:, :]).then_inc(sp_hi, 1)
                for k in range(KT):
                    i = KT * br + k
                    n = NRB + i
                    if n + 1 < NB1:
                        whi_block(n + 1, (n + 1) // 2, (n + 1) % 2)
                    else:
                        whi(W_OUT, W_OUT % 2, W_OUT // 2, WRAW[0][:, :], WOH[:, 0, :])
                    act.wait_ge(mg_in[i % 2], 16 * (i // 2 + 1))
                    act.activation(MG[i % 2][:, :], MG[i % 2][:, :], ACT.Sigmoid).then_inc(mg_ok, 1)
            for k in range(1, KT):
                w = W_OUT + k
                whi(w, w % 2, w // 2, WRAW[w % 2][:, :], WOH[:, k, :])
            for k in range(KT):
                if k == 0:
                    act.wait_ge(mm, NC * NB1)
                    act.wait_ge(ev, NC * NB1)
                copy(XH[:, k, :], MIX[:, k, :]).then_inc(sp_hi, 1)
            act.wait_ge(sp_lo, 3 * KT)
            act.wait_ge(gb_in, 16)
            DB = ((0, 1), (2, 7))
            for t in range(NT + 1):
                if t < NT:
                    act.wait_ge(d_mm, t + 1)
                    act.wait_ge(n_ss, NT + max(t - 1, 0))
                    if t:
                        act.wait_ge(d_ss, t)
                    for q in range(2):
                        last = act.activation(SQJ2[:, 512 * q:512 * (q + 1)], psum[DB[t % 2][q]][:, :], ACT.Square,
                                              accum_out=dss[:, 2 * t + q:2 * t + q + 1])
                    last.then_inc(d_ss, 1)
                if t >= 1:
                    tt = NT + t - 1
                    act.wait_ge(d_x1, t)
                    act.wait_ge(d_ss, min(t + 1, NT))
                    act.activation(SQJ2[:, :], X1R[(t - 1) % 2][:, :], ACT.Square, accum_out=ssc[:, tt:tt + 1]).then_inc(n_ss, 1)
                if t == 3:
                    whi(W_FFN, 0, W_FFN // 2, as_block(WRAW[0]), WHI[0][:, :, :])
                if t >= 1:
                    norm_xh(NT + t - 1, TM2, t - 1)
            NG = FF // 512
            act.wait_ge(n_xl, 4 * NT)
            act.wait_ge(w_lo, W_FFN + 1)

            def mlp(g, last):
                w0 = W_FFN + 1 + 8 * g

                def split(i):
                    q = (W_FFN + 1 + i) % 2
                    m = (W_FFN + 1 + i) // 2 + 4 * g
                    if i % 2 == 0:
                        if i == 0:
                            act.wait_ge(dn, 18 * g + 1)
                        whi(w0 + i, q, m, WRAW[q][:, :], WDH[:, i // 2, :])
                    else:
                        b = (i // 2 + 1) % 4
                        whi(w0 + i, q, m, as_block(WRAW[q]), WHI[b % 2][:, :, :],
                            NC * (NB1 + 4 * g + i // 2))
                for b in range(4):
                    for c in range(NC):
                        if c == 0:
                            split(2 * b)
                        if c == 1 and b < 3:
                            split(2 * b + 1)
                        x = NC * b + c
                        act.wait_ge(mm, NC * NB1 + 12 * g + x + 1)
                        if x >= 2:
                            act.wait_ge(f_t2, 12 * g + x - 1)
                        act.activation(T1[x % 2][:, :], psum[c][:, 0:CH], ACT.Relu).then_inc(f_t1, 1)
                        act.wait_ge(f_t2, 12 * g + x + 1)
                        copy(UH[:, b, c * CH:(c + 1) * CH], T2[x % 2][:, :]).then_inc(f_uh, 1)
                if not last:
                    split(7)
            act.sem_inc(dn, 1)
            with act.Fori(0, NG - 1) as g:
                mlp(g, False)
            mlp(NG - 1, True)
            act.wait_ge(dn, 18 * NG + 1)
            for t in range(NT):
                act.wait_ge(dn_ev, 18 * (NG - 1) + 2 * t + 3)
                if t:
                    act.wait_ge(y_ss, t)
                act.activation(SQJ3[:, :], ACC[:, t, :], ACT.Square, accum_out=yss[:, t:t + 1]).then_inc(y_ss, 1)

        @block.vector
        def _(dve):
            ch = Chain(dve, dve_ch)

            def wlo(w, src, hi, lo):
                dve.wait_ge(w_hi, w + 1)
                dve.tensor_tensor(lo, src, plain(hi), ALU.subtract).then_inc(w_lo, 1)

            def wlo_block(n, p):
                wlo(n, as_block(WRAW[p]), WHI[p][:, :, :], WLO[p][:, :, :])

            def norm_ms(tt):
                dve.wait_ge(n_ss, tt + 1)
                dve.tensor_scalar(msc[:, tt:tt + 1], ssc[:, tt:tt + 1], 1.0 / D, EPS, ALU.mult, ALU.add).then_inc(n_ms, 1)

            def norm_row(tt, src, dst):
                dve.wait_ge(n_rs, tt + 1)
                if tt >= 2:
                    dve.wait_ge(n_tp, 2 * (tt - 2) + 2)
                dve.tensor_scalar(dst[:, :], src[:, :], rsc[:, tt:tt + 1], None, ALU.mult).then_inc(n_hr, 1)

            def norm_cols(tt, tm, which, t):
                b = 3 + 2 * (tt % 2)
                for g in range(2):
                    dve.wait_ge(n_tp, 2 * tt + g + 1)
                    if tt:
                        dve.wait_ge(n_xh, 2 * (tt - 1) + g + 1)
                        dve.wait_ge(n_xl, 2 * (tt - 1) + g + 1)
                    gain = gcol[:, which, 4 * g:4 * g + 4].unsqueeze(2).to_broadcast([P, 4, P])
                    dve.tensor_tensor(tm[g][:, :, :], psum[b + g][:, :].rearrange("p (k t) -> p k t", k=4),
                                      gain, ALU.mult).then_inc(n_tm, 1)
                for g in range(2):
                    dve.wait_ge(n_xh, 2 * tt + g + 1)
                    ks, ts = slice(4 * g, 4 * g + 4), slice(t * P, (t + 1) * P)
                    dve.tensor_tensor(XL[:, ks, ts], tm[g][:, :, :], plain(XH[:, ks, ts]), ALU.subtract).then_inc(n_xl, 1)

            dve.wait_ge(c_in, 48)
            dve.tensor_tensor(LBM[:, :], LB[:, 0, :], LB[:, 1, :], ALU.max).then_inc(lb_ch, 1)
            dve.wait_ge(lb_ch, 1)
            dve.tensor_tensor(LB[:, :, :], LB[:, :, :], LBM[:, :].unsqueeze(1).to_broadcast([P, 2, HH]),
                              ALU.subtract).then_inc(lb_ch, 1)
            for tt in range(NT + 1):
                if tt < NT:
                    norm_ms(tt)
                    norm_row(tt, XR[tt % 2], HR[tt % 2])
                if tt == 4:
                    wlo_block(0, 0)
                if tt == 5:
                    wlo_block(1, 1)
                if tt:
                    norm_cols(tt - 1, TM, 0, tt - 1)
            dve.wait_ge(lb_e, 1)
            ch(dve.tensor_tensor(LBM[:, :], LB[:, 0, :], LB[:, 1, :], ALU.add))
            ch(dve.reciprocal(LBM[:, :], LBM[:, :]))
            ch(dve.tensor_tensor(LBC[:, 0, :], LB[:, 0, :], LBM[:, :], ALU.mult))
            ch(dve.tensor_scalar(LBC[:, 1, :], LBC[:, 0, :], -1.0, 1.0, ALU.mult, ALU.add))
            ch(dve.memset(ones[:, :], 1.0))
            ch.reset()
            for s in (R.att, R.st_ev, R.ms, R.u_ok, R.w_ok, H.att, H.st_ev, H.ms, H.u_ok, H.w_ok):
                dve.sem_inc(s, 1)

            wlo_block(2, 0)
            with dve.Fori(1, 4) as m:
                for p in range(2):
                    wlo_block(2 * m + p + 1, (p + 1) % 2)

            def norm_sum(K, h, c, width):
                dve.wait_ge(K.rb, 3 * h + c + 2)
                dve.tensor_scalar(MS[:, :], PRB[:, 0:TPC], 1.0 / width, EPS, ALU.mult, ALU.add).then_inc(K.ms, 1)
                dve.wait_ge(K.rs, 3 * h + c + 1)
                dve.tensor_tensor(DG[:, :, :], ident[:, :].unsqueeze(1).to_broadcast([P, TPC, P]),
                                  RST[:, :].unsqueeze(2).to_broadcast([P, TPC, P]), ALU.mult).then_inc(K.dg, 1)

            def gated(K, h, c, ne, src):
                dve.wait_ge(K.gt, 3 * h + c + 1)
                dve.wait_ge(K.rbb, 3 * h + c + 1)
                dve.tensor_tensor(SG[:, 0:ne, :], SG[:, 0:ne, :],
                                  PRB[:, 0:CH].unsqueeze(1).to_broadcast([P, ne, CH]), ALU.mult).then_inc(K.w_ok, 1)
                dve.wait_ge(K.w_ok, 3 * h + c + 2)
                dve.wait_ge(K.u_st, 48 * h + 16 * c + 16)
                dve.tensor_tensor(UB[:, 0:ne, :], SG[:, 0:ne, :], src, ALU.mult).then_inc(K.u_ok, 1)

            def rotate_q(h, c):
                s = slice(c * CH, (c + 1) * CH)
                cs, sn = CS[:, 0, s], CS[:, 1, s]
                dve.tensor_tensor(RTMP[:, 0, :], ZQ[:, 0, s], cs, ALU.mult)
                ch(dve.tensor_tensor(RTMP[:, 1, :], ZQ[:, 1, s], sn, ALU.mult))
                ch(dve.tensor_tensor(QR[:, 0, s], RTMP[:, 0, :], RTMP[:, 1, :], ALU.subtract))
                dve.tensor_tensor(RTMP[:, 0, :], ZQ[:, 0, s], sn, ALU.mult)
                ch(dve.tensor_tensor(RTMP[:, 1, :], ZQ[:, 1, s], cs, ALU.mult))
                ch(dve.tensor_tensor(QR[:, 1, s], RTMP[:, 0, :], RTMP[:, 1, :], ALU.add))
                n = TPC if c < NC - 1 else TPC - 1
                for d in range(2):
                    v = lambda x: x[:, d, c * CH:c * CH + n * P].rearrange("p (a t) -> p a t", t=P)
                    last = dve.tensor_tensor(v(QX), v(QR), XI[:, 0, :].unsqueeze(1).to_broadcast([P, n, P]), ALU.mult)
                    if c == NC - 1:
                        last = dve.tensor_tensor(QX[:, d, TP:T], QR[:, d, TP:T], XI[:, 1, :], ALU.mult)
                ch(last)

            def rotate_k0(c):
                s = slice(c * CH, (c + 1) * CH)
                dve.tensor_tensor(RTMP[:, 0, :], ZK[:, 0, s], CS[:, 0, s], ALU.mult)
                ch(dve.tensor_tensor(RTMP[:, 1, :], ZK[:, 1, s], CS[:, 1, s], ALU.mult))
                ch(dve.tensor_tensor(KR[:, 0, s], RTMP[:, 0, :], RTMP[:, 1, :], ALU.subtract))

            dve.wait_ge(c_in2, 48)
            with dve.Fori(0, RH) as h:
                for s in range(RET_SLOTS):
                    j, c = divmod(s, NC)
                    n = 8 + 8 * h + j
                    if c == 0:
                        wlo_block(n + 1, (j + 1) % 2)
                    for i in range(NC):
                        if s == R_NORM[i]:
                            norm_sum(R, h, i, RD)
                        if s == R_NORM[i] + 1:
                            gated(R, h, i, 2, QX[:, :, i * CH:(i + 1) * CH])
                    if s < 3:
                        if s == 0:
                            dve.wait_ge(R.in_[0], 16 * h + 16)
                            dve.wait_ge(R.in_[3], 16 * h + 16)
                        rotate_q(h, s)
                    if s == 3:
                        dve.wait_ge(R.in_[1], 16 * h + 16)
                        for c in range(NC):
                            rotate_k0(c)
                        dve.sem_inc(R.q_ok, 1)
                    for t in range(NT):
                        if s == RA + 2 * t:
                            dve.wait_ge(R.sc, 9 * h + t + 1)
                            dve.wait_ge(R.st_full, 16 * h + (t if t >= 2 else 1))
                            dve.tensor_tensor(ATT[t % 2][:, :], PSC[:, 0:P], DM[:, t // NTP, :], ALU.mult).then_inc(R.att, 1)
                        if s == RB_ + 2 * t and t < NT - 1:
                            dve.wait_ge(R.st_full, 16 * h + t + 2)
                            pst = PST[:, :].rearrange("p (d e) -> p d e", d=2)
                            if t == 0:
                                dve.wait_ge(R.sr_st, 16 * h + 16)
                                dve.tensor_copy(SR[:, :, :], pst).then_inc(R.st_ev, 1)
                            else:
                                dve.wait_ge(R.st_ev, 16 * h + t + 1)
                                dve.scalar_tensor_tensor(SR[:, :, :], SR[:, :, :], G128, pst, ALU.mult, ALU.add)\
                                   .then_inc(R.st_ev, 1)
                        if s == RB_ + 2 * t and t == NT - 1:
                            dve.wait_ge(R.s8_in[0], 32 * h + 32)
                            dve.wait_ge(R.s8_in[1], 32 * h + 32)
                            for b in range(NS):
                                st = S8A[:, b, :, :] if b < 4 else S8B[:, b - 4, :, :]
                                dve.wait_ge(R.st_full, 16 * h + b + 10)
                                dve.scalar_tensor_tensor(st, st, G16, (PST, PRB)[b % 2][:, :].rearrange(
                                    "p (d e) -> p d e", d=2), ALU.mult, ALU.add).then_inc(R.st_ev, 1)
                ch.reset()

            def prep_q(h, c, part):
                s = slice(c * CH, (c + 1) * CH)
                if part == 0:
                    ch(dve.tensor_copy(PP[:, s], FG[:, s]))
                for l in (range(0, 3), range(3, LEV))[part]:
                    w = 1 << l
                    n = CH if l < LEVS or c < NC - 1 else CH - P
                    v = lambda x: x[:, c * CH:c * CH + n].rearrange("p (g a w) -> p g a w", a=2, w=w)
                    q = QE[c % 2][:, l, 0:n // 2].rearrange("p (g w) -> p g w", w=w)
                    pp = v(PP)
                    dve.tensor_tensor(q, v(HZ[0])[:, :, 1, :], pp[:, :, 1, :], ALU.mult)
                    ch(dve.tensor_tensor(pp[:, :, 1, :], pp[:, :, 1, :],
                                         pp[:, :, 0, w - 1:w].to_broadcast([P, n // (2 * w), w]), ALU.mult))
                if part == 1:
                    ch(dve.tensor_tensor(QP[:, s], HZ[0][:, s], PP[:, s], ALU.mult))
                    dve.sem_inc(H.q_ok, 1)

            def weights(h, t):
                dve.wait_ge(H.sc, 9 * h + t + 1)
                dve.wait_ge(H.st_full, 16 * h + (t if t >= 2 else 1))
                dve.wait_ge(H.kv, 9 * h + t + 2)
                at = ATT[t % 2]
                ch(dve.tensor_tensor(at[:, :], PSC[:, 0:P], ident[:, :], ALU.mult))
                for l in range(LEV if t < NT - 1 else LEVS):
                    w = 1 << l
                    src = PSC[:, P + 64 * l:P + 64 * (l + 1)] if l < 6 else PT[:, 2 * P:2 * P + 64]
                    g = lambda x: x.rearrange("p (g w) -> p g w", w=w)
                    last = dve.copy_predicated(at[:, :].rearrange("p (g a w) -> p g a w", a=2, w=w)[:, :, 1, :],
                                               g(MK[:, l, :]), g(src))
                    if l < (LEV if t < NT - 1 else LEVS) - 1:
                        ch(last)
                last.then_inc(H.att, 1)

            ret_done(dve)
            with dve.Fori(0, HH // 2) as i:
                for u in range(2):
                    h = 2 * i + u
                    for s in range(HG_SLOTS):
                        j, c = divmod(s, NC)
                        jj = HG_BLOCKS * u + j
                        n = 40 + 10 * i + jj
                        if c == 0:
                            wlo_block(n + 1, (jj + 1) % 2)
                        if s == 0:
                            dve.wait_ge(H.f_ok, h + 1)
                            ch(dve.tensor_scalar(FG[:, :], FG[:, :], LBC[:, 1, bass.ds(h, 1)], LBC[:, 0, bass.ds(h, 1)],
                                                 ALU.mult, ALU.add))
                            ch(dve.tensor_scalar(KK[:, :], FG[:, :], -1.0, 1.0, ALU.mult, ALU.add))
                            dve.sem_inc(H.fk, 1)
                            dve.wait_ge(H.in_[0], 16 * h + 16)
                        for x in range(NC):
                            if s == H_NORM[x]:
                                norm_sum(H, h, x, HD)
                            if s == H_NORM[x] + 1:
                                gated(H, h, x, 1, OH[:, x * CH:(x + 1) * CH].unsqueeze(1))
                        if s in (0, 1, 3, 4, 6, 7):
                            if s == 6:
                                dve.wait_ge(H.sc, 9 * h + 3)
                            prep_q(h, s // 3, s % 3)
                        if s >= 3 and s - 3 < NT:
                            weights(h, s - 3)
                        if s >= 4 and s - 4 < NT:
                            t = s - 4
                            if t < NT - 1:
                                dve.wait_ge(H.st_full, 16 * h + t + 2)
                                if t == 0:
                                    dve.wait_ge(H.sr_st, 16 * h + 16)
                                    dve.tensor_copy(SH[:, :], PST[:, 0:P]).then_inc(H.st_ev, 1)
                                else:
                                    dve.wait_ge(H.st_ev, 16 * h + t + 1)
                                    e = (t + 1) * P - 1
                                    dve.scalar_tensor_tensor(SH[:, :], SH[:, :], PP[:, e:e + 1], PST[:, 0:P],
                                                             ALU.mult, ALU.add).then_inc(H.st_ev, 1)
                            else:
                                dve.wait_ge(H.s8_in[0], 16 * h + 16)
                                for b in range(NS):
                                    e = TP + (b + 1) * TS - 1
                                    dve.wait_ge(H.st_full, 16 * h + b + 10)
                                    dve.scalar_tensor_tensor(SH8[:, b, :], SH8[:, b, :], PP[:, e:e + 1],
                                                             (PST, PRB)[b % 2][:, 0:P], ALU.mult, ALU.add).then_inc(H.st_ev, 1)
                    ch.reset()

            hg_done(dve)
            for br in range(2):
                for k in range(KT):
                    i = KT * br + k
                    dve.wait_ge(sp_hi, i + 1)
                    dve.tensor_tensor(XL[:, k, :], URAW[i % 2][:, :], plain(XH[:, k, :]), ALU.subtract).then_inc(sp_lo, 1)
                for k in range(KT):
                    i = KT * br + k
                    n = NRB + i
                    if n + 1 < NB1:
                        wlo_block(n + 1, (n + 1) % 2)
                    else:
                        wlo(W_OUT, WRAW[0][:, :], WOH[:, 0, :], WOL[:, 0, :])
                    dve.wait_ge(mg_ok, i + 1)
                    for c in range(NC):
                        s = slice(c * CH, (c + 1) * CH)
                        dve.wait_ge(mm, NC * n + c + 1)
                        if br == 0:
                            dve.tensor_tensor(MIX[:, k, s], psum[c][:, 0:CH], MG[i % 2][:, s], ALU.mult).then_inc(ev, 1)
                        else:
                            ch(dve.tensor_tensor(MG[i % 2][:, s], psum[c][:, 0:CH], MG[i % 2][:, s], ALU.mult))
                            dve.tensor_tensor(MIX[:, k, s], MIX[:, k, s], MG[i % 2][:, s], ALU.add).then_inc(ev, 1)
            for k in range(1, KT):
                w = W_OUT + k
                wlo(w, WRAW[w % 2][:, :], WOH[:, k, :], WOL[:, k, :])
            for k in range(KT):
                dve.wait_ge(sp_hi, 2 * KT + k + 1)
                dve.tensor_tensor(XL[:, k, :], MIX[:, k, :], plain(XH[:, k, :]), ALU.subtract).then_inc(sp_lo, 1)
            dve.wait_ge(gb_in, 16)
            DB = ((0, 1), (2, 7))
            for t in range(NT + 1):
                if t < NT:
                    dve.wait_ge(d_ss, t + 1)
                    ch(dve.tensor_tensor(dss[:, 2 * t:2 * t + 1], dss[:, 2 * t:2 * t + 1], dss[:, 2 * t + 1:2 * t + 2], ALU.add))
                    dve.tensor_scalar(dms[:, t:t + 1], dss[:, 2 * t:2 * t + 1], 1.0 / D, EPS, ALU.mult, ALU.add).then_inc(d_ms, 1)
                    dve.wait_ge(d_rs, t + 1)
                    if t >= 2:
                        dve.wait_ge(x1_st[t % 2], 16 * (t // 2))
                    dve.wait_ge(xi_in[t % 2], 16 * (t // 2 + 1))
                    for q in range(2):
                        ns = slice(512 * q, 512 * (q + 1))
                        ch(dve.scalar_tensor_tensor(X1R[t % 2][:, ns], psum[DB[t % 2][q]][:, :], drs[:, t:t + 1],
                                                    GB[:, ns], ALU.mult, ALU.mult))
                    dve.tensor_tensor(X1R[t % 2][:, :], X1R[t % 2][:, :], XI2[t % 2][:, :], ALU.add).then_inc(d_x1, 1)
                if t >= 1:
                    tt = NT + t - 1
                    norm_ms(tt)
                    norm_row(tt, X1R[(t - 1) % 2], HR2[tt % 2])
                if t == 3:
                    wlo_block(W_FFN, 0)
                if t >= 1:
                    norm_cols(NT + t - 1, TM2, 1, t - 1)
            ch.reset()
            NG = FF // 512
            dve.wait_ge(acc0, 1)
            dve.sem_inc(dn_ev, 1)

            def mlp(g, last):
                w0 = W_FFN + 1 + 8 * g

                def split(i):
                    q = (W_FFN + 1 + i) % 2
                    if i % 2 == 0:
                        wlo(w0 + i, WRAW[q][:, :], WDH[:, i // 2, :], WDL[:, i // 2, :])
                    else:
                        b = (i // 2 + 1) % 4
                        wlo(w0 + i, as_block(WRAW[q]), WHI[b % 2][:, :, :], WLO[b % 2][:, :, :])
                for b in range(4):
                    for c in range(NC):
                        if c == 0:
                            split(2 * b)
                        if c == 1 and b < 3:
                            split(2 * b + 1)
                        x = NC * b + c
                        dve.wait_ge(f_t1, 12 * g + x + 1)
                        if x >= 2:
                            dve.wait_ge(f_ul, 12 * g + x - 1)
                        dve.tensor_tensor(T2[x % 2][:, :], T1[x % 2][:, :], T1[x % 2][:, :], ALU.mult).then_inc(f_t2, 1)
                        dve.wait_ge(f_uh, 12 * g + x + 1)
                        us_ = slice(c * CH, (c + 1) * CH)
                        dve.tensor_tensor(UL[:, b, us_], T2[x % 2][:, :], plain(UH[:, b, us_]), ALU.subtract).then_inc(f_ul, 1)
                if not last:
                    split(7)
                for x in range(2 * NT):
                    t, q = divmod(x, 2)
                    ns = slice(512 * q, 512 * (q + 1))
                    dve.wait_ge(dn, 18 * g + x + 2)
                    dve.tensor_tensor(ACC[:, t, ns], ACC[:, t, ns], psum[3 + x % 5][:, :], ALU.add).then_inc(dn_ev, 1)
            with dve.Fori(0, NG - 1) as g:
                mlp(g, False)
            mlp(NG - 1, True)
            dve.wait_ge(gb_in, 32)
            for t in range(NT):
                dve.wait_ge(y_ss, t + 1)
                dve.tensor_scalar(yms[:, t:t + 1], yss[:, t:t + 1], 1.0 / D, EPS, ALU.mult, ALU.add).then_inc(y_ms, 1)
                dve.wait_ge(y_rs, t + 1)
                if t >= 2:
                    dve.wait_ge(y_st[t % 2], 16 * (t // 2))
                dve.wait_ge(x1_in[t % 2], 16 * (t // 2 + 1))
                ch(dve.scalar_tensor_tensor(OF[t % 2][:, :], ACC[:, t, :], yrs[:, t:t + 1], GF[:, :], ALU.mult, ALU.mult))
                dve.tensor_tensor(OF[t % 2][:, :], OF[t % 2][:, :], X1F[t % 2][:, :], ALU.add).then_inc(y_ok, 1)

        @block.gpsimd
        def _(pool):
            ch = Chain(pool, pool_ch)
            ch(pool.memset(mhalf[:, :], -0.5))

            def rsqrt(dst, src, n=1):
                e = mhalf[:, :] if n == 1 else mhalf[:, :].to_broadcast([P, n])
                return pool.tensor_tensor(dst, src, e, ALU.pow)

            for tt in range(NT):
                pool.wait_ge(n_ms, tt + 1)
                rsqrt(rsc[:, tt:tt + 1], msc[:, tt:tt + 1]).then_inc(n_rs, 1)
            ch.reset()

            def gate(K, h, c, ne, g):
                pool.wait_ge(K.sg, 3 * h + c + 1)
                pool.tensor_tensor(SG[:, 0:ne, :], SG[:, 0:ne, :], g, ALU.mult).then_inc(K.gt, 1)
                pool.wait_ge(K.ms, 3 * h + c + 2)
                if c:
                    pool.wait_ge(K.dg, 3 * h + c)
                rsqrt(RST[:, :], MS[:, :], TPC).then_inc(K.rs, 1)

            pool.wait_ge(c_in2, 48)
            with pool.Fori(0, RH) as h:
                pool.wait_ge(R.in_[1], 16 * h + 16)
                pool.wait_ge(R.att, 9 * h + 1)
                for c in range(NC):
                    s = slice(c * CH, (c + 1) * CH)
                    cs, sn = CS[:, 0, s], CS[:, 1, s]
                    pool.tensor_tensor(PTMP[:, 0, :], ZK[:, 0, s], sn, ALU.mult)
                    ch(pool.tensor_tensor(PTMP[:, 1, :], ZK[:, 1, s], cs, ALU.mult))
                    last = pool.tensor_tensor(KR[:, 1, s], PTMP[:, 0, :], PTMP[:, 1, :], ALU.add)
                    if c < NC - 1:
                        ch(last)
                last.then_inc(R.k_ok, 1)
                for c in range(NC):
                    gate(R, h, c, 2, ZG[c % 2][:, :, :])
                ch.reset()

            ret_done(pool)
            for i in range(2):
                ch(pool.memset(KE[i][:, :, :], 0.0))
            ch.reset()

            def prep_k(h, c):
                s = slice(c * CH, (c + 1) * CH)
                off, tot = 0, FG[:, s]
                pool.tensor_tensor(FT[:, 0:CH // 2], FG[:, c * CH:(c + 1) * CH:2], FG[:, c * CH + 1:(c + 1) * CH:2], ALU.mult)
                ch(pool.memset(RR[:, s], 1.0))
                for l in range(LEV):
                    w = 1 << l
                    n = CH if l < LEVS or c < NC - 1 else CH - P
                    v = lambda x: x[:, 0:n].rearrange("p (g a w) -> p g a w", a=2, w=w)
                    pairs = tot[:, 0:n // w].rearrange("p (g a) -> p g a", a=2)
                    rr = v(RR[:, s])
                    pool.tensor_tensor(v(KE[c % 2][:, l, :])[:, :, 0, :], v(KK[:, s])[:, :, 0, :], rr[:, :, 0, :], ALU.mult)
                    if l < LEV - 1:
                        nxt = FT[:, off:off + n // (2 * w)]
                        if l:
                            pool.tensor_tensor(nxt, pairs[:, :, 0], pairs[:, :, 1], ALU.mult)
                        off += n // (2 * w)
                    ch(pool.tensor_tensor(rr[:, :, 0, :], rr[:, :, 0, :],
                                          pairs[:, :, 1:2].to_broadcast([P, n // (2 * w), w]), ALU.mult))
                    tot = nxt
                ch(pool.tensor_tensor(KRH[:, s], KK[:, s], RR[:, s], ALU.mult))
                pool.sem_inc(H.k_ok, 1)

            with pool.Fori(0, HH) as h:
                pool.wait_ge(H.fk, h + 1)
                pool.wait_ge(H.att, 9 * h + 1)
                prep_k(h, 0)
                prep_k(h, 1)
                pool.wait_ge(H.att, 9 * h + 4)
                prep_k(h, 2)
                for c in range(NC):
                    gate(H, h, c, 1, HZ[3][:, c * CH:(c + 1) * CH].unsqueeze(1))
                ch.reset()

            for t in range(NT + 1):
                if t < NT:
                    pool.wait_ge(d_ms, t + 1)
                    rsqrt(drs[:, t:t + 1], dms[:, t:t + 1]).then_inc(d_rs, 1)
                if t >= 1:
                    tt = NT + t - 1
                    pool.wait_ge(n_ms, tt + 1)
                    rsqrt(rsc[:, tt:tt + 1], msc[:, tt:tt + 1]).then_inc(n_rs, 1)
            pool.wait_ge(n_xl, 4 * NT)
            pool.wait_ge(n_xh, 4 * NT)
            for i in range(2):
                pool.wait_ge(x1_st[i], 16 * ((NT + 1 - i) // 2))
            pool.memset(ACC[:, :, :], 0.0).then_inc(acc0, 1)
            for t in range(NT):
                pool.wait_ge(y_ms, t + 1)
                rsqrt(yrs[:, t:t + 1], yms[:, t:t + 1]).then_inc(y_rs, 1)


_INS = ["x_prompt", "x_sample", "state_ret", "state_hgrn", "w_in", "w_a", "w_b", "w_out", "w_up", "w_down",
        "g_post_mix", "g_post_ffn"]
_OUTS = [("y_p", (1, TP, D)), ("y_s", (NS, TS, D)), ("ret_p", (1, 1, RH, RD, RD)), ("hg_p", (1, 1, HH, HD, HD)),
         ("ret_s", (1, NS, RH, RD, RD)), ("hg_s", (1, NS, HH, HD, HD))]


def shape_tables(np):
    f = np.float32
    inv = (f(10000.0) ** (-np.arange(0, RD, 2, dtype=f) / f(RD))).astype(f)
    pos = np.concatenate([np.arange(TP), PAST + np.arange(NS * TS) % TS]).astype(f)
    ang = (inv[:, None] * pos[None, :]).astype(f)
    rope = np.stack([np.cos(ang), np.sin(ang)], axis=1).astype(f)
    gam = np.log(1.0 - np.exp(np.linspace(np.log(1.0 / 32), np.log(1.0 / 512), RH))).astype(f).astype(np.float64)
    i = np.arange(P)
    ret = np.zeros((RH, P, 4 * P + 12), f)
    for h in range(RH):
        lg = gam[h]
        ret[h, :, 0:P] = np.exp((i + 1) * lg)[None]
        ret[h, :, P:2 * P] = np.exp((i % TS + 1) * lg)[None]
        m, n = i[:, None], i[None, :]
        ret[h, :, 2 * P:3 * P] = np.where(m // 64 <= n // 64, np.exp(np.abs(n - m) * lg), 0) * RD ** -0.5
        ret[h, :, 3 * P:4 * P] = np.where(m // TS == n // TS, np.exp(np.abs(n - m) * lg), 0) * RD ** -0.5
        ret[h, :, 4 * P] = np.exp((P - 1 - i) * lg) * RD ** -0.5
        ret[h, :, 4 * P + 1] = np.exp(P * lg)
        ret[h, :, 4 * P + 2] = np.exp(TS * lg)
        for b in range(NS):
            ret[h, :, 4 * P + 3 + b] = np.where(i // TS == b, np.exp((TS - 1 - i % TS) * lg), 0) * RD ** -0.5
    mask = np.zeros((P, LEV, 64), np.uint32)
    for l in range(LEV):
        w = 1 << l
        t = np.arange(64) // w * 2 * w + w + np.arange(64) % w
        mask[:, l] = (i[:, None] // w == t[None, :] // w - 1)
    rows = (i[:, None] // TS == np.arange(NS)[None]).astype(f)
    return {"c_rope": rope, "c_ret": ret, "c_mask": mask, "c_rows": rows, "c_ident": np.eye(P, dtype=f)}


def kernel(**inputs):
    import numpy as _np
    import concourse.bacc as _bacc
    from concourse import mybir as _mybir
    from concourse.bass_utils import run_bass_kernel_spmd as _run

    nc = _bacc.Bacc("TRN2", target_bir_lowering=False, num_devices=1)
    data = {n: _np.ascontiguousarray(inputs[n]) for n in _INS}
    data["g_pre_cols"] = _np.ascontiguousarray(
        _np.stack([inputs["g_pre_mix"], inputs["g_pre_ffn"]]).reshape(2, KT, P).transpose(2, 0, 1))
    data["lb_cols"] = _np.ascontiguousarray(_np.asarray(inputs["lb_logits"]).reshape(2, HH, P).transpose(2, 0, 1))
    data.update(shape_tables(_np))
    arrays, a, o = {}, {}, {}
    for name, x in data.items():
        arrays[f"in_{name}"] = x
        a[name] = nc.dram_tensor(f"in_{name}", x.shape, _mybir.dt.from_np(x.dtype), kind="ExternalInput").ap()
    for name, shape in _OUTS:
        o[name] = nc.dram_tensor(f"out_{name}", shape, _mybir.dt.float32, kind="ExternalOutput").ap()
    scr = {n: nc.dram_tensor(f"scratch_{n}", s, _mybir.dt.float32, kind="Internal").ap()
           for n, s in (("z", (80, P, T)), ("u", (16, P, T)), ("x1", (T, D)))}
    program(nc, a, o, scr)
    r = _run(nc, [arrays], core_ids=[0])
    return tuple(r.results[0][f"out_{name}"] for name, _ in _OUTS)
```

```python
import concourse.bass as bass
from concourse import mybir
from contextlib import ExitStack

F32 = mybir.dt.float32
F32R = mybir.dt.float32r
U32 = mybir.dt.uint32
ALU = mybir.AluOpType
ACT = mybir.ActivationFunctionType

P = 128
D = 1024
KT = D // P
TP = 1024
NS, TS = 8, 16
T = TP + NS * TS
NT = T // P
NTP = TP // P
CH = T // 3
NC = 3
TPC = NT // NC
RH, RD = 4, 256
HH, HD = 8, 128
FF = 4 * D
DIN = 10 * D
LEV = 7
LEVS = 4
PAST = 512
EPS = 1e-6

RET_SLOTS = 8 * NC
HG_BLOCKS = 5
HG_SLOTS = HG_BLOCKS * NC
RA = 8
HA = 3
R_NORM = (12, 15, 18)
H_NORM = (8, 11, 13)


class Chain:

    def __init__(self, eng, sem):
        self.eng, self.sem, self.n = eng, sem, 0

    def __call__(self, ins):
        self.n += 1
        ins.then_inc(self.sem, 1)
        self.eng.wait_ge(self.sem, self.n)

    def reset(self):
        self.eng.sem_clear(self.sem)
        self.n = 0


def program(nc, a, o, scr):
    ctx = ExitStack()
    with ctx:
        def sem(name):
            return ctx.enter_context(nc.semaphore(name))

        def sb(name, shape, dt=F32, stack=ctx):
            return stack.enter_context(nc.sbuf_tensor(name, shape, dt))

        pf = ExitStack()
        GF, SQJ3 = sb("GF", [P, D], F32, pf), sb("SQJ3", [P, D], F32, pf)
        X1F = [sb(f"X1F{i}", [P, D], F32, pf) for i in range(2)]
        OF = [sb(f"OF{i}", [P, D], F32, pf) for i in range(2)]
        pf.close()

        XH, XL = sb("XH", [P, KT, T], F32R), sb("XL", [P, KT, T], F32R)
        WRAW = [sb(f"WRAW{i}", [P, 1024]) for i in range(2)]
        WHI = [sb(f"WHI{i}", [P, KT, P], F32R) for i in range(2)]
        WLO = [sb(f"WLO{i}", [P, KT, P], F32R) for i in range(2)]
        ident = sb("ident", [P, P])
        gcol = sb("gcol", [P, 2, KT])
        mhalf = sb("mhalf", [P, 1])
        LB = sb("LB", [P, 2, HH])
        LBM = sb("LBM", [P, HH])
        LBC = sb("LBC", [P, 2, HH])
        ssc = sb("ssc", [P, 2 * NT])
        msc = sb("msc", [P, 2 * NT])
        rsc = sb("rsc", [P, 2 * NT])
        dss, dms, drs = sb("dss", [P, 2 * NT]), sb("dms", [P, NT]), sb("drs", [P, NT])
        yss, yms, yrs = (sb(n, [P, NT]) for n in ("yss", "yms", "yrs"))
        psum = [ctx.enter_context(nc.psum_tensor(f"bank{i}", [P, 512], F32)) for i in range(8)]
        PT, PSC, PRB, PO, PST = psum[3], psum[4], psum[5], psum[6], psum[7]

        p0 = ExitStack()
        XR = [sb(f"XR{i}", [P, D], F32, p0) for i in range(2)]
        HR = [sb(f"HR{i}", [P, D], F32, p0) for i in range(2)]
        TM = [sb(f"TM{i}", [P, 4, P], F32, p0) for i in range(2)]
        SQJ = sb("SQJ", [P, D], F32, p0)
        p0.close()

        pa = ExitStack()
        ZST = [sb(f"ZST{i}", [P, T], F32, pa) for i in range(2)]
        KVT = [sb(f"KVT{i}", [P, 2, 256], F32, pa) for i in range(2)]
        ATT = [sb(f"ATT{i}", [P, P], F32, pa) for i in range(2)]
        SQ = sb("SQ", [P, 2, CH], F32, pa)
        SG = sb("SG", [P, 2, CH], F32, pa)
        MS = sb("MS", [P, TPC], F32, pa)
        RST = sb("RST", [P, TPC], F32, pa)
        DG = sb("DG", [P, TPC, P], F32, pa)
        UB = sb("UB", [P, 2, CH], F32, pa)
        ones = sb("ones", [P, P], F32, pa)
        MK = sb("MK", [P, LEV, 64], U32, pa)
        RM = sb("RM", [P, NS], F32, pa)

        pr = ExitStack()
        ZQ = sb("ZQ", [P, 2, T], F32, pr)
        ZK = sb("ZK", [P, 2, T], F32, pr)
        ZV = sb("ZV", [P, 2, T], F32, pr)
        ZG = [sb(f"ZG{i}", [P, 2, CH], F32, pr) for i in range(2)]
        QR = sb("QR", [P, 2, T], F32, pr)
        KR = sb("KR", [P, 2, T], F32, pr)
        QX = ZQ
        RTMP = sb("RTMP", [P, 2, CH], F32, pr)
        PTMP = sb("PTMP", [P, 2, CH], F32, pr)
        CS = sb("CS", [P, 2, T], F32, pr)
        HC = sb("HC", [P, 4 * P + 12], F32, pr)
        XI = HC[:, 0:2 * P].rearrange("p (a n) -> p a n", a=2)
        DM = HC[:, 2 * P:4 * P].rearrange("p (a n) -> p a n", a=2)
        ZETA, G128, G16 = (HC[:, 4 * P + i:4 * P + i + 1] for i in range(3))
        SR = sb("SR", [P, 2, RD], F32, pr)
        S8B = sb("S8B", [P, 4, 2, RD], F32, pr)
        S8A = ZK[:, :, :].rearrange("p a t -> p (a t)")[:, 0:4 * 2 * RD].rearrange("p (b d e) -> p b d e", b=4, d=2)
        KZ8 = [sb(f"KZ8{i}", [P, RD], F32, pr) for i in range(2)]
        pr.close()

        ph = ExitStack()
        HZ = [sb(f"HZ{i}", [P, T], F32, ph) for i in range(4)]
        FG = HZ[1]
        KK, PP, RR = (sb(n, [P, T], F32, ph) for n in ("KK", "PP", "RR"))
        QP, KRH = (sb(n, [P, T], F32, ph) for n in ("QP", "KRH"))
        OH = QP
        QE = [sb(f"QE{i}", [P, LEV, CH // 2], F32, ph) for i in range(2)]
        KE = [sb(f"KE{i}", [P, LEV, CH], F32, ph) for i in range(2)]
        FT = sb("FT", [P, CH], F32, ph)
        SH = sb("SH", [P, HD], F32, ph)
        SH8 = sb("SH8", [P, NS, HD], F32, ph)
        KM8 = [sb(f"KM8{i}", [P, HD], F32, ph) for i in range(2)]
        NU = 3
        URAW = [sb(f"URAW{i}", [P, CH], F32, ph) for i in range(NU)]
        ph.close()
        pa.close()

        pb = ExitStack()
        MIX = sb("MIX", [P, KT, T], F32, pb)
        sb("hold_wo", [P, 2 * KT * D - 2 * T], F32, pb)
        MG = [sb(f"MG{i}", [P, T], F32, pb) for i in range(2)]
        pb.close()

        pd = ExitStack()
        sb("hold_mix", [P, KT, T], F32, pd)
        WOH, WOL = sb("WOH", [P, KT, D], F32R, pd), sb("WOL", [P, KT, D], F32R, pd)
        pd.close()
        pd2 = ExitStack()
        XI2 = [sb(f"XI2{i}", [P, D], F32, pd2) for i in range(2)]
        X1R = [sb(f"X1R{i}", [P, D], F32, pd2) for i in range(2)]
        HR2 = [sb(f"HR2{i}", [P, D], F32, pd2) for i in range(2)]
        TM2 = [sb(f"TM2{i}", [P, 4, P], F32, pd2) for i in range(2)]
        SQJ2 = sb("SQJ2", [P, D], F32, pd2)
        GB = sb("GB", [P, D], F32, pd2)
        pd2.close()
        pe_ = ExitStack()
        UH, UL = sb("UH", [P, 4, T], F32R, pe_), sb("UL", [P, 4, T], F32R, pe_)
        ACC = sb("ACC", [P, NT, D], F32, pe_)
        WDH, WDL = sb("WDH", [P, 4, D], F32R, pe_), sb("WDL", [P, 4, D], F32R, pe_)
        T1 = [sb(f"T1{i}", [P, CH], F32, pe_) for i in range(2)]
        T2 = [sb(f"T2{i}", [P, CH], F32, pe_) for i in range(2)]
        pe_.close()
        w_raw = [sem("w_raw0"), sem("w_raw1")]
        w_hi, w_lo = sem("w_hi"), sem("w_lo")
        mm = sem("mm")
        ev = sem("ev")
        z_st = [sem("z_st0"), sem("z_st1")]
        c_in = sem("c_in")
        c_in2 = sem("c_in2")
        lb_ch, lb_e = sem("lb_ch"), sem("lb_e")
        act_ch, dve_ch, pool_ch = sem("act_ch"), sem("dve_ch"), sem("pool_ch")
        x_in = [sem("x_in0"), sem("x_in1")]
        n_ss, n_ms, n_rs, n_hr = sem("n_ss"), sem("n_ms"), sem("n_rs"), sem("n_hr")
        n_tp, n_tm, n_xh, n_xl = sem("n_tp"), sem("n_tm"), sem("n_xh"), sem("n_xl")

        class Heads:

            def __init__(self, k):
                self.in_ = [sem(f"{k}_in{i}") for i in range(4)]
                self.g_in = [sem(f"{k}_g_in0"), sem(f"{k}_g_in1")]
                self.s8_in = [sem(f"{k}_s8_in0"), sem(f"{k}_s8_in1")]
                self.q_ok, self.k_ok = sem(f"{k}_q_ok"), sem(f"{k}_k_ok")
                self.f_ok, self.fk = sem(f"{k}_f_ok"), sem(f"{k}_fk")
                self.t_full, self.kv = sem(f"{k}_t_full"), sem(f"{k}_kv")
                self.sc, self.att = sem(f"{k}_sc"), sem(f"{k}_att")
                self.o_full, self.o_ev = sem(f"{k}_o_full"), sem(f"{k}_o_ev")
                self.st_full, self.st_ev = sem(f"{k}_st_full"), sem(f"{k}_st_ev")
                self.kz8 = sem(f"{k}_kz8")
                self.sq, self.rb, self.ms = sem(f"{k}_sq"), sem(f"{k}_rb"), sem(f"{k}_ms")
                self.sg, self.w_ok, self.u_ok = sem(f"{k}_sg"), sem(f"{k}_w_ok"), sem(f"{k}_u_ok")
                self.rs, self.dg, self.rbb, self.gt = (sem(f"{k}_{x}") for x in ("rs", "dg", "rbb", "gt"))
                self.u_st, self.sr_st = sem(f"{k}_u_st"), sem(f"{k}_sr_st")
                self.s8_st = [sem(f"{k}_s8_st0"), sem(f"{k}_s8_st1")]

        R, H = Heads("r"), Heads("h")
        ur_in = [sem(f"ur_in{i}") for i in range(NU)]
        mg_in = [sem("mg_in0"), sem("mg_in1")]
        sp_hi, sp_lo = sem("sp_hi"), sem("sp_lo")
        mg_ok = sem("mg_ok")
        mtm_ok = sem("mtm_ok")
        gb_in, xi_in = sem("gb_in"), [sem("xi_in0"), sem("xi_in1")]
        d_mm, d_ss, d_ms, d_rs, d_x1 = sem("d_mm"), sem("d_ss"), sem("d_ms"), sem("d_rs"), sem("d_x1")
        x1_st = [sem("x1_st0"), sem("x1_st1")]
        f_t1, f_t2, f_uh, f_ul = sem("f_t1"), sem("f_t2"), sem("f_uh"), sem("f_ul")
        dn, dn_ev = sem("dn"), sem("dn_ev")
        acc0 = sem("acc0")
        x1_in = [sem("x1_in0"), sem("x1_in1")]
        y_ss, y_ms, y_rs, y_ok = sem("y_ss"), sem("y_ms"), sem("y_rs"), sem("y_ok")
        y_st = [sem("y_st0"), sem("y_st1")]

        zs, us, x1s = scr["z"], scr["u"], scr["x1"]
        NRB = 10 * KT
        NB1 = NRB + 2 * KT
        W_OUT = NB1
        W_FFN = W_OUT + KT

        LATE = 5

        def half(n):
            return n // 2, n % 2

        def z_block(n):
            if n < 32:
                h, j = divmod(n, 8)
                return (j // 2) * D + h * RD + (j % 2) * P, n
            if n < 40:
                h, j = divmod(n - 32, 4)
                return (4 + j) * D + h * HD, n
            i, j = divmod(n - 40, HG_BLOCKS)
            if i < 6 and j < 4:
                return (4 + j) * D + (i + 2) * HD, 40 + 4 * i + j
            mi = i if i < 6 else 6 + (n - 70)
            return 8 * D + mi * P, 64 + mi

        def w_item(n):
            k = n - NRB - KT
            return n if k < 0 else n + min(k, LATE)

        def w_row(k):
            return w_item(NRB + KT + k) + 1 if k < LATE else NB1 + k

        def w_src(w):
            if w < NRB:
                c = z_block(w)[0]
                return a["w_in"][0, :, c:c + P].rearrange("(k p) n -> p k n", p=P)
            if w < NRB + KT:
                c = (w - NRB) * P
                return a["w_a"][0, :, c:c + P].rearrange("(k p) n -> p k n", p=P)
            for k in range(KT):
                if w == w_row(k):
                    return a["w_out"][0, k * P:(k + 1) * P, :].rearrange("p (k n) -> p k n", n=P)
                if w == w_item(NRB + KT + k):
                    return a["w_b"][0, :, k * P:(k + 1) * P].rearrange("(k p) n -> p k n", p=P)

        def as_block(t):
            return t[:, :].rearrange("p (k n) -> p k n", k=KT)

        def plain(x):
            return x.bitcast(F32)

        def y_store(sp, t):
            sp.wait_ge(y_ok, t + 1)
            dst = o["y_p"][0, t * P:(t + 1) * P, :] if t < NTP else o["y_s"].rearrange("b t d -> (b t) d")
            sp.dma_start(dst, OF[t % 2][:, :]).then_inc(y_st[t % 2], 16)

        def ret_done(e):
            e.wait_ge(R.u_st, 16 * 3 * RH + 16)
            e.wait_ge(R.sr_st, 16 * RH + 16)
            for s in R.s8_st:
                e.wait_ge(s, 32 * RH + 16)

        def hg_done(e):
            e.wait_ge(H.u_st, 16 * 3 * HH + 16)
            e.wait_ge(H.sr_st, 16 * HH + 16)
            e.wait_ge(H.s8_st[0], 16 * HH + 16)
            for q in range(2):
                e.wait_ge(z_st[q], 16 * NRB // 2)

        block = ctx.enter_context(nc.Block())

        @block.sync
        def _(sp):
            def load_w(w):
                m, p = half(w)
                if w >= 2:
                    sp.wait_ge(w_lo, w - 1)
                sp.dma_start(as_block(WRAW[p]), w_src(w)).then_inc(w_raw[p], 16)

            def store_z(n):
                m, p = half(n)
                sp.wait_ge(ev, NC * n + NC)
                sp.dma_start(zs[z_block(n)[1]], ZST[p][:, :]).then_inc(z_st[p], 16)

            def z_stored(n):
                for q in (n, n - 1):
                    if q >= 0:
                        sp.wait_ge(z_st[q % 2], 16 * (q // 2 + 1))

            def rows(tt, dst, s):
                src = a["x_prompt"][0, tt * P:(tt + 1) * P, :] if tt < NTP else \
                    a["x_sample"].rearrange("b t d -> (b t) d")
                sp.dma_start(dst[:, :], src).then_inc(s, 16)

            def store_u(h, c):
                sp.wait_ge(H.u_ok, 3 * h + c + 2)
                sp.dma_start(us[KT + h, :, c * CH:(c + 1) * CH], UB[:, 0, :]).then_inc(H.u_st, 16)

            rows(0, XR[0], x_in[0])
            rows(1, XR[1], x_in[1])
            sp.dma_start(ident[:, :], a["c_ident"]).then_inc(c_in, 16)
            sp.dma_start(gcol[:, :, :], a["g_pre_cols"]).then_inc(c_in, 16)
            sp.dma_start(LB[:, :, :], a["lb_cols"]).then_inc(c_in, 16)
            load_w(0)
            load_w(1)
            for tt in range(2, NT):
                sp.wait_ge(n_hr, tt - 1)
                rows(tt, XR[tt % 2], x_in[tt % 2])
            sp.wait_ge(n_xl, 2 * NT)
            sp.wait_ge(n_xh, 2 * NT)
            sp.dma_start(CS[:, :, :], a["c_rope"]).then_inc(c_in2, 16)
            sp.dma_start(MK[:, :, :], a["c_mask"]).then_inc(c_in2, 16)
            sp.dma_start(RM[:, :], a["c_rows"]).then_inc(c_in2, 16)
            for s in (R.u_st, R.sr_st, *R.s8_st, H.u_st, H.sr_st, *H.s8_st):
                sp.sem_inc(s, 16)

            for n in range(8):
                load_w(n + 2)
                if n:
                    store_z(n - 1)

            for h in range(RH):
                for j in range(8):
                    n = 8 + 8 * h + j
                    load_w(n + 2)
                    store_z(n - 1)
                    if j == 0:
                        z_stored(n - 1)
                        if h:
                            sp.wait_ge(R.o_ev, 9 * h + 1)
                            sp.wait_ge(R.u_ok, 3 * h + 1)
                            sp.wait_ge(R.st_ev, 16 * h + 1)
                        z = zs[8 * h:8 * h + 8].rearrange("(g e) p t -> g p e t", e=2)
                        sp.dma_start(HC[:, :], a["c_ret"][h]).then_inc(R.in_[3], 16)
                        sp.dma_start(ZQ[:, :, :], z[0]).then_inc(R.in_[0], 16)
                        if h:
                            sp.wait_ge(R.s8_st[0], 32 * h + 16)
                        sp.dma_start(ZK[:, :, :], z[1]).then_inc(R.in_[1], 16)
                        sp.dma_start(ZV[:, :, :], z[2]).then_inc(R.in_[2], 16)
                        if h:
                            sp.wait_ge(R.s8_st[1], 32 * h + 16)
                        for d in range(2):
                            sp.dma_start(S8B[:, :, d, :], a["state_ret"][0, 4:8, h, d * P:(d + 1) * P, :]
                                         .rearrange("b p e -> p b e")).then_inc(R.s8_in[1], 16)
                        for c in range(2):
                            sp.dma_start(ZG[c][:, :, :], z[3][:, :, c * CH:(c + 1) * CH]).then_inc(R.g_in[c], 16)
                    if j == 2:
                        sp.wait_ge(R.k_ok, h + 1)
                        sp.wait_ge(R.q_ok, h + 1)
                        for d in range(2):
                            sp.dma_start(S8A[:, :, d, :], a["state_ret"][0, 0:4, h, d * P:(d + 1) * P, :]
                                         .rearrange("b p e -> p b e")).then_inc(R.s8_in[0], 16)
                    for c in range(NC):
                        if j == (4, 5, 7)[c]:
                            if c == 0:
                                sp.wait_ge(R.gt, 3 * h + 1)
                                sp.dma_start(ZG[0][:, :, :], z[3][:, :, 2 * CH:]).then_inc(R.g_in[0], 16)
                            sp.wait_ge(R.u_ok, 3 * h + c + 2)
                            sp.dma_start(us[2 * h:2 * h + 2, :, c * CH:(c + 1) * CH].rearrange("e p t -> p e t"),
                                         UB[:, :, :]).then_inc(R.u_st, 16)
                sp.wait_ge(R.st_ev, 16 * h + 9)
                sp.dma_start(o["ret_p"][0, 0, h].rearrange("(d p) e -> p d e", p=P), SR[:, :, :]).then_inc(R.sr_st, 16)
                sp.wait_ge(R.st_ev, 16 * h + 17)
                for g, t8 in enumerate((S8A, S8B[:, :, :, :])):
                    for d in range(2):
                        sp.dma_start(o["ret_s"][0, 4 * g:4 * g + 4, h, d * P:(d + 1) * P, :]
                                     .rearrange("b p e -> p b e"), t8[:, :, d, :]).then_inc(R.s8_st[g], 16)

            def load_q(h):
                for i in (1, 0, 2):
                    sp.dma_start(HZ[i][:, :], zs[32 + 4 * h + i]).then_inc(H.in_[i], 16)

            def load_u(br, x):
                i = 3 * KT * br + x
                c, k = divmod(x, KT)
                if i >= NU:
                    sp.wait_ge(sp_lo, i - NU + 1)
                sp.dma_start(URAW[i % NU][:, :], us[KT * br + k, :, c * CH:(c + 1) * CH]).then_inc(ur_in[i % NU], 16)

            ret_done(sp)
            z_stored(38)
            load_q(0)
            for h in range(HH):
                for j in range(HG_BLOCKS):
                    n = 40 + HG_BLOCKS * h + j
                    load_w(n + 2)
                    store_z(n - 1)
                    if j == 0:
                        z_stored(n - 1)
                        if h:
                            sp.wait_ge(H.u_ok, 3 * h + 1)
                            sp.wait_ge(H.s8_st[0], 16 * h + 16)
                        sp.dma_start(HZ[3][:, :], zs[35 + 4 * h]).then_inc(H.in_[3], 16)
                        sp.dma_start(SH8[:, :, :], a["state_hgrn"][0, :, h].rearrange("b p e -> p b e"))\
                            .then_inc(H.s8_in[0], 16)
                    if j == HG_BLOCKS - 1 and h < HH - 1:
                        sp.wait_ge(H.att, 9 * h + 10)
                        load_q(h + 1)
                    for c in range(NC):
                        if j == (3, 4, 4)[c] and c < 2:
                            store_u(h, c)
                if h == HH - 1:
                    for x in range(2 * KT):
                        load_u(0, x)
                store_u(h, 2)
                sp.wait_ge(H.st_ev, 16 * h + 9)
                sp.dma_start(o["hg_p"][0, 0, h], SH[:, :]).then_inc(H.sr_st, 16)
                sp.wait_ge(H.st_ev, 16 * h + 17)
                sp.dma_start(o["hg_s"][0, :, h].rearrange("b p e -> p b e"), SH8[:, :, :]).then_inc(H.s8_st[0], 16)

            for x in range(2 * KT, 3 * KT):
                load_u(0, x)
            store_z(NRB - 1)
            hg_done(sp)
            for k in range(2 * KT):
                n = NRB + k
                if k >= 2:
                    sp.wait_ge(ev, NC * (n - 2) + NC)
                sp.dma_start(MG[k % 2][:, :], zs[64 + k]).then_inc(mg_in[k % 2], 16)
                for w in range(w_item(n + 1) + 1, (w_item(n + 2) if k < 2 * KT - 2 else w_item(n + 1)) + 1):
                    load_w(w)
                if k == KT - 1:
                    for x in range(3 * KT):
                        load_u(1, x)
            for k in range(LATE, KT):
                load_w(w_row(k))
            sp.wait_ge(w_lo, W_FFN - 1)
            sp.dma_start(as_block(WRAW[0]), a["w_up"][0, :, 0:P].rearrange("(k p) n -> p k n", p=P)).then_inc(w_raw[0], 16)
            sp.wait_ge(sp_lo, 9 * KT)
            sp.wait_ge(sp_hi, 9 * KT)
            sp.dma_start(GB[:, :], a["g_post_mix"].to_broadcast([P, D])).then_inc(gb_in, 16)
            for t in range(NT):
                if t >= 2:
                    sp.wait_ge(d_x1, t - 1)
                rows(t, XI2[t % 2], xi_in[t % 2])
                if t >= 1:
                    sp.wait_ge(d_x1, t)
                    sp.dma_start(x1s[(t - 1) * P:t * P, :], X1R[(t - 1) % 2][:, :]).then_inc(x1_st[(t - 1) % 2], 16)
            sp.wait_ge(d_x1, NT)
            sp.dma_start(x1s[(NT - 1) * P:, :], X1R[(NT - 1) % 2][:, :]).then_inc(x1_st[(NT - 1) % 2], 16)
            def mlp_w(g, last):
                for i in range(7):
                    w = W_FFN + 1 + 8 * g + i
                    sp.wait_ge(w_lo, w - 1)
                    s = w_raw[(W_FFN + 1 + i) % 2]
                    dst = WRAW[(W_FFN + 1 + i) % 2]
                    if i % 2 == 0:
                        sp.dma_start(dst[:, :], a["w_down"][0, bass.ds(g * 512 + (i // 2) * P, P), :]).then_inc(s, 16)
                    else:
                        sp.dma_start(as_block(dst), a["w_up"][0, :, bass.ds(g * 512 + (i // 2 + 1) * P, P)]
                                     .rearrange("(k p) n -> p k n", p=P)).then_inc(s, 16)
                if not last:
                    w = W_FFN + 8 + 8 * g
                    sp.wait_ge(w_lo, w - 1)
                    sp.dma_start(as_block(WRAW[W_FFN % 2]), a["w_up"][0, :, bass.ds(g * 512 + 512, P)]
                                 .rearrange("(k p) n -> p k n", p=P)).then_inc(w_raw[W_FFN % 2], 16)

            with sp.Fori(0, FF // 512 - 1) as g:
                mlp_w(g, False)
            mlp_w(FF // 512 - 1, True)
            sp.wait_ge(mm, NC * NB1 + 12 * (FF // 512))
            for i in range(2):
                sp.wait_ge(x1_st[i], 16 * ((NT + 1 - i) // 2))
            sp.dma_start(GF[:, :], a["g_post_ffn"].to_broadcast([P, D])).then_inc(gb_in, 16)
            for t in range(NT):
                if t >= 2:
                    sp.wait_ge(y_ok, t - 1)
                sp.dma_start(X1F[t % 2][:, :], x1s[t * P:(t + 1) * P, :]).then_inc(x1_in[t % 2], 16)
                if t >= 1:
                    y_store(sp, t - 1)
            y_store(sp, NT - 1)
            for i in range(2):
                sp.wait_ge(y_st[i], 16 * ((NT + 1 - i) // 2))
            sp.wait_ge(H.sr_st, 16 * HH + 16)
            sp.wait_ge(H.s8_st[0], 16 * HH + 16)


        @block.tensor
        def _(pe):
            def norm_transpose(tt, src):
                b = 3 + 2 * (tt % 2)
                pe.wait_ge(n_hr, tt + 1)
                for g in range(2):
                    if tt >= 2:
                        pe.wait_ge(n_tm, 2 * (tt - 2) + g + 1)
                    for i in range(4):
                        k = 4 * g + i
                        last = pe.transpose(psum[b + g][:, i * P:(i + 1) * P], src[:, k * P:(k + 1) * P], ident[:, :])
                    last.then_inc(n_tp, 1)

            def gemm(n, m, p, c, first=False, w=None):
                if c == 0:
                    pe.wait_ge(w_lo, (n if w is None else w) + 1)
                if not first:
                    pe.wait_ge(ev, NC * (n - 1) + c + 1)
                s = slice(c * CH, (c + 1) * CH)
                for k in range(KT):
                    pe.matmul(psum[c][:, 0:CH], WHI[p][:, k, :], XH[:, k, s], start=(k == 0), stop=False)
                    pe.matmul(psum[c][:, 0:CH], WHI[p][:, k, :], XL[:, k, s], start=False, stop=False)
                    last = pe.matmul(psum[c][:, 0:CH], WLO[p][:, k, :], XH[:, k, s], start=False, stop=(k == KT - 1))
                last.then_inc(mm, 1)

            for s in (R.rb, H.rb, R.st_full, H.st_full):
                pe.sem_inc(s, 1)
            pe.wait_ge(c_in, 48)
            for c in range(NC):
                for tt in range(TPC * c, TPC * (c + 1)):
                    norm_transpose(tt, HR[tt % 2])
                if c:
                    pe.wait_ge(n_xh, 2 * TPC * c)
                    pe.wait_ge(n_xl, 2 * TPC * c)
                    gemm(0, 0, 0, c - 1, first=True)
            pe.wait_ge(n_xh, 2 * NT)
            pe.wait_ge(n_xl, 2 * NT)
            gemm(0, 0, 0, NC - 1, first=True)
            for c in range(NC):
                gemm(1, 0, 1, c)
            with pe.Fori(1, 4) as m:
                for p in range(2):
                    for c in range(NC):
                        gemm(2 * m + p, m, p, c)

            def ret_a(h, t):
                s = slice(t * P, (t + 1) * P)
                if t == 0:
                    pe.wait_ge(R.in_[2], 16 * h + 16)
                    pe.wait_ge(R.q_ok, h + 1)
                    pe.wait_ge(R.k_ok, h + 1)
                    pe.wait_ge(R.kz8, 8 * h + 1)
                pe.wait_ge(R.kv, 9 * h + t + 1)
                for e in range(2):
                    pe.transpose(PT[:, e * P:(e + 1) * P], ZV[:, e, s], ident[:, :])
                for e in range(2):
                    last = pe.transpose(PT[:, (2 + e) * P:(3 + e) * P], KR[:, e, s], ident[:, :])
                last.then_inc(R.t_full, 1)
                pe.wait_ge(R.att, 9 * h + t + 1)
                pe.matmul(PSC[:, 0:P], KR[:, 0, s], QR[:, 0, s], start=True, stop=False)
                pe.matmul(PSC[:, 0:P], KR[:, 1, s], QR[:, 1, s], start=False, stop=True).then_inc(R.sc, 1)

            def ret_b(h, t):
                s = slice(t * P, (t + 1) * P)
                kv, at = KVT[t % 2], ATT[t % 2]
                pe.wait_ge(R.kv, 9 * h + t + 2)
                pe.wait_ge(R.att, 9 * h + t + 2)
                pe.wait_ge(R.o_ev, 9 * h + t + 1)
                pe.wait_ge(R.st_ev, 16 * h + t + 1)
                if t == NT - 1:
                    pe.wait_ge(R.s8_in[0], 32 * h + 32)
                    pe.wait_ge(R.s8_in[1], 32 * h + 32)
                for e in range(2):
                    es = slice(e * P, (e + 1) * P)
                    last = pe.matmul(PO[:, es], kv[:, 0, es], at[:, :], start=(e == 0), stop=(t == 0), skip_group_check=True)
                    if 0 < t < NT - 1:
                        for d in range(2):
                            last = pe.matmul(PO[:, es], SR[:, d, es], QX[:, d, s], start=False, stop=(d == 1), skip_group_check=True)
                    if t == NT - 1:
                        for b in range(NS):
                            st = S8A[:, b, :, :] if b < 4 else S8B[:, b - 4, :, :]
                            for d in range(2):
                                last = pe.matmul(PO[:, e * P + b * TS:e * P + (b + 1) * TS], st[:, d, es],
                                                 QX[:, d, TP + b * TS:TP + (b + 1) * TS],
                                                 start=False, stop=(b == NS - 1 and d == 1), skip_group_check=True)
                last.then_inc(R.o_full, 1)
                if t < NT - 1:
                    for d in range(2):
                        last = pe.matmul(PST[:, d * RD:(d + 1) * RD], kv[:, 1, d * P:(d + 1) * P], kv[:, 0, :],
                                         start=(d == 0), stop=(d == 1), skip_group_check=True)
                    last.then_inc(R.st_full, 1)
                    return
                for b in range(NS):
                    bank = (PST, PRB)[b % 2]
                    pe.wait_ge(R.kz8, 8 * h + b + 2)
                    if b == 1:
                        pe.wait_ge(R.w_ok, 3 * h + 3)
                    if b >= 2:
                        pe.wait_ge(R.st_ev, 16 * h + 8 + b)
                    for d in range(2):
                        last = pe.matmul(bank[:, d * RD:(d + 1) * RD], KZ8[b % 2][:, d * P:(d + 1) * P], kv[:, 0, :],
                                         start=(d == 0), stop=(d == 1), skip_group_check=True)
                    last.then_inc(R.st_full, 1)

            def head_sum(K, h, c, ne):
                pe.wait_ge(K.sq, 3 * h + c + 1)
                pe.wait_ge(K.w_ok, 3 * h + c + 1)
                if c == 2:
                    pe.wait_ge(K.st_ev, 16 * h + 17)
                for r in range(TPC):
                    for e in range(ne):
                        last = pe.matmul(PRB[:, r:r + 1], SQ[:, e, r * P:(r + 1) * P], ones[:, 0:1],
                                         start=(e == 0), stop=(e == ne - 1))
                last.then_inc(K.rb, 1)

            def head_spread(K, h, c):
                pe.wait_ge(K.dg, 3 * h + c + 1)
                pe.matmul(PRB[:, 0:CH], ones[:, :], DG[:, :, :].rearrange("p r t -> p (r t)"),
                          start=True, stop=True).then_inc(K.rbb, 1)

            with pe.Fori(0, RH) as h:
                for s in range(RET_SLOTS):
                    j, c = divmod(s, NC)
                    gemm(8 + 8 * h + j, 4 + 4 * h + j // 2, j % 2, c)
                    for i in range(NC):
                        if s == R_NORM[i]:
                            head_sum(R, h, i, 2)
                        if s == R_NORM[i] + 1:
                            head_spread(R, h, i)
                    for t in range(NT):
                        if s == RA + t:
                            ret_a(h, t)
                        if s == RA + 1 + t:
                            ret_b(h, t)

            def hg_a(h, t):
                s = slice(t * P, (t + 1) * P)
                c, r = divmod(t, TPC)
                if t == 0:
                    pe.wait_ge(H.in_[2], 16 * h + 16)
                    pe.wait_ge(H.fk, h + 1)
                    pe.wait_ge(H.kz8, 8 * h + 1)
                if r == 0:
                    pe.wait_ge(H.q_ok, 3 * h + c + 1)
                    pe.wait_ge(H.k_ok, 3 * h + c + 1)
                pe.wait_ge(H.kv, 9 * h + t + 1)
                pe.wait_ge(H.att, 9 * h + t + 1)
                pe.transpose(PT[:, 0:P], HZ[2][:, s], ident[:, :])
                tr = pe.transpose(PT[:, P:2 * P], KRH[:, s], ident[:, :])
                if t == NT - 1:
                    tr.then_inc(H.t_full, 1)
                last = pe.matmul(PSC[:, 0:P], KK[:, s], HZ[0][:, s], start=True, stop=True, skip_group_check=True)
                kt = slice(r * P, (r + 1) * P)
                qt = slice(r * 64, (r + 1) * 64)
                for l in range(min(6, LEV if t < NT - 1 else LEVS)):
                    last = pe.matmul(PSC[:, P + 64 * l:P + 64 * (l + 1)], KE[c % 2][:, l, kt], QE[c % 2][:, l, qt],
                                     start=True, stop=True, skip_group_check=True)
                last.then_inc(H.sc, 1)
                if t < NT - 1:
                    last = pe.matmul(PT[:, 2 * P:2 * P + 64], KE[c % 2][:, 6, kt], QE[c % 2][:, 6, qt], start=True, stop=True)
                    last.then_inc(H.t_full, 1)

            def hg_b(h, t):
                s = slice(t * P, (t + 1) * P)
                kv, at = KVT[t % 2], ATT[t % 2]
                pe.wait_ge(H.kv, 9 * h + t + 2)
                pe.wait_ge(H.att, 9 * h + t + 2)
                pe.wait_ge(H.o_ev, 9 * h + t + 1)
                pe.wait_ge(H.st_ev, 16 * h + t + 1)
                if t == NT - 1:
                    pe.wait_ge(H.s8_in[0], 16 * h + 16)
                last = pe.matmul(PO[:, 0:P], kv[:, 0, 0:P], at[:, :], start=True, stop=(t == 0), skip_group_check=True)
                if 0 < t < NT - 1:
                    last = pe.matmul(PO[:, 0:P], SH[:, :], QP[:, s], start=False, stop=True, skip_group_check=True)
                if t == NT - 1:
                    for b in range(NS):
                        last = pe.matmul(PO[:, b * TS:(b + 1) * TS], SH8[:, b, :], QP[:, TP + b * TS:TP + (b + 1) * TS],
                                         start=False, stop=(b == NS - 1), skip_group_check=True)
                last.then_inc(H.o_full, 1)
                if t < NT - 1:
                    pe.matmul(PST[:, 0:P], kv[:, 1, 0:P], kv[:, 0, 0:P], start=True, stop=True).then_inc(H.st_full, 1)
                    return
                for b in range(NS):
                    pe.wait_ge(H.kz8, 8 * h + b + 2)
                    if b == 1:
                        pe.wait_ge(H.w_ok, 3 * h + 3)
                    if b >= 2:
                        pe.wait_ge(H.st_ev, 16 * h + 8 + b)
                    pe.matmul((PST, PRB)[b % 2][:, 0:P], KM8[b % 2][:, :], kv[:, 0, 0:P],
                              start=True, stop=True).then_inc(H.st_full, 1)

            pe.wait_ge(R.kv, 9 * RH + 1)
            pe.wait_ge(R.kz8, 8 * RH + 1)
            pe.wait_ge(R.att, 9 * RH + 1)
            pe.wait_ge(R.o_ev, 9 * RH + 1)
            pe.wait_ge(R.st_ev, 16 * RH + 1)
            pe.wait_ge(R.w_ok, 3 * RH + 1)
            def hg_pair(i):
                for u in range(2):
                    h = 2 * i + u
                    for s in range(HG_SLOTS):
                        j, c = divmod(s, NC)
                        jj = HG_BLOCKS * u + j
                        gemm(40 + 10 * i + jj, 20 + 5 * i + jj // 2, jj % 2, c)
                        for x in range(NC):
                            if s == H_NORM[x]:
                                head_sum(H, h, x, 1)
                            if s == H_NORM[x] + 1:
                                head_spread(H, h, x)
                        if s >= HA and s - HA < NT:
                            hg_a(h, s - HA)
                        if s > HA and s - HA - 1 < NT:
                            hg_b(h, s - HA - 1)

            with pe.Fori(0, HH // 2) as i:
                hg_pair(i)

            for br in range(2):
                for p in range(2):
                    for c in range(NC):
                        n = NRB + KT * br + p
                        if p == 0:
                            pe.wait_ge(sp_hi, 3 * KT * br + KT * (c + 1))
                            pe.wait_ge(sp_lo, 3 * KT * br + KT * (c + 1))
                        gemm(n, None, p, c, w=w_item(n))
                if br == 0:
                    with pe.Fori(1, KT // 2) as i:
                        for p in range(2):
                            for c in range(NC):
                                gemm(NRB + 2 * i + p, None, p, c)
                else:
                    for n in range(NRB + KT + 2, NB1):
                        for c in range(NC):
                            gemm(n, None, n % 2, c, w=w_item(n))

            pe.wait_ge(w_lo, W_OUT + KT)
            pe.wait_ge(ev, NC * NB1)
            pe.wait_ge(H.kv, 9 * HH + 1)
            pe.wait_ge(H.kz8, 8 * HH + 1)
            pe.wait_ge(H.att, 9 * HH + 1)
            pe.wait_ge(H.o_ev, 9 * HH + 1)
            pe.wait_ge(H.st_ev, 16 * HH + 1)
            pe.wait_ge(H.w_ok, 3 * HH + 1)
            DB = ((0, 1), (2, 7))
            for t in range(NT + 2):
                if t < NT:
                    s = slice(t * P, (t + 1) * P)
                    pe.wait_ge(sp_hi, 6 * KT + KT * (t // TPC + 1))
                    pe.wait_ge(sp_lo, 6 * KT + KT * (t // TPC + 1))
                    if t >= 2:
                        pe.wait_ge(d_x1, t - 1)
                    for q in range(2):
                        bank = psum[DB[t % 2][q]]
                        ns = slice(512 * q, 512 * (q + 1))
                        for k in range(KT):
                            pe.matmul(bank[:, :], XH[:, k, s], WOH[:, k, ns], start=(k == 0), stop=False)
                            pe.matmul(bank[:, :], XH[:, k, s], WOL[:, k, ns], start=False, stop=False)
                            last = pe.matmul(bank[:, :], XL[:, k, s], WOH[:, k, ns], start=False, stop=(k == KT - 1))
                    last.then_inc(d_mm, 1)
                if t >= 2:
                    norm_transpose(NT + t - 2, HR2[(NT + t - 2) % 2])

            pe.wait_ge(n_xh, 4 * NT)
            pe.wait_ge(n_xl, 4 * NT)
            pe.wait_ge(d_x1, NT)
            NG = FF // 512
            with pe.Fori(0, NG) as g:
                for b in range(4):
                    pe.wait_ge(w_lo, W_FFN + 8 * g + 2 * b + 1)
                    for c in range(NC):
                        if b:
                            pe.wait_ge(f_t1, NC * (4 * g + b - 1) + c + 1)
                        s = slice(c * CH, (c + 1) * CH)
                        for k in range(KT):
                            pe.matmul(psum[c][:, 0:CH], WHI[b % 2][:, k, :], XH[:, k, s], start=(k == 0), stop=False)
                            pe.matmul(psum[c][:, 0:CH], WHI[b % 2][:, k, :], XL[:, k, s], start=False, stop=False)
                            last = pe.matmul(psum[c][:, 0:CH], WLO[b % 2][:, k, :], XH[:, k, s], start=False, stop=(k == KT - 1))
                        last.then_inc(mm, 1)
                pe.wait_ge(w_lo, W_FFN + 8 * g + 8)
                pe.wait_ge(f_ul, 12 * g + 12)
                for t in range(NT):
                    s = slice(t * P, (t + 1) * P)
                    for q in range(2):
                        x = 2 * t + q
                        bank = psum[3 + x % 5]
                        ns = slice(512 * q, 512 * (q + 1))
                        if x >= 5:
                            pe.wait_ge(dn_ev, 18 * g + x - 5 + 2)
                        else:
                            pe.wait_ge(dn_ev, 18 * g + 1)
                        for k in range(4):
                            pe.matmul(bank[:, :], UH[:, k, s], WDH[:, k, ns], start=(k == 0), stop=False)
                            pe.matmul(bank[:, :], UH[:, k, s], WDL[:, k, ns], start=False, stop=False)
                            last = pe.matmul(bank[:, :], UL[:, k, s], WDH[:, k, ns], start=False, stop=(k == 3))
                        last.then_inc(dn, 1)

        @block.scalar
        def _(act):
            ch = Chain(act, act_ch)

            def copy(dst, src):
                return act.activation(dst, src, ACT.Copy)

            def whi(w, p, m, src, dst, free=None):
                act.wait_ge(w_raw[p], 16 * m + 16)
                if free is not None:
                    act.wait_ge(mm, free)
                copy(dst, src).then_inc(w_hi, 1)

            def whi_block(n, m, p, free=True):
                whi(n, p, m, as_block(WRAW[p]), WHI[p][:, :, :], 3 * n - 3 if free else None)

            def evac(n, m, p, c, first=False):
                act.wait_ge(mm, NC * n + c + 1)
                if c == 0 and not first:
                    act.wait_ge(z_st[p], 16 * m)
                copy(ZST[p][:, c * CH:(c + 1) * CH], psum[c][:, 0:CH]).then_inc(ev, 1)

            def norm_sq(tt, src, junk):
                if tt:
                    act.wait_ge(n_ss, tt)
                act.activation(junk[:, :], src[:, :], ACT.Square, accum_out=ssc[:, tt:tt + 1]).then_inc(n_ss, 1)

            def norm_xh(tt, tm, t):
                for g in range(2):
                    act.wait_ge(n_tm, 2 * tt + g + 1)
                    copy(XH[:, 4 * g:4 * g + 4, t * P:(t + 1) * P], tm[g][:, :, :]).then_inc(n_xh, 1)

            for tt in range(NT + 1):
                if tt < NT:
                    act.wait_ge(x_in[tt % 2], 16 * (tt // 2 + 1))
                    norm_sq(tt, XR[tt % 2], SQJ)
                if tt == 3:
                    whi_block(0, 0, 0, free=False)
                if tt == 4:
                    whi_block(1, 0, 1, free=False)
                if tt:
                    norm_xh(tt - 1, TM, tt - 1)
            act.wait_ge(lb_ch, 2)
            act.activation(LB[:, :, :], LB[:, :, :], ACT.Exp).then_inc(lb_e, 1)
            for s in (R.kv, R.o_ev, R.kz8, H.kv, H.o_ev, H.kz8):
                act.sem_inc(s, 1)

            def block_slot(n, m, p, c):
                if c == 0:
                    mn, pn = (m, 1) if p == 0 else (m + 1, 0)
                    whi_block(n + 1, mn, pn)
                evac(n, m, p, c)

            act.wait_ge(n_xl, 2 * NT)
            for n in range(2):
                for c in range(NC):
                    if c == 0 and n == 1:
                        whi_block(2, 1, 0)
                    evac(n, 0, n, c, first=True)
            with act.Fori(1, 4) as m:
                for p in range(2):
                    for c in range(NC):
                        block_slot(2 * m + p, m, p, c)

            def kv_ret(h, t):
                act.wait_ge(R.t_full, 9 * h + t + 1)
                act.wait_ge(R.st_full, 16 * h + (t if t >= 2 else 1))
                if t == 0:
                    act.wait_ge(R.in_[3], 16 * h + 16)
                if t < NT - 1:
                    copy(KVT[t % 2][:, 0, :], PT[:, 0:RD])
                    act.activation(KVT[t % 2][:, 1, :], PT[:, RD:2 * RD], ACT.Copy, scale=ZETA).then_inc(R.kv, 1)
                else:
                    copy(KVT[t % 2][:, 0, :], PT[:, 0:RD]).then_inc(R.kv, 1)

            def kz_ret(h):
                for b in range(NS):
                    if b >= 2:
                        act.wait_ge(R.st_full, 16 * h + 8 + b)
                    act.activation(KZ8[b % 2][:, :], PT[:, RD:2 * RD], ACT.Copy,
                                   scale=HC[:, 4 * P + 3 + b:4 * P + 4 + b]).then_inc(R.kz8, 1)

            def head_sq(K, h, c, ne, src, gate, g_in, g_v):
                act.wait_ge(K.o_ev, 9 * h + TPC * c + TPC + 1)
                act.wait_ge(K.rb, 3 * h + c + 1)
                act.activation(SQ[:, 0:ne, :], src, ACT.Square).then_inc(K.sq, 1)
                act.wait_ge(g_in, g_v)
                act.wait_ge(K.u_ok, 3 * h + c + 1)
                act.activation(SG[:, 0:ne, :], gate, ACT.Sigmoid).then_inc(K.sg, 1)

            with act.Fori(0, RH) as h:
                for s in range(RET_SLOTS):
                    j, c = divmod(s, NC)
                    block_slot(8 + 8 * h + j, 4 + 4 * h + j // 2, j % 2, c)
                    for t in range(NT):
                        if s == RA + t:
                            kv_ret(h, t)
                        if s == RA + 1 + t:
                            act.wait_ge(R.o_full, 9 * h + t + 1)
                            copy(QX[:, :, t * P:(t + 1) * P],
                                 PO[:, 0:RD].rearrange("p (e t) -> p e t", e=2)).then_inc(R.o_ev, 1)
                            if t == NT - 1:
                                kz_ret(h)
                    for i in range(NC):
                        if s == R_NORM[i] - 1:
                            g_v = 32 * h + (16, 16, 32)[i]
                            if i == 1:
                                g_v = 16 * h + 16
                            head_sq(R, h, i, 2, QX[:, :, i * CH:(i + 1) * CH], ZG[i % 2][:, :, :], R.g_in[i % 2], g_v)

            ret_done(act)

            def kv_hg(h, t):
                act.wait_ge(H.t_full, 9 * h + t + 1)
                act.wait_ge(H.st_full, 16 * h + (t if t >= 2 else 1))
                if t < NT - 1:
                    copy(KVT[t % 2][:, :, 0:P], PT[:, 0:2 * P].rearrange("p (a d) -> p a d", a=2)).then_inc(H.kv, 1)
                else:
                    copy(KVT[t % 2][:, 0, 0:P], PT[:, 0:P]).then_inc(H.kv, 1)

            def kz_hg(h):
                for b in range(NS):
                    if b >= 2:
                        act.wait_ge(H.st_full, 16 * h + 8 + b)
                    act.activation(KM8[b % 2][:, :], PT[:, P:2 * P], ACT.Copy, scale=RM[:, b:b + 1]).then_inc(H.kz8, 1)

            act.wait_ge(c_in2, 48)

            def forget(h):
                act.wait_ge(H.in_[1], 16 * h + 16)
                act.activation(FG[:, :], HZ[1][:, :], ACT.Sigmoid).then_inc(H.f_ok, 1)

            def piece(i):
                act.wait_ge(ur_in[i % NU], 16 * (i // NU + 1))
                c, k = divmod(i % (3 * KT), KT)
                copy(XH[:, k, c * CH:(c + 1) * CH], URAW[i % NU][:, :]).then_inc(sp_hi, 1)

            def hg_pair(i, last):
                for u in range(2):
                    h = 2 * i + u
                    end = last and u == 1
                    for s in range(HG_SLOTS):
                        j, c = divmod(s, NC)
                        jj = HG_BLOCKS * u + j
                        block_slot(40 + 10 * i + jj, 20 + 5 * i + jj // 2, jj % 2, c)
                        if s == HG_SLOTS - 2 and not end:
                            forget(h + 1)
                        if s >= HA and s - HA < NT:
                            kv_hg(h, s - HA)
                        if s > HA and s - HA - 1 < NT:
                            t = s - HA - 1
                            act.wait_ge(H.o_full, 9 * h + t + 1)
                            copy(OH[:, t * P:(t + 1) * P], PO[:, 0:P]).then_inc(H.o_ev, 1)
                            if t == NT - 1:
                                kz_hg(h)
                        for x in range(NC):
                            if s == H_NORM[x] - 1:
                                head_sq(H, h, x, 1, OH[:, x * CH:(x + 1) * CH].unsqueeze(1),
                                        HZ[3][:, x * CH:(x + 1) * CH].unsqueeze(1), H.in_[3], 16 * h + 16)
                        if end and j == HG_BLOCKS - 1:
                            for x in range(KT):
                                piece(KT * c + x)

            forget(0)
            with act.Fori(0, HH // 2 - 1) as i:
                hg_pair(i, False)
            hg_pair(HH // 2 - 1, True)

            for k in range(2 * KT):
                n = NRB + k
                act.wait_ge(mg_in[k % 2], 16 * (k // 2 + 1))
                act.activation(MG[k % 2][:, :], MG[k % 2][:, :], ACT.Sigmoid).then_inc(mg_ok, 1)
                if KT <= k < KT + LATE:
                    w = w_row(k - KT)
                    whi(w, w % 2, w // 2, WRAW[w % 2][:, :], WOH[:, k - KT, :])
                if n + 1 < NB1:
                    w = w_item(n + 1)
                    whi(w, w % 2, w // 2, as_block(WRAW[w % 2]), WHI[(n + 1) % 2][:, :, :], 3 * n)
                if k == KT - 1:
                    for c in range(NC):
                        act.wait_ge(mm, NC * n + c + 1)
                        for x in range(KT):
                            piece(3 * KT + KT * c + x)
            for k in range(LATE, KT):
                w = w_row(k)
                whi(w, w % 2, w // 2, WRAW[w % 2][:, :], WOH[:, k, :])
            for c in range(NC):
                act.wait_ge(ev, NC * (NB1 - 1) + c + 1)
                for k in range(KT):
                    copy(XH[:, k, c * CH:(c + 1) * CH], MIX[:, k, c * CH:(c + 1) * CH]).then_inc(sp_hi, 1)
            act.wait_ge(sp_lo, 9 * KT)
            act.wait_ge(gb_in, 16)
            DB = ((0, 1), (2, 7))
            for t in range(NT + 2):
                if t < NT:
                    act.wait_ge(d_mm, t + 1)
                    act.wait_ge(n_ss, NT + t)
                    if t:
                        act.wait_ge(d_ss, t)
                    for q in range(2):
                        last = act.activation(SQJ2[:, 512 * q:512 * (q + 1)], psum[DB[t % 2][q]][:, :], ACT.Square,
                                              accum_out=dss[:, 2 * t + q:2 * t + q + 1])
                    last.then_inc(d_ss, 1)
                if t == 3:
                    whi(W_FFN, 0, W_FFN // 2, as_block(WRAW[0]), WHI[0][:, :, :])
                if t >= 2:
                    norm_xh(NT + t - 2, TM2, t - 2)
                if t < NT:
                    act.wait_ge(d_x1, t + 1)
                    act.wait_ge(d_ss, t + 1)
                    act.activation(SQJ2[:, :], X1R[t % 2][:, :], ACT.Square, accum_out=ssc[:, NT + t:NT + t + 1]).then_inc(n_ss, 1)
            NG = FF // 512
            act.wait_ge(n_xl, 4 * NT)
            act.wait_ge(w_lo, W_FFN + 1)

            def mlp(g, last):
                w0 = W_FFN + 1 + 8 * g

                def split(i):
                    q = (W_FFN + 1 + i) % 2
                    m = (W_FFN + 1 + i) // 2 + 4 * g
                    if i % 2 == 0:
                        if i == 0:
                            act.wait_ge(dn, 18 * g + 1)
                        whi(w0 + i, q, m, WRAW[q][:, :], WDH[:, i // 2, :])
                    else:
                        b = (i // 2 + 1) % 4
                        whi(w0 + i, q, m, as_block(WRAW[q]), WHI[b % 2][:, :, :],
                            NC * (NB1 + 4 * g + i // 2))
                for b in range(4):
                    for c in range(NC):
                        if c == 0:
                            split(2 * b)
                        if c == 1 and b < 3:
                            split(2 * b + 1)
                        x = NC * b + c
                        act.wait_ge(mm, NC * NB1 + 12 * g + x + 1)
                        if x >= 2:
                            act.wait_ge(f_t2, 12 * g + x - 1)
                        act.activation(T1[x % 2][:, :], psum[c][:, 0:CH], ACT.Relu).then_inc(f_t1, 1)
                        act.wait_ge(f_t2, 12 * g + x + 1)
                        copy(UH[:, b, c * CH:(c + 1) * CH], T2[x % 2][:, :]).then_inc(f_uh, 1)
                if not last:
                    split(7)
            act.sem_inc(dn, 1)
            with act.Fori(0, NG - 1) as g:
                mlp(g, False)
            mlp(NG - 1, True)
            act.wait_ge(mm, NC * NB1 + 12 * NG)
            for t in range(NT):
                act.wait_ge(dn_ev, 18 * (NG - 1) + 2 * t + 3)
                if t:
                    act.wait_ge(y_ss, t)
                act.activation(SQJ3[:, :], ACC[:, t, :], ACT.Square, accum_out=yss[:, t:t + 1]).then_inc(y_ss, 1)

        @block.vector
        def _(dve):
            ch = Chain(dve, dve_ch)

            def wlo(w, src, hi, lo):
                dve.wait_ge(w_hi, w + 1)
                dve.tensor_tensor(lo, src, plain(hi), ALU.subtract).then_inc(w_lo, 1)

            def wlo_block(n, p):
                wlo(n, as_block(WRAW[p]), WHI[p][:, :, :], WLO[p][:, :, :])

            def norm_ms(tt):
                dve.wait_ge(n_ss, tt + 1)
                dve.tensor_scalar(msc[:, tt:tt + 1], ssc[:, tt:tt + 1], 1.0 / D, EPS, ALU.mult, ALU.add).then_inc(n_ms, 1)

            def norm_row(tt, src, dst):
                dve.wait_ge(n_rs, tt + 1)
                if tt >= 2:
                    dve.wait_ge(n_tp, 2 * (tt - 2) + 2)
                dve.tensor_scalar(dst[:, :], src[:, :], rsc[:, tt:tt + 1], None, ALU.mult).then_inc(n_hr, 1)

            def norm_cols(tt, tm, which, t):
                b = 3 + 2 * (tt % 2)
                for g in range(2):
                    dve.wait_ge(n_tp, 2 * tt + g + 1)
                    if tt:
                        dve.wait_ge(n_xh, 2 * (tt - 1) + g + 1)
                        dve.wait_ge(n_xl, 2 * (tt - 1) + g + 1)
                    gain = gcol[:, which, 4 * g:4 * g + 4].unsqueeze(2).to_broadcast([P, 4, P])
                    dve.tensor_tensor(tm[g][:, :, :], psum[b + g][:, :].rearrange("p (k t) -> p k t", k=4),
                                      gain, ALU.mult).then_inc(n_tm, 1)
                for g in range(2):
                    dve.wait_ge(n_xh, 2 * tt + g + 1)
                    ks, ts = slice(4 * g, 4 * g + 4), slice(t * P, (t + 1) * P)
                    dve.tensor_tensor(XL[:, ks, ts], tm[g][:, :, :], plain(XH[:, ks, ts]), ALU.subtract).then_inc(n_xl, 1)

            dve.wait_ge(c_in, 48)
            dve.tensor_tensor(LBM[:, :], LB[:, 0, :], LB[:, 1, :], ALU.max).then_inc(lb_ch, 1)
            dve.wait_ge(lb_ch, 1)
            dve.tensor_tensor(LB[:, :, :], LB[:, :, :], LBM[:, :].unsqueeze(1).to_broadcast([P, 2, HH]),
                              ALU.subtract).then_inc(lb_ch, 1)
            for tt in range(NT + 1):
                if tt < NT:
                    norm_ms(tt)
                    norm_row(tt, XR[tt % 2], HR[tt % 2])
                if tt == 4:
                    wlo_block(0, 0)
                if tt == 5:
                    wlo_block(1, 1)
                if tt:
                    norm_cols(tt - 1, TM, 0, tt - 1)
            dve.wait_ge(lb_e, 1)
            ch(dve.tensor_tensor(LBM[:, :], LB[:, 0, :], LB[:, 1, :], ALU.add))
            ch(dve.reciprocal(LBM[:, :], LBM[:, :]))
            ch(dve.tensor_tensor(LBC[:, 0, :], LB[:, 0, :], LBM[:, :], ALU.mult))
            ch(dve.tensor_scalar(LBC[:, 1, :], LBC[:, 0, :], -1.0, 1.0, ALU.mult, ALU.add))
            ch(dve.memset(ones[:, :], 1.0))
            ch.reset()
            for s in (R.att, R.st_ev, R.ms, R.u_ok, R.w_ok, H.att, H.st_ev, H.ms, H.u_ok, H.w_ok):
                dve.sem_inc(s, 1)

            wlo_block(2, 0)
            with dve.Fori(1, 4) as m:
                for p in range(2):
                    wlo_block(2 * m + p + 1, (p + 1) % 2)

            def norm_sum(K, h, c, width):
                dve.wait_ge(K.rb, 3 * h + c + 2)
                dve.tensor_scalar(MS[:, :], PRB[:, 0:TPC], 1.0 / width, EPS, ALU.mult, ALU.add).then_inc(K.ms, 1)
                dve.wait_ge(K.rs, 3 * h + c + 1)
                dve.tensor_tensor(DG[:, :, :], ident[:, :].unsqueeze(1).to_broadcast([P, TPC, P]),
                                  RST[:, :].unsqueeze(2).to_broadcast([P, TPC, P]), ALU.mult).then_inc(K.dg, 1)

            def gated(K, h, c, ne, src):
                dve.wait_ge(K.gt, 3 * h + c + 1)
                dve.wait_ge(K.rbb, 3 * h + c + 1)
                dve.tensor_tensor(SG[:, 0:ne, :], SG[:, 0:ne, :],
                                  PRB[:, 0:CH].unsqueeze(1).to_broadcast([P, ne, CH]), ALU.mult).then_inc(K.w_ok, 1)
                dve.wait_ge(K.w_ok, 3 * h + c + 2)
                dve.wait_ge(K.u_st, 48 * h + 16 * c + 16)
                dve.tensor_tensor(UB[:, 0:ne, :], SG[:, 0:ne, :], src, ALU.mult).then_inc(K.u_ok, 1)

            def rotate_q(h, c):
                s = slice(c * CH, (c + 1) * CH)
                cs, sn = CS[:, 0, s], CS[:, 1, s]
                dve.tensor_tensor(RTMP[:, 0, :], ZQ[:, 0, s], cs, ALU.mult)
                ch(dve.tensor_tensor(RTMP[:, 1, :], ZQ[:, 1, s], sn, ALU.mult))
                ch(dve.tensor_tensor(QR[:, 0, s], RTMP[:, 0, :], RTMP[:, 1, :], ALU.subtract))
                dve.tensor_tensor(RTMP[:, 0, :], ZQ[:, 0, s], sn, ALU.mult)
                ch(dve.tensor_tensor(RTMP[:, 1, :], ZQ[:, 1, s], cs, ALU.mult))
                ch(dve.tensor_tensor(QR[:, 1, s], RTMP[:, 0, :], RTMP[:, 1, :], ALU.add))
                n = TPC if c < NC - 1 else TPC - 1
                for d in range(2):
                    v = lambda x: x[:, d, c * CH:c * CH + n * P].rearrange("p (a t) -> p a t", t=P)
                    last = dve.tensor_tensor(v(QX), v(QR), XI[:, 0, :].unsqueeze(1).to_broadcast([P, n, P]), ALU.mult)
                    if c == NC - 1:
                        last = dve.tensor_tensor(QX[:, d, TP:T], QR[:, d, TP:T], XI[:, 1, :], ALU.mult)
                ch(last)

            def rotate_k0(c):
                s = slice(c * CH, (c + 1) * CH)
                dve.tensor_tensor(RTMP[:, 0, :], ZK[:, 0, s], CS[:, 0, s], ALU.mult)
                ch(dve.tensor_tensor(RTMP[:, 1, :], ZK[:, 1, s], CS[:, 1, s], ALU.mult))
                ch(dve.tensor_tensor(KR[:, 0, s], RTMP[:, 0, :], RTMP[:, 1, :], ALU.subtract))

            dve.wait_ge(c_in2, 48)
            with dve.Fori(0, RH) as h:
                for s in range(RET_SLOTS):
                    j, c = divmod(s, NC)
                    n = 8 + 8 * h + j
                    if c == 0:
                        wlo_block(n + 1, (j + 1) % 2)
                    for i in range(NC):
                        if s == R_NORM[i]:
                            norm_sum(R, h, i, RD)
                        if s == R_NORM[i] + 1:
                            gated(R, h, i, 2, QX[:, :, i * CH:(i + 1) * CH])
                    if s < 3:
                        if s == 0:
                            dve.wait_ge(R.in_[0], 16 * h + 16)
                            dve.wait_ge(R.in_[3], 16 * h + 16)
                        rotate_q(h, s)
                    if s == 3:
                        dve.wait_ge(R.in_[1], 16 * h + 16)
                        for c in range(NC):
                            rotate_k0(c)
                        dve.sem_inc(R.q_ok, 1)
                    for t in range(NT):
                        if s == RA + t:
                            dve.wait_ge(R.sc, 9 * h + t + 1)
                            dve.wait_ge(R.st_full, 16 * h + (t if t >= 2 else 1))
                            dve.tensor_tensor(ATT[t % 2][:, :], PSC[:, 0:P], DM[:, t // NTP, :], ALU.mult).then_inc(R.att, 1)
                        if s == RA + 1 + t and t < NT - 1:
                            dve.wait_ge(R.st_full, 16 * h + t + 2)
                            pst = PST[:, :].rearrange("p (d e) -> p d e", d=2)
                            if t == 0:
                                dve.wait_ge(R.sr_st, 16 * h + 16)
                                dve.tensor_copy(SR[:, :, :], pst).then_inc(R.st_ev, 1)
                            else:
                                dve.wait_ge(R.st_ev, 16 * h + t + 1)
                                dve.scalar_tensor_tensor(SR[:, :, :], SR[:, :, :], G128, pst, ALU.mult, ALU.add)\
                                   .then_inc(R.st_ev, 1)
                        if s == RA + 1 + t and t == NT - 1:
                            dve.wait_ge(R.s8_in[0], 32 * h + 32)
                            dve.wait_ge(R.s8_in[1], 32 * h + 32)
                            for b in range(NS):
                                st = S8A[:, b, :, :] if b < 4 else S8B[:, b - 4, :, :]
                                dve.wait_ge(R.st_full, 16 * h + b + 10)
                                dve.scalar_tensor_tensor(st, st, G16, (PST, PRB)[b % 2][:, :].rearrange(
                                    "p (d e) -> p d e", d=2), ALU.mult, ALU.add).then_inc(R.st_ev, 1)
                ch.reset()

            def prep_q(h, c, part):
                s = slice(c * CH, (c + 1) * CH)
                if part == 0:
                    ch(dve.tensor_copy(PP[:, s], FG[:, s]))
                for l in (range(0, 3), range(3, LEV))[part]:
                    w = 1 << l
                    n = CH if l < LEVS or c < NC - 1 else CH - P
                    v = lambda x: x[:, c * CH:c * CH + n].rearrange("p (g a w) -> p g a w", a=2, w=w)
                    q = QE[c % 2][:, l, 0:n // 2].rearrange("p (g w) -> p g w", w=w)
                    pp = v(PP)
                    dve.tensor_tensor(q, v(HZ[0])[:, :, 1, :], pp[:, :, 1, :], ALU.mult)
                    ch(dve.tensor_tensor(pp[:, :, 1, :], pp[:, :, 1, :],
                                         pp[:, :, 0, w - 1:w].to_broadcast([P, n // (2 * w), w]), ALU.mult))
                if part == 1:
                    ch(dve.tensor_tensor(QP[:, s], HZ[0][:, s], PP[:, s], ALU.mult))
                    dve.sem_inc(H.q_ok, 1)

            def weights(h, t):
                dve.wait_ge(H.sc, 9 * h + t + 1)
                dve.wait_ge(H.st_full, 16 * h + (t if t >= 2 else 1))
                dve.wait_ge(H.kv, 9 * h + t + 2)
                at = ATT[t % 2]
                ch(dve.tensor_tensor(at[:, :], PSC[:, 0:P], ident[:, :], ALU.mult))
                for l in range(LEV if t < NT - 1 else LEVS):
                    w = 1 << l
                    src = PSC[:, P + 64 * l:P + 64 * (l + 1)] if l < 6 else PT[:, 2 * P:2 * P + 64]
                    g = lambda x: x.rearrange("p (g w) -> p g w", w=w)
                    last = dve.copy_predicated(at[:, :].rearrange("p (g a w) -> p g a w", a=2, w=w)[:, :, 1, :],
                                               g(MK[:, l, :]), g(src))
                    if l < (LEV if t < NT - 1 else LEVS) - 1:
                        ch(last)
                last.then_inc(H.att, 1)

            def forget(h):
                dve.wait_ge(H.f_ok, h + 1)
                ch(dve.tensor_scalar(FG[:, :], FG[:, :], LBC[:, 1, bass.ds(h, 1)], LBC[:, 0, bass.ds(h, 1)],
                                     ALU.mult, ALU.add))
                ch(dve.tensor_scalar(KK[:, :], FG[:, :], -1.0, 1.0, ALU.mult, ALU.add))
                dve.sem_inc(H.fk, 1)
                dve.wait_ge(H.in_[0], 16 * h + 16)

            def piece(i):
                dve.wait_ge(sp_hi, i + 1)
                c, k = divmod(i % (3 * KT), KT)
                cs = slice(c * CH, (c + 1) * CH)
                dve.tensor_tensor(XL[:, k, cs], URAW[i % NU][:, :], plain(XH[:, k, cs]), ALU.subtract).then_inc(sp_lo, 1)

            def hg_pair(i, final):
                for u in range(2):
                    h = 2 * i + u
                    end = final and u == 1
                    for s in range(HG_SLOTS):
                        j, c = divmod(s, NC)
                        jj = HG_BLOCKS * u + j
                        n = 40 + 10 * i + jj
                        if c == 0:
                            wlo_block(n + 1, (jj + 1) % 2)
                        for x in range(NC):
                            if s == H_NORM[x]:
                                norm_sum(H, h, x, HD)
                            if s == H_NORM[x] + 1:
                                gated(H, h, x, 1, OH[:, x * CH:(x + 1) * CH].unsqueeze(1))
                        if s in (0, 1, 6, 7):
                            if s == 6:
                                dve.wait_ge(H.sc, 9 * h + 3)
                            prep_q(h, 1 + s // 6, s % 6)
                        if s >= HA and s - HA < NT:
                            weights(h, s - HA)
                        if s > HA and s - HA - 1 < NT:
                            t = s - HA - 1
                            if t < NT - 1:
                                dve.wait_ge(H.st_full, 16 * h + t + 2)
                                if t == 0:
                                    dve.wait_ge(H.sr_st, 16 * h + 16)
                                    dve.tensor_copy(SH[:, :], PST[:, 0:P]).then_inc(H.st_ev, 1)
                                else:
                                    dve.wait_ge(H.st_ev, 16 * h + t + 1)
                                    e = (t + 1) * P - 1
                                    dve.scalar_tensor_tensor(SH[:, :], SH[:, :], PP[:, e:e + 1], PST[:, 0:P],
                                                             ALU.mult, ALU.add).then_inc(H.st_ev, 1)
                            else:
                                dve.wait_ge(H.s8_in[0], 16 * h + 16)
                                for b in range(NS):
                                    e = TP + (b + 1) * TS - 1
                                    dve.wait_ge(H.st_full, 16 * h + b + 10)
                                    dve.scalar_tensor_tensor(SH8[:, b, :], SH8[:, b, :], PP[:, e:e + 1],
                                                             (PST, PRB)[b % 2][:, 0:P], ALU.mult, ALU.add).then_inc(H.st_ev, 1)
                        if s >= HG_SLOTS - 2 and not end:
                            if s == HG_SLOTS - 2:
                                forget(h + 1)
                            prep_q(h + 1, 0, s - HG_SLOTS + 2)
                        if end and j == HG_BLOCKS - 1:
                            for x in range(KT):
                                piece(KT * c + x)
                    ch.reset()

            ret_done(dve)
            forget(0)
            prep_q(0, 0, 0)
            prep_q(0, 0, 1)
            ch.reset()
            with dve.Fori(0, HH // 2 - 1) as i:
                hg_pair(i, False)
            hg_pair(HH // 2 - 1, True)

            hg_done(dve)
            for k in range(2 * KT):
                n = NRB + k
                dve.wait_ge(mg_ok, k + 1)
                if KT <= k < KT + LATE:
                    w = w_row(k - KT)
                    wlo(w, WRAW[w % 2][:, :], WOH[:, k - KT, :], WOL[:, k - KT, :])
                if n + 1 < NB1:
                    w = w_item(n + 1)
                    p = (n + 1) % 2
                    wlo(w, as_block(WRAW[w % 2]), WHI[p][:, :, :], WLO[p][:, :, :])
                for c in range(NC):
                    s = slice(c * CH, (c + 1) * CH)
                    dve.wait_ge(mm, NC * n + c + 1)
                    if k < KT:
                        dve.tensor_tensor(MIX[:, k, s], psum[c][:, 0:CH], MG[k % 2][:, s], ALU.mult).then_inc(ev, 1)
                    else:
                        ch(dve.tensor_tensor(MG[k % 2][:, s], psum[c][:, 0:CH], MG[k % 2][:, s], ALU.mult))
                        dve.tensor_tensor(MIX[:, k - KT, s], MIX[:, k - KT, s], MG[k % 2][:, s], ALU.add).then_inc(ev, 1)
                    if k == KT - 1:
                        for x in range(KT):
                            piece(3 * KT + KT * c + x)
            for k in range(LATE, KT):
                w = w_row(k)
                wlo(w, WRAW[w % 2][:, :], WOH[:, k, :], WOL[:, k, :])
            for c in range(NC):
                for k in range(KT):
                    s = slice(c * CH, (c + 1) * CH)
                    dve.wait_ge(sp_hi, 6 * KT + KT * c + k + 1)
                    dve.tensor_tensor(XL[:, k, s], MIX[:, k, s], plain(XH[:, k, s]), ALU.subtract).then_inc(sp_lo, 1)
            dve.wait_ge(gb_in, 16)
            DB = ((0, 1), (2, 7))
            for t in range(NT + 2):
                if t < NT:
                    dve.wait_ge(d_ss, t + 1)
                    ch(dve.tensor_tensor(dss[:, 2 * t:2 * t + 1], dss[:, 2 * t:2 * t + 1], dss[:, 2 * t + 1:2 * t + 2], ALU.add))
                    dve.tensor_scalar(dms[:, t:t + 1], dss[:, 2 * t:2 * t + 1], 1.0 / D, EPS, ALU.mult, ALU.add).then_inc(d_ms, 1)
                    dve.wait_ge(d_rs, t + 1)
                    if t >= 2:
                        dve.wait_ge(x1_st[t % 2], 16 * (t // 2))
                    dve.wait_ge(xi_in[t % 2], 16 * (t // 2 + 1))
                    for q in range(2):
                        ns = slice(512 * q, 512 * (q + 1))
                        ch(dve.scalar_tensor_tensor(X1R[t % 2][:, ns], psum[DB[t % 2][q]][:, :], drs[:, t:t + 1],
                                                    GB[:, ns], ALU.mult, ALU.mult))
                    dve.tensor_tensor(X1R[t % 2][:, :], X1R[t % 2][:, :], XI2[t % 2][:, :], ALU.add).then_inc(d_x1, 1)
                if 1 <= t <= NT:
                    tt = NT + t - 1
                    norm_ms(tt)
                    norm_row(tt, X1R[(t - 1) % 2], HR2[tt % 2])
                if t == 3:
                    wlo_block(W_FFN, 0)
                if t >= 2:
                    norm_cols(NT + t - 2, TM2, 1, t - 2)
            ch.reset()
            NG = FF // 512
            dve.wait_ge(acc0, 1)
            dve.sem_inc(dn_ev, 1)

            def finish(t):
                dve.wait_ge(y_ss, t + 1)
                dve.tensor_scalar(yms[:, t:t + 1], yss[:, t:t + 1], 1.0 / D, EPS, ALU.mult, ALU.add).then_inc(y_ms, 1)
                dve.wait_ge(y_rs, t + 1)
                if t >= 2:
                    dve.wait_ge(y_st[t % 2], 16 * (t // 2))
                dve.wait_ge(x1_in[t % 2], 16 * (t // 2 + 1))
                dve.wait_ge(gb_in, 32)
                ch(dve.scalar_tensor_tensor(OF[t % 2][:, :], ACC[:, t, :], yrs[:, t:t + 1], GF[:, :], ALU.mult, ALU.mult))
                dve.tensor_tensor(OF[t % 2][:, :], OF[t % 2][:, :], X1F[t % 2][:, :], ALU.add).then_inc(y_ok, 1)

            def mlp(g, last):
                w0 = W_FFN + 1 + 8 * g

                def split(i):
                    q = (W_FFN + 1 + i) % 2
                    if i % 2 == 0:
                        wlo(w0 + i, WRAW[q][:, :], WDH[:, i // 2, :], WDL[:, i // 2, :])
                    else:
                        b = (i // 2 + 1) % 4
                        wlo(w0 + i, as_block(WRAW[q]), WHI[b % 2][:, :, :], WLO[b % 2][:, :, :])
                for b in range(4):
                    for c in range(NC):
                        if c == 0:
                            split(2 * b)
                        if c == 1 and b < 3:
                            split(2 * b + 1)
                        x = NC * b + c
                        dve.wait_ge(f_t1, 12 * g + x + 1)
                        if x >= 2:
                            dve.wait_ge(f_ul, 12 * g + x - 1)
                        dve.tensor_tensor(T2[x % 2][:, :], T1[x % 2][:, :], T1[x % 2][:, :], ALU.mult).then_inc(f_t2, 1)
                        dve.wait_ge(f_uh, 12 * g + x + 1)
                        us_ = slice(c * CH, (c + 1) * CH)
                        dve.tensor_tensor(UL[:, b, us_], T2[x % 2][:, :], plain(UH[:, b, us_]), ALU.subtract).then_inc(f_ul, 1)
                if not last:
                    split(7)
                for x in range(2 * NT):
                    t, q = divmod(x, 2)
                    ns = slice(512 * q, 512 * (q + 1))
                    dve.wait_ge(dn, 18 * g + x + 2)
                    dve.tensor_tensor(ACC[:, t, ns], ACC[:, t, ns], psum[3 + x % 5][:, :], ALU.add).then_inc(dn_ev, 1)
                    if last and q and t:
                        finish(t - 1)
            with dve.Fori(0, NG - 1) as g:
                mlp(g, False)
            mlp(NG - 1, True)
            finish(NT - 1)

        @block.gpsimd
        def _(pool):
            ch = Chain(pool, pool_ch)
            ch(pool.memset(mhalf[:, :], -0.5))

            def rsqrt(dst, src, n=1):
                e = mhalf[:, :] if n == 1 else mhalf[:, :].to_broadcast([P, n])
                return pool.tensor_tensor(dst, src, e, ALU.pow)

            for tt in range(NT):
                pool.wait_ge(n_ms, tt + 1)
                rsqrt(rsc[:, tt:tt + 1], msc[:, tt:tt + 1]).then_inc(n_rs, 1)
            ch.reset()

            def gate(K, h, c, ne, g):
                pool.wait_ge(K.sg, 3 * h + c + 1)
                pool.tensor_tensor(SG[:, 0:ne, :], SG[:, 0:ne, :], g, ALU.mult).then_inc(K.gt, 1)
                pool.wait_ge(K.ms, 3 * h + c + 2)
                if c:
                    pool.wait_ge(K.dg, 3 * h + c)
                rsqrt(RST[:, :], MS[:, :], TPC).then_inc(K.rs, 1)

            pool.wait_ge(c_in2, 48)
            with pool.Fori(0, RH) as h:
                pool.wait_ge(R.in_[1], 16 * h + 16)
                pool.wait_ge(R.att, 9 * h + 1)
                for c in range(NC):
                    s = slice(c * CH, (c + 1) * CH)
                    cs, sn = CS[:, 0, s], CS[:, 1, s]
                    pool.tensor_tensor(PTMP[:, 0, :], ZK[:, 0, s], sn, ALU.mult)
                    ch(pool.tensor_tensor(PTMP[:, 1, :], ZK[:, 1, s], cs, ALU.mult))
                    last = pool.tensor_tensor(KR[:, 1, s], PTMP[:, 0, :], PTMP[:, 1, :], ALU.add)
                    if c < NC - 1:
                        ch(last)
                last.then_inc(R.k_ok, 1)
                for c in range(NC):
                    gate(R, h, c, 2, ZG[c % 2][:, :, :])
                ch.reset()

            ret_done(pool)
            for i in range(2):
                ch(pool.memset(KE[i][:, :, :], 0.0))
            ch.reset()

            def prep_k(h, c):
                s = slice(c * CH, (c + 1) * CH)
                off, tot = 0, FG[:, s]
                pool.tensor_tensor(FT[:, 0:CH // 2], FG[:, c * CH:(c + 1) * CH:2], FG[:, c * CH + 1:(c + 1) * CH:2], ALU.mult)
                ch(pool.memset(RR[:, s], 1.0))
                for l in range(LEV):
                    w = 1 << l
                    n = CH if l < LEVS or c < NC - 1 else CH - P
                    v = lambda x: x[:, 0:n].rearrange("p (g a w) -> p g a w", a=2, w=w)
                    pairs = tot[:, 0:n // w].rearrange("p (g a) -> p g a", a=2)
                    rr = v(RR[:, s])
                    pool.tensor_tensor(v(KE[c % 2][:, l, :])[:, :, 0, :], v(KK[:, s])[:, :, 0, :], rr[:, :, 0, :], ALU.mult)
                    if l < LEV - 1:
                        nxt = FT[:, off:off + n // (2 * w)]
                        if l:
                            pool.tensor_tensor(nxt, pairs[:, :, 0], pairs[:, :, 1], ALU.mult)
                        off += n // (2 * w)
                    ch(pool.tensor_tensor(rr[:, :, 0, :], rr[:, :, 0, :],
                                          pairs[:, :, 1:2].to_broadcast([P, n // (2 * w), w]), ALU.mult))
                    tot = nxt
                ch(pool.tensor_tensor(KRH[:, s], KK[:, s], RR[:, s], ALU.mult))
                pool.sem_inc(H.k_ok, 1)

            def hg_head(h, last):
                prep_k(h, 1)
                pool.wait_ge(H.att, 9 * h + 4)
                prep_k(h, 2)
                for c in range(NC):
                    gate(H, h, c, 1, HZ[3][:, c * CH:(c + 1) * CH].unsqueeze(1))
                if not last:
                    pool.wait_ge(H.fk, h + 2)
                    pool.wait_ge(H.att, 9 * h + 10)
                    prep_k(h + 1, 0)
                ch.reset()

            pool.wait_ge(H.fk, 1)
            prep_k(0, 0)
            ch.reset()
            with pool.Fori(0, HH - 1) as h:
                hg_head(h, False)
            hg_head(HH - 1, True)

            for t in range(NT + 1):
                if t < NT:
                    pool.wait_ge(d_ms, t + 1)
                    rsqrt(drs[:, t:t + 1], dms[:, t:t + 1]).then_inc(d_rs, 1)
                if t >= 1:
                    tt = NT + t - 1
                    pool.wait_ge(n_ms, tt + 1)
                    rsqrt(rsc[:, tt:tt + 1], msc[:, tt:tt + 1]).then_inc(n_rs, 1)
            pool.wait_ge(n_xl, 4 * NT)
            pool.wait_ge(n_xh, 4 * NT)
            for i in range(2):
                pool.wait_ge(x1_st[i], 16 * ((NT + 1 - i) // 2))
            pool.memset(ACC[:, :, :], 0.0).then_inc(acc0, 1)
            for t in range(NT):
                pool.wait_ge(y_ms, t + 1)
                rsqrt(yrs[:, t:t + 1], yms[:, t:t + 1]).then_inc(y_rs, 1)


_INS = ["x_prompt", "x_sample", "state_ret", "state_hgrn", "w_in", "w_a", "w_b", "w_out", "w_up", "w_down",
        "g_post_mix", "g_post_ffn"]
_OUTS = [("y_p", (1, TP, D)), ("y_s", (NS, TS, D)), ("ret_p", (1, 1, RH, RD, RD)), ("hg_p", (1, 1, HH, HD, HD)),
         ("ret_s", (1, NS, RH, RD, RD)), ("hg_s", (1, NS, HH, HD, HD))]


def shape_tables(np):
    f = np.float32
    inv = (f(10000.0) ** (-np.arange(0, RD, 2, dtype=f) / f(RD))).astype(f)
    pos = np.concatenate([np.arange(TP), PAST + np.arange(NS * TS) % TS]).astype(f)
    ang = (inv[:, None] * pos[None, :]).astype(f)
    rope = np.stack([np.cos(ang), np.sin(ang)], axis=1).astype(f)
    gam = np.log(1.0 - np.exp(np.linspace(np.log(1.0 / 32), np.log(1.0 / 512), RH))).astype(f).astype(np.float64)
    i = np.arange(P)
    ret = np.zeros((RH, P, 4 * P + 12), f)
    for h in range(RH):
        lg = gam[h]
        ret[h, :, 0:P] = np.exp((i + 1) * lg)[None]
        ret[h, :, P:2 * P] = np.exp((i % TS + 1) * lg)[None]
        m, n = i[:, None], i[None, :]
        ret[h, :, 2 * P:3 * P] = np.where(m // 64 <= n // 64, np.exp(np.abs(n - m) * lg), 0) * RD ** -0.5
        ret[h, :, 3 * P:4 * P] = np.where(m // TS == n // TS, np.exp(np.abs(n - m) * lg), 0) * RD ** -0.5
        ret[h, :, 4 * P] = np.exp((P - 1 - i) * lg) * RD ** -0.5
        ret[h, :, 4 * P + 1] = np.exp(P * lg)
        ret[h, :, 4 * P + 2] = np.exp(TS * lg)
        for b in range(NS):
            ret[h, :, 4 * P + 3 + b] = np.where(i // TS == b, np.exp((TS - 1 - i % TS) * lg), 0) * RD ** -0.5
    mask = np.zeros((P, LEV, 64), np.uint32)
    for l in range(LEV):
        w = 1 << l
        t = np.arange(64) // w * 2 * w + w + np.arange(64) % w
        mask[:, l] = (i[:, None] // w == t[None, :] // w - 1)
    rows = (i[:, None] // TS == np.arange(NS)[None]).astype(f)
    return {"c_rope": rope, "c_ret": ret, "c_mask": mask, "c_rows": rows, "c_ident": np.eye(P, dtype=f)}


def kernel(**inputs):
    import numpy as _np
    import concourse.bacc as _bacc
    from concourse import mybir as _mybir
    from concourse.bass_utils import run_bass_kernel_spmd as _run

    nc = _bacc.Bacc("TRN2", target_bir_lowering=False, num_devices=1)
    data = {n: _np.ascontiguousarray(inputs[n]) for n in _INS}
    data["g_pre_cols"] = _np.ascontiguousarray(
        _np.stack([inputs["g_pre_mix"], inputs["g_pre_ffn"]]).reshape(2, KT, P).transpose(2, 0, 1))
    data["lb_cols"] = _np.ascontiguousarray(_np.asarray(inputs["lb_logits"]).reshape(2, HH, P).transpose(2, 0, 1))
    data.update(shape_tables(_np))
    arrays, a, o = {}, {}, {}
    for name, x in data.items():
        arrays[f"in_{name}"] = x
        a[name] = nc.dram_tensor(f"in_{name}", x.shape, _mybir.dt.from_np(x.dtype), kind="ExternalInput").ap()
    for name, shape in _OUTS:
        o[name] = nc.dram_tensor(f"out_{name}", shape, _mybir.dt.float32, kind="ExternalOutput").ap()
    scr = {n: nc.dram_tensor(f"scratch_{n}", s, _mybir.dt.float32, kind="Internal").ap()
           for n, s in (("z", (80, P, T)), ("u", (16, P, T)), ("x1", (T, D)))}
    program(nc, a, o, scr)
    r = _run(nc, [arrays], core_ids=[0])
    return tuple(r.results[0][f"out_{name}"] for name, _ in _OUTS)
```

```python
import concourse.bass as bass
from concourse import mybir
from contextlib import ExitStack

F32 = mybir.dt.float32
F32R = mybir.dt.float32r
U32 = mybir.dt.uint32
ALU = mybir.AluOpType
ACT = mybir.ActivationFunctionType

P = 128
D = 1024
KT = D // P
TP = 1024
NS, TS = 8, 16
T = TP + NS * TS
NT = T // P
NTP = TP // P
CH = T // 3
NC = 3
TPC = NT // NC
RH, RD = 4, 256
HH, HD = 8, 128
FF = 4 * D
LEV = 7
LEVS = 4
PAST = 512
EPS = 1e-6

RET_SLOTS = 8 * NC
HG_BLOCKS = 5
HG_SLOTS = HG_BLOCKS * NC
RA = 8
HA = 3
R_NORM = (12, 15, 18)
H_NORM = (8, 11, 13)


class Chain:

    def __init__(self, eng, sem):
        self.eng, self.sem, self.n = eng, sem, 0

    def __call__(self, ins):
        self.n += 1
        ins.then_inc(self.sem, 1)
        self.eng.wait_ge(self.sem, self.n)

    def reset(self):
        self.eng.sem_clear(self.sem)
        self.n = 0


def program(nc, a, o, scr):
    ctx = ExitStack()
    with ctx:
        def sem(name):
            return ctx.enter_context(nc.semaphore(name))

        def sb(name, shape, dt=F32, stack=ctx):
            return stack.enter_context(nc.sbuf_tensor(name, shape, dt))

        pf = ExitStack()
        GF, SQJ3 = sb("GF", [P, D], F32, pf), sb("SQJ3", [P, D], F32, pf)
        X1F = [sb(f"X1F{i}", [P, D], F32, pf) for i in range(2)]
        OF = [sb(f"OF{i}", [P, D], F32, pf) for i in range(2)]
        pf.close()

        XH, XL = sb("XH", [P, KT, T], F32R), sb("XL", [P, KT, T], F32R)
        WRAW = [sb(f"WRAW{i}", [P, 1024]) for i in range(2)]
        WHI = [sb(f"WHI{i}", [P, KT, P], F32R) for i in range(2)]
        WLO = [sb(f"WLO{i}", [P, KT, P], F32R) for i in range(2)]
        ident = sb("ident", [P, P])
        gcol = sb("gcol", [P, 2, KT])
        mhalf = sb("mhalf", [P, 1])
        LB = sb("LB", [P, 2, HH])
        LBM = sb("LBM", [P, HH])
        LBC = sb("LBC", [P, 2, HH])
        ssc = sb("ssc", [P, 2 * NT])
        msc = sb("msc", [P, 2 * NT])
        rsc = sb("rsc", [P, 2 * NT])
        dss, dms, drs = sb("dss", [P, 2 * NT]), sb("dms", [P, NT]), sb("drs", [P, NT])
        yss, yms, yrs = (sb(n, [P, NT]) for n in ("yss", "yms", "yrs"))
        psum = [ctx.enter_context(nc.psum_tensor(f"bank{i}", [P, 512], F32)) for i in range(8)]
        PT, PSC, PRB, PO, PST = psum[3], psum[4], psum[5], psum[6], psum[7]

        p0 = ExitStack()
        XR = [sb(f"XR{i}", [P, D], F32, p0) for i in range(NT)]
        HR = [sb(f"HR{i}", [P, D], F32, p0) for i in range(2)]
        TM = [sb(f"TM{i}", [P, 4, P], F32, p0) for i in range(2)]
        SQJ = sb("SQJ", [P, D], F32, p0)
        p0.close()

        pa = ExitStack()
        ZST = [sb(f"ZST{i}", [P, T], F32, pa) for i in range(2)]
        KVT = [sb(f"KVT{i}", [P, 2, 256], F32, pa) for i in range(2)]
        ATT = [sb(f"ATT{i}", [P, P], F32, pa) for i in range(2)]
        SQ = sb("SQ", [P, 2, CH], F32, pa)
        SG = sb("SG", [P, 2, CH], F32, pa)
        MS = sb("MS", [P, TPC], F32, pa)
        RST = sb("RST", [P, TPC], F32, pa)
        DG = sb("DG", [P, TPC, P], F32, pa)
        UB = sb("UB", [P, 2, CH], F32, pa)
        ones = sb("ones", [P, P], F32, pa)
        MK = sb("MK", [P, LEV, 64], U32, pa)
        RM = sb("RM", [P, NS], F32, pa)

        pr = ExitStack()
        ZV = sb("ZV", [P, 2, T], F32, pr)
        QR = sb("QR", [P, 2, T], F32, pr)
        KR = sb("KR", [P, 2, T], F32, pr)
        CS = sb("CS", [P, 2, T], F32, pr)
        RTMP = sb("RTMP", [P, 2, CH], F32, pr)
        PTMP = sb("PTMP", [P, 2, CH], F32, pr)
        ZQ = sb("ZQ", [P, 2, T], F32, pr)
        ZK = sb("ZK", [P, 2, T], F32, pr)
        ZG = [sb(f"ZG{i}", [P, 2, CH], F32, pr) for i in range(2)]
        QX = ZQ
        HC = sb("HC", [P, 4 * P + 12], F32, pr)
        XI = HC[:, 0:2 * P].rearrange("p (a n) -> p a n", a=2)
        DM = HC[:, 2 * P:4 * P].rearrange("p (a n) -> p a n", a=2)
        ZETA, G128, G16 = (HC[:, 4 * P + i:4 * P + i + 1] for i in range(3))
        SR = sb("SR", [P, 2, RD], F32, pr)
        S8B = sb("S8B", [P, 4, 2, RD], F32, pr)
        S8A = ZK[:, :, :].rearrange("p a t -> p (a t)")[:, 0:4 * 2 * RD].rearrange("p (b d e) -> p b d e", b=4, d=2)
        KZ8 = [sb(f"KZ8{i}", [P, RD], F32, pr) for i in range(2)]
        pr.close()

        ph = ExitStack()
        HZ = [sb(f"HZ{i}", [P, T], F32, ph) for i in range(4)]
        FG = HZ[1]
        KE = [sb(f"KE{i}", [P, LEV, CH], F32, ph) for i in range(2)]
        FT = sb("FT", [P, CH], F32, ph)
        KK, PP, RR = (sb(n, [P, T], F32, ph) for n in ("KK", "PP", "RR"))
        QP, KRH = (sb(n, [P, T], F32, ph) for n in ("QP", "KRH"))
        OH = QP
        QE = [sb(f"QE{i}", [P, LEV, CH // 2], F32, ph) for i in range(2)]
        SH = sb("SH", [P, HD], F32, ph)
        SH8 = sb("SH8", [P, NS, HD], F32, ph)
        KM8 = [(SQ, SG, UB)[b // 3][:, 1, (b % 3) * HD:(b % 3 + 1) * HD] for b in range(NS)]
        URAW = sb("URAW", [P, CH], F32, ph)
        UA = [[HZ[k // NC][:, k % NC * CH:(k % NC + 1) * CH] for k in range(KT - 1)] + [URAW[:, :]]] + \
            [[KE[i][:, k, :] for k in range(LEV)] + [HZ[2][:, (i + 1) * CH:(i + 2) * CH]] for i in range(2)]
        ph.close()
        pa.close()

        pb = ExitStack()
        MIX = sb("MIX", [P, KT, T], F32, pb)
        pb1 = ExitStack()
        UR1 = sb("UR1", [P, KT, T], F32, pb1)
        pb1.close()
        sb("hold_wo", [P, 2 * KT * D], F32, pb)
        MG = [sb(f"MG{i}", [P, T], F32, pb) for i in range(2)]
        pb.close()

        pd = ExitStack()
        sb("hold_mix", [P, KT, T], F32, pd)
        WOH, WOL = sb("WOH", [P, KT, D], F32R, pd), sb("WOL", [P, KT, D], F32R, pd)
        pd.close()
        pd2 = ExitStack()
        XI2 = [sb(f"XI2{i}", [P, D], F32, pd2) for i in range(2)]
        X1R = [sb(f"X1R{i}", [P, D], F32, pd2) for i in range(2)]
        HR2 = [sb(f"HR2{i}", [P, D], F32, pd2) for i in range(2)]
        TM2 = [sb(f"TM2{i}", [P, 4, P], F32, pd2) for i in range(2)]
        SQJ2 = sb("SQJ2", [P, D], F32, pd2)
        GB = sb("GB", [P, D], F32, pd2)
        pd2.close()
        pe_ = ExitStack()
        UH, UL = sb("UH", [P, 4, T], F32R, pe_), sb("UL", [P, 4, T], F32R, pe_)
        ACC = sb("ACC", [P, NT, D], F32, pe_)
        WDH, WDL = sb("WDH", [P, 4, D], F32R, pe_), sb("WDL", [P, 4, D], F32R, pe_)
        T1 = [sb(f"T1{i}", [P, CH], F32, pe_) for i in range(2)]
        T2 = [sb(f"T2{i}", [P, CH], F32, pe_) for i in range(2)]
        pe_.close()
        w_raw = [sem("w_raw0"), sem("w_raw1")]
        w_hi, w_lo = sem("w_hi"), sem("w_lo")
        mm = sem("mm")
        ev = sem("ev")
        z_st = [sem("z_st0"), sem("z_st1")]
        c_in = sem("c_in")
        c_in2 = sem("c_in2")
        lb_ch, lb_e = sem("lb_ch"), sem("lb_e")
        act_ch, dve_ch, pool_ch = sem("act_ch"), sem("dve_ch"), sem("pool_ch")
        x_in = [sem(f"x_in{i}") for i in range(NT)]
        n_ss, n_ms, n_rs, n_hr = sem("n_ss"), sem("n_ms"), sem("n_rs"), sem("n_hr")
        n_tp, n_tm, n_xh, n_xl = sem("n_tp"), sem("n_tm"), sem("n_xh"), sem("n_xl")

        class Heads:

            def __init__(self, k):
                self.in_ = [sem(f"{k}_in{i}") for i in range(4)]
                self.g_in = [sem(f"{k}_g_in0"), sem(f"{k}_g_in1")]
                self.s8_in = [sem(f"{k}_s8_in0"), sem(f"{k}_s8_in1")]
                self.q_ok, self.k_ok = sem(f"{k}_q_ok"), sem(f"{k}_k_ok")
                self.f_ok, self.fk = sem(f"{k}_f_ok"), sem(f"{k}_fk")
                self.t_full, self.kv = sem(f"{k}_t_full"), sem(f"{k}_kv")
                self.sc, self.att = sem(f"{k}_sc"), sem(f"{k}_att")
                self.o_full, self.o_ev = sem(f"{k}_o_full"), sem(f"{k}_o_ev")
                self.st_full, self.st_ev = sem(f"{k}_st_full"), sem(f"{k}_st_ev")
                self.kz8 = sem(f"{k}_kz8")
                self.sq, self.rb, self.ms = sem(f"{k}_sq"), sem(f"{k}_rb"), sem(f"{k}_ms")
                self.sg, self.w_ok, self.u_ok = sem(f"{k}_sg"), sem(f"{k}_w_ok"), sem(f"{k}_u_ok")
                self.rs, self.dg, self.rbb, self.gt = (sem(f"{k}_{x}") for x in ("rs", "dg", "rbb", "gt"))
                self.u_st, self.sr_st = sem(f"{k}_u_st"), sem(f"{k}_sr_st")
                self.s8_st = [sem(f"{k}_s8_st0"), sem(f"{k}_s8_st1")]

        R, H = Heads("r"), Heads("h")
        ua_in = [sem(f"ua_in{c}") for c in range(NC)]
        ur1_in = [sem(f"ur1_in{k}") for k in range(KT)]
        mg_in = [sem("mg_in0"), sem("mg_in1")]
        sp_hi, sp_lo = sem("sp_hi"), sem("sp_lo")
        mg_ok = sem("mg_ok")
        gb_in, xi_in = sem("gb_in"), [sem("xi_in0"), sem("xi_in1")]
        d_mm, d_ss, d_ms, d_rs, d_x1 = sem("d_mm"), sem("d_ss"), sem("d_ms"), sem("d_rs"), sem("d_x1")
        x1_st = [sem("x1_st0"), sem("x1_st1")]
        f_t1, f_t2, f_uh, f_ul = sem("f_t1"), sem("f_t2"), sem("f_uh"), sem("f_ul")
        dn, dn_ev = sem("dn"), sem("dn_ev")
        acc0 = sem("acc0")
        x1_in = [sem("x1_in0"), sem("x1_in1")]
        y_ss, y_ms, y_rs, y_ok = sem("y_ss"), sem("y_ms"), sem("y_rs"), sem("y_ok")
        y_st = [sem("y_st0"), sem("y_st1")]

        zs, us, x1s = scr["z"], scr["u"], scr["x1"]
        NRB = 10 * KT
        NB1 = NRB + 2 * KT
        W_OUT = NB1
        W_FFN = W_OUT + KT

        def z_block(n):
            if n < 32:
                h, j = divmod(n, 8)
                return (j // 2) * D + h * RD + (j % 2) * P, n
            if n < 40:
                h, j = divmod(n - 32, 4)
                return (4 + j) * D + h * HD, n
            i, j = divmod(n - 40, HG_BLOCKS)
            if i < 6 and j < 4:
                return (4 + j) * D + (i + 2) * HD, 40 + 4 * i + j
            mi = i if i < 6 else 6 + (n - 70)
            return 8 * D + mi * P, 64 + mi

        def w_item(n):
            return n if n < NRB + KT else 2 * n - NRB - KT

        def w_row(k):
            return w_item(NRB + KT + k) + 1

        def w_src(w):
            if w < NRB:
                c = z_block(w)[0]
                return a["w_in"][0, :, c:c + P].rearrange("(k p) n -> p k n", p=P)
            if w < NRB + KT:
                c = (w - NRB) * P
                return a["w_a"][0, :, c:c + P].rearrange("(k p) n -> p k n", p=P)
            for k in range(KT):
                if w == w_row(k):
                    return a["w_out"][0, k * P:(k + 1) * P, :].rearrange("p (k n) -> p k n", n=P)
                if w == w_item(NRB + KT + k):
                    return a["w_b"][0, :, k * P:(k + 1) * P].rearrange("(k p) n -> p k n", p=P)

        def as_block(t):
            return t[:, :].rearrange("p (k n) -> p k n", k=KT)

        def row_bank(t, q):
            return psum[((7, 3) if t == 0 else (0, 1) if t % 2 else (2, 7))[q]]

        def plain(x):
            return x.bitcast(F32)

        def y_store(sp, t):
            sp.wait_ge(y_ok, t + 1)
            dst = o["y_p"][0, t * P:(t + 1) * P, :] if t < NTP else o["y_s"].rearrange("b t d -> (b t) d")
            sp.dma_start(dst, OF[t % 2][:, :]).then_inc(y_st[t % 2], 16)

        def ret_mixed(e):
            e.wait_ge(R.att, 9 * RH + 1)

        def ret_done(e):
            e.wait_ge(R.u_st, 16 * 3 * RH + 16)
            e.wait_ge(R.sr_st, 16 * RH + 16)
            for s in R.s8_st:
                e.wait_ge(s, 32 * RH + 16)

        def hg_done(e):
            e.wait_ge(H.u_st, 16 * 3 * HH + 16)
            e.wait_ge(H.sr_st, 16 * HH + 16)
            e.wait_ge(H.s8_st[0], 16 * HH + 16)
            for q in range(2):
                e.wait_ge(z_st[q], 16 * NRB // 2)

        block = ctx.enter_context(nc.Block())

        @block.sync
        def _(sp):
            def load_w(w):
                p = w % 2
                if w >= 2:
                    sp.wait_ge(w_lo, w - 1)
                sp.dma_start(as_block(WRAW[p]), w_src(w)).then_inc(w_raw[p], 16)

            def store_z(n):
                p = n % 2
                sp.wait_ge(ev, NC * n + NC)
                sp.dma_start(zs[z_block(n)[1]], ZST[p][:, :]).then_inc(z_st[p], 16)

            def z_stored(n):
                for q in (n, n - 1):
                    if q >= 0:
                        sp.wait_ge(z_st[q % 2], 16 * (q // 2 + 1))

            def rows(tt, dst, s):
                src = a["x_prompt"][0, tt * P:(tt + 1) * P, :] if tt < NTP else \
                    a["x_sample"].rearrange("b t d -> (b t) d")
                sp.dma_start(dst[:, :], src).then_inc(s, 16)

            def store_u(h, c):
                sp.wait_ge(H.u_ok, 3 * h + c + 2)
                sp.dma_start(us[KT + h, :, c * CH:(c + 1) * CH], UB[:, 0, :]).then_inc(H.u_st, 16)

            for tt in range(2):
                rows(tt, XR[tt], x_in[tt])
            sp.dma_start(ident[:, :], a["c_ident"]).then_inc(c_in, 16)
            sp.dma_start(gcol[:, :, :], a["g_pre_cols"]).then_inc(c_in, 16)
            sp.dma_start(LB[:, :, :], a["lb_cols"]).then_inc(c_in, 16)
            for tt in range(2, NT):
                rows(tt, XR[tt], x_in[tt])
                if tt in (3, 5):
                    load_w((tt - 3) // 2)
            sp.wait_ge(n_xl, 2 * NT)
            sp.wait_ge(n_xh, 2 * NT)
            sp.dma_start(CS[:, :, :], a["c_rope"]).then_inc(c_in2, 16)
            sp.dma_start(MK[:, :, :], a["c_mask"]).then_inc(c_in2, 16)
            sp.dma_start(RM[:, :], a["c_rows"]).then_inc(c_in2, 16)
            for s in (R.u_st, R.sr_st, *R.s8_st, H.u_st, H.sr_st, *H.s8_st):
                sp.sem_inc(s, 16)

            for n in range(8):
                load_w(n + 2)
                if n:
                    store_z(n - 1)

            for h in range(RH):
                for j in range(8):
                    n = 8 + 8 * h + j
                    load_w(n + 2)
                    store_z(n - 1)
                    if j == 0:
                        z_stored(n - 1)
                        if h:
                            sp.wait_ge(R.o_ev, 9 * h + 1)
                            sp.wait_ge(R.u_ok, 3 * h + 1)
                            sp.wait_ge(R.st_ev, 16 * h + 1)
                        z = zs[8 * h:8 * h + 8].rearrange("(g e) p t -> g p e t", e=2)
                        sp.dma_start(HC[:, :], a["c_ret"][h]).then_inc(R.in_[3], 16)
                        sp.dma_start(ZQ[:, :, :], z[0]).then_inc(R.in_[0], 16)
                        if h:
                            sp.wait_ge(R.s8_st[0], 32 * h + 16)
                        sp.dma_start(ZK[:, :, :], z[1]).then_inc(R.in_[1], 16)
                        sp.dma_start(ZV[:, :, :], z[2]).then_inc(R.in_[2], 16)
                        if h:
                            sp.wait_ge(R.s8_st[1], 32 * h + 16)
                        for d in range(2):
                            sp.dma_start(S8B[:, :, d, :], a["state_ret"][0, 4:8, h, d * P:(d + 1) * P, :]
                                         .rearrange("b p e -> p b e")).then_inc(R.s8_in[1], 16)
                        for c in range(2):
                            sp.dma_start(ZG[c][:, :, :], z[3][:, :, c * CH:(c + 1) * CH]).then_inc(R.g_in[c], 16)
                    if j == 2:
                        sp.wait_ge(R.k_ok, h + 1)
                        sp.wait_ge(R.q_ok, h + 1)
                        for d in range(2):
                            sp.dma_start(S8A[:, :, d, :], a["state_ret"][0, 0:4, h, d * P:(d + 1) * P, :]
                                         .rearrange("b p e -> p b e")).then_inc(R.s8_in[0], 16)
                    for c in range(NC):
                        if j == (4, 5, 7)[c]:
                            if c == 0:
                                sp.wait_ge(R.gt, 3 * h + 1)
                                sp.dma_start(ZG[0][:, :, :], z[3][:, :, 2 * CH:]).then_inc(R.g_in[0], 16)
                            sp.wait_ge(R.u_ok, 3 * h + c + 2)
                            sp.dma_start(us[2 * h:2 * h + 2, :, c * CH:(c + 1) * CH].rearrange("e p t -> p e t"),
                                         UB[:, :, :]).then_inc(R.u_st, 16)
                sp.wait_ge(R.st_ev, 16 * h + 9)
                sp.dma_start(o["ret_p"][0, 0, h].rearrange("(d p) e -> p d e", p=P), SR[:, :, :]).then_inc(R.sr_st, 16)
                sp.wait_ge(R.st_ev, 16 * h + 17)
                for g, t8 in enumerate((S8A, S8B[:, :, :, :])):
                    for d in range(2):
                        sp.dma_start(o["ret_s"][0, 4 * g:4 * g + 4, h, d * P:(d + 1) * P, :]
                                     .rearrange("b p e -> p b e"), t8[:, :, d, :]).then_inc(R.s8_st[g], 16)

            def load_q(h):
                for i in (1, 0, 2):
                    sp.dma_start(HZ[i][:, :], zs[32 + 4 * h + i]).then_inc(H.in_[i], 16)

            def load_ua():
                for i in range(2):
                    sp.dma_start(HZ[i][:, :].rearrange("p (k t) -> p k t", k=NC),
                                 us[NC * i:NC * i + NC, :, 0:CH].rearrange("k p t -> p k t")).then_inc(ua_in[0], 16)
                for k in (KT - 2, KT - 1):
                    sp.dma_start(UA[0][k], us[k, :, 0:CH]).then_inc(ua_in[0], 16)
                for c in (1, 2):
                    cs = slice(c * CH, (c + 1) * CH)
                    sp.dma_start(KE[c - 1][:, :, :], us[0:LEV, :, cs].rearrange("k p t -> p k t")).then_inc(ua_in[c], 16)
                    sp.dma_start(UA[c][LEV], us[LEV, :, cs]).then_inc(ua_in[c], 16)

            ret_mixed(sp)
            z_stored(38)
            load_q(0)
            for h in range(HH):
                for j in range(HG_BLOCKS):
                    n = 40 + HG_BLOCKS * h + j
                    load_w(n + 2)
                    store_z(n - 1)
                    if j == 0:
                        z_stored(n - 1)
                        if h:
                            sp.wait_ge(H.u_ok, 3 * h + 1)
                            sp.wait_ge(H.s8_st[0], 16 * h + 16)
                        sp.dma_start(HZ[3][:, :], zs[35 + 4 * h]).then_inc(H.in_[3], 16)
                        sp.dma_start(SH8[:, :, :], a["state_hgrn"][0, :, h].rearrange("b p e -> p b e"))\
                            .then_inc(H.s8_in[0], 16)
                    if j == HG_BLOCKS - 1:
                        sp.wait_ge(H.att, 9 * h + 10)
                        if h < HH - 1:
                            load_q(h + 1)
                        else:
                            load_ua()
                    for c in range(NC):
                        if j == (3, 4, 4)[c] and c < 2:
                            store_u(h, c)
                store_u(h, 2)
                sp.wait_ge(H.st_ev, 16 * h + 9)
                sp.dma_start(o["hg_p"][0, 0, h], SH[:, :]).then_inc(H.sr_st, 16)
                sp.wait_ge(H.st_ev, 16 * h + 17)
                sp.dma_start(o["hg_s"][0, :, h].rearrange("b p e -> p b e"), SH8[:, :, :]).then_inc(H.s8_st[0], 16)

            store_z(NRB - 1)
            hg_done(sp)
            for k in range(2 * KT):
                n = NRB + k
                if k >= 2:
                    sp.wait_ge(ev, NC * (n - 2) + NC)
                sp.dma_start(MG[k % 2][:, :], zs[64 + k]).then_inc(mg_in[k % 2], 16)
                for w in range(w_item(n + 1) + 1, w_item(min(n + 2, NB1 - 1)) + 1):
                    load_w(w)
                if k == 0:
                    sp.wait_ge(sp_lo, 3 * KT)
                if k < KT:
                    sp.dma_start(UR1[:, k, :], us[KT + k]).then_inc(ur1_in[k], 16)
            load_w(w_row(KT - 1))
            sp.wait_ge(w_lo, W_FFN - 1)
            sp.dma_start(as_block(WRAW[0]), a["w_up"][0, :, 0:P].rearrange("(k p) n -> p k n", p=P)).then_inc(w_raw[0], 16)
            sp.wait_ge(sp_lo, 9 * KT)
            sp.wait_ge(sp_hi, 9 * KT)
            sp.dma_start(GB[:, :], a["g_post_mix"].to_broadcast([P, D])).then_inc(gb_in, 16)
            for t in range(NT):
                if t >= 2:
                    sp.wait_ge(d_x1, t - 1)
                rows(t, XI2[t % 2], xi_in[t % 2])
                if t >= 1:
                    sp.wait_ge(d_x1, t)
                    sp.dma_start(x1s[(t - 1) * P:t * P, :], X1R[(t - 1) % 2][:, :]).then_inc(x1_st[(t - 1) % 2], 16)
            sp.wait_ge(d_x1, NT)
            sp.dma_start(x1s[(NT - 1) * P:, :], X1R[(NT - 1) % 2][:, :]).then_inc(x1_st[(NT - 1) % 2], 16)
            def mlp_w(g, last):
                for i in range(7):
                    w = W_FFN + 1 + 8 * g + i
                    sp.wait_ge(w_lo, w - 1)
                    s = w_raw[(W_FFN + 1 + i) % 2]
                    dst = WRAW[(W_FFN + 1 + i) % 2]
                    if i % 2 == 0:
                        sp.dma_start(dst[:, :], a["w_down"][0, bass.ds(g * 512 + (i // 2) * P, P), :]).then_inc(s, 16)
                    else:
                        sp.dma_start(as_block(dst), a["w_up"][0, :, bass.ds(g * 512 + (i // 2 + 1) * P, P)]
                                     .rearrange("(k p) n -> p k n", p=P)).then_inc(s, 16)
                if not last:
                    w = W_FFN + 8 + 8 * g
                    sp.wait_ge(w_lo, w - 1)
                    sp.dma_start(as_block(WRAW[W_FFN % 2]), a["w_up"][0, :, bass.ds(g * 512 + 512, P)]
                                 .rearrange("(k p) n -> p k n", p=P)).then_inc(w_raw[W_FFN % 2], 16)

            with sp.Fori(0, FF // 512 - 1) as g:
                mlp_w(g, False)
            mlp_w(FF // 512 - 1, True)
            sp.wait_ge(mm, NC * NB1 + 12 * (FF // 512))
            for i in range(2):
                sp.wait_ge(x1_st[i], 16 * ((NT + 1 - i) // 2))
            sp.dma_start(GF[:, :], a["g_post_ffn"].to_broadcast([P, D])).then_inc(gb_in, 16)
            for t in range(NT):
                if t >= 2:
                    sp.wait_ge(y_ok, t - 1)
                sp.dma_start(X1F[t % 2][:, :], x1s[t * P:(t + 1) * P, :]).then_inc(x1_in[t % 2], 16)
                if t >= 1:
                    y_store(sp, t - 1)
            y_store(sp, NT - 1)
            for i in range(2):
                sp.wait_ge(y_st[i], 16 * ((NT + 1 - i) // 2))
            sp.wait_ge(H.sr_st, 16 * HH + 16)
            sp.wait_ge(H.s8_st[0], 16 * HH + 16)


        @block.tensor
        def _(pe):
            def norm_transpose(tt, src):
                b = 3 + 2 * (tt % 2)
                pe.wait_ge(n_hr, tt + 1)
                for g in range(2):
                    if tt >= 2:
                        pe.wait_ge(n_tm, 2 * (tt - 2) + g + 1)
                    for i in range(4):
                        k = 4 * g + i
                        last = pe.transpose(psum[b + g][:, i * P:(i + 1) * P], src[:, k * P:(k + 1) * P], ident[:, :])
                    last.then_inc(n_tp, 1)

            def gemm(n, m, p, c, first=False, w=None, part=range(KT), beside=None):
                if c == 0:
                    pe.wait_ge(w_lo, (n if w is None else w) + 1)
                if not first:
                    pe.wait_ge(ev, NC * (n - 1) + c + 1)
                s = slice(c * CH, (c + 1) * CH)
                for k in part:
                    pe.matmul(psum[c][:, 0:CH], WHI[p][:, k, :], XH[:, k, s], start=(k == 0), stop=False)
                    pe.matmul(psum[c][:, 0:CH], WHI[p][:, k, :], XL[:, k, s], start=False, stop=False)
                    last = pe.matmul(psum[c][:, 0:CH], WLO[p][:, k, :], XH[:, k, s], start=False, stop=(k == KT - 1))
                    if k == KT - 1:
                        last.then_inc(mm, 1)
                    if beside:
                        beside(k)

            for s in (R.rb, H.rb, R.st_full, H.st_full):
                pe.sem_inc(s, 1)
            pe.wait_ge(c_in, 48)
            for tt in range(NT):
                norm_transpose(tt, HR[tt % 2])
                if tt in (3, 6):
                    pe.wait_ge(n_xh, 2 * tt)
                    pe.wait_ge(n_xl, 2 * tt)
                    gemm(0, 0, 0, tt // 3 - 1, first=True, part=range(0, KT // 2))
                if tt in (4, 7):
                    gemm(0, 0, 0, tt // 3 - 1, first=True, part=range(KT // 2, KT))
            pe.wait_ge(n_xh, 2 * NT)
            pe.wait_ge(n_xl, 2 * NT)
            gemm(0, 0, 0, NC - 1, first=True)
            for c in range(NC):
                gemm(1, 0, 1, c)
            with pe.Fori(1, 4) as m:
                for p in range(2):
                    for c in range(NC):
                        gemm(2 * m + p, m, p, c)

            def ret_a(h, t):
                s = slice(t * P, (t + 1) * P)
                if t == 0:
                    pe.wait_ge(R.in_[2], 16 * h + 16)
                    pe.wait_ge(R.q_ok, h + 1)
                    pe.wait_ge(R.k_ok, h + 1)
                    pe.wait_ge(R.kz8, 8 * h + 1)
                pe.wait_ge(R.kv, 9 * h + t + 1)
                for e in range(2):
                    pe.transpose(PT[:, e * P:(e + 1) * P], ZV[:, e, s], ident[:, :])
                for e in range(2):
                    last = pe.transpose(PT[:, (2 + e) * P:(3 + e) * P], KR[:, e, s], ident[:, :])
                last.then_inc(R.t_full, 1)
                pe.wait_ge(R.att, 9 * h + t + 1)
                pe.matmul(PSC[:, 0:P], KR[:, 0, s], QR[:, 0, s], start=True, stop=False)
                pe.matmul(PSC[:, 0:P], KR[:, 1, s], QR[:, 1, s], start=False, stop=True).then_inc(R.sc, 1)

            def ret_b(h, t):
                s = slice(t * P, (t + 1) * P)
                kv, at = KVT[t % 2], ATT[t % 2]
                pe.wait_ge(R.kv, 9 * h + t + 2)
                pe.wait_ge(R.att, 9 * h + t + 2)
                pe.wait_ge(R.o_ev, 9 * h + t + 1)
                pe.wait_ge(R.st_ev, 16 * h + t + 1)
                for e in range(2):
                    es = slice(e * P, (e + 1) * P)
                    last = pe.matmul(PO[:, es], kv[:, 0, es], at[:, :], start=(e == 0), stop=(t == 0), skip_group_check=True)
                    if 0 < t < NT - 1:
                        for d in range(2):
                            last = pe.matmul(PO[:, es], SR[:, d, es], QX[:, d, s], start=False, stop=(d == 1), skip_group_check=True)
                last.then_inc(R.o_full, 1)
                for d in range(2):
                    last = pe.matmul(PST[:, d * RD:(d + 1) * RD], kv[:, 1, d * P:(d + 1) * P], kv[:, 0, :],
                                     start=(d == 0), stop=(d == 1), skip_group_check=True)
                last.then_inc(R.st_full, 1)

            def stream_out(h, b, e):
                st = S8A[:, b, :, :] if b < 4 else S8B[:, b - 4, :, :]
                if b == 0 and e == 0:
                    pe.wait_ge(R.o_ev, 9 * h + NT)
                    pe.wait_ge(R.s8_in[0], 32 * h + 32)
                    pe.wait_ge(R.s8_in[1], 32 * h + 32)
                for d in range(2):
                    pe.matmul(PO[:, e * P + b * TS:e * P + (b + 1) * TS], st[:, d, e * P:(e + 1) * P],
                              QX[:, d, TP + b * TS:TP + (b + 1) * TS], start=(b + d + e == 0), stop=False,
                              skip_group_check=True)

            def ret_b8(h):
                kv, at = KVT[0], ATT[0]
                pe.wait_ge(R.kv, 9 * h + NT + 1)
                pe.wait_ge(R.st_ev, 16 * h + NT)
                for b in range(NS):
                    stream_out(h, b, 1)
                    bank = (PST, PRB)[b % 2]
                    pe.wait_ge(R.kz8, 8 * h + b + 2)
                    if b == 1:
                        pe.wait_ge(R.w_ok, 3 * h + 3)
                    if b >= 2:
                        pe.wait_ge(R.st_ev, 16 * h + 8 + b)
                    for d in range(2):
                        last = pe.matmul(bank[:, d * RD:(d + 1) * RD], KZ8[b % 2][:, d * P:(d + 1) * P], kv[:, 0, :],
                                         start=(d == 0), stop=(d == 1), skip_group_check=True)
                    last.then_inc(R.st_full, 1)
                pe.wait_ge(R.att, 9 * h + NT + 1)
                for e in range(2):
                    es = slice(e * P, (e + 1) * P)
                    last = pe.matmul(PO[:, es], kv[:, 0, es], at[:, :], start=False, stop=True, skip_group_check=True)
                last.then_inc(R.o_full, 1)

            def head_sum(K, h, c, ne):
                pe.wait_ge(K.sq, 3 * h + c + 1)
                pe.wait_ge(K.w_ok, 3 * h + c + 1)
                if c == 2:
                    pe.wait_ge(K.st_ev, 16 * h + 17)
                for r in range(TPC):
                    for e in range(ne):
                        last = pe.matmul(PRB[:, r:r + 1], SQ[:, e, r * P:(r + 1) * P], ones[:, 0:1],
                                         start=(e == 0), stop=(e == ne - 1))
                last.then_inc(K.rb, 1)

            def head_spread(K, h, c):
                pe.wait_ge(K.dg, 3 * h + c + 1)
                pe.matmul(PRB[:, 0:CH], ones[:, :], DG[:, :, :].rearrange("p r t -> p (r t)"),
                          start=True, stop=True).then_inc(K.rbb, 1)

            with pe.Fori(0, RH) as h:
                for s in range(RET_SLOTS):
                    j, c = divmod(s, NC)
                    gemm(8 + 8 * h + j, 4 + 4 * h + j // 2, j % 2, c,
                         beside=(lambda b: stream_out(h, b, 0)) if s == RA + NT else None)
                    for i in range(NC):
                        if s == R_NORM[i]:
                            head_sum(R, h, i, 2)
                        if s == R_NORM[i] + 1:
                            head_spread(R, h, i)
                    for t in range(NT):
                        if s == RA + t:
                            ret_a(h, t)
                        if s == RA + 1 + t:
                            ret_b(h, t) if t < NT - 1 else ret_b8(h)

            def hg_a(h, t):
                s = slice(t * P, (t + 1) * P)
                c, r = divmod(t, TPC)
                if t == 0:
                    pe.wait_ge(H.in_[2], 16 * h + 16)
                    pe.wait_ge(H.fk, h + 1)
                    pe.wait_ge(H.kz8, 8 * h + 1)
                if r == 0:
                    pe.wait_ge(H.q_ok, 3 * h + c + 1)
                    pe.wait_ge(H.k_ok, 3 * h + c + 1)
                pe.wait_ge(H.kv, 9 * h + t + 1)
                pe.wait_ge(H.att, 9 * h + t + 1)
                pe.transpose(PT[:, 0:P], HZ[2][:, s], ident[:, :])
                tr = pe.transpose(PT[:, P:2 * P], KRH[:, s], ident[:, :])
                if t == NT - 1:
                    tr.then_inc(H.t_full, 1)
                last = pe.matmul(PSC[:, 0:P], KK[:, s], HZ[0][:, s], start=True, stop=True, skip_group_check=True)
                kt = slice(r * P, (r + 1) * P)
                qt = slice(r * 64, (r + 1) * 64)
                for l in range(min(6, LEV if t < NT - 1 else LEVS)):
                    last = pe.matmul(PSC[:, P + 64 * l:P + 64 * (l + 1)], KE[c % 2][:, l, kt], QE[c % 2][:, l, qt],
                                     start=True, stop=True, skip_group_check=True)
                last.then_inc(H.sc, 1)
                if t < NT - 1:
                    last = pe.matmul(PT[:, 2 * P:2 * P + 64], KE[c % 2][:, 6, kt], QE[c % 2][:, 6, qt], start=True, stop=True)
                    last.then_inc(H.t_full, 1)

            def hg_b(h, t):
                s = slice(t * P, (t + 1) * P)
                kv, at = KVT[t % 2], ATT[t % 2]
                pe.wait_ge(H.kv, 9 * h + t + 2)
                pe.wait_ge(H.att, 9 * h + t + 2)
                pe.wait_ge(H.o_ev, 9 * h + t + 1)
                pe.wait_ge(H.st_ev, 16 * h + t + 1)
                if t == NT - 1:
                    pe.wait_ge(H.s8_in[0], 16 * h + 16)
                last = pe.matmul(PO[:, 0:P], kv[:, 0, 0:P], at[:, :], start=True, stop=(t == 0), skip_group_check=True)
                if 0 < t < NT - 1:
                    last = pe.matmul(PO[:, 0:P], SH[:, :], QP[:, s], start=False, stop=True, skip_group_check=True)
                if t == NT - 1:
                    for b in range(NS):
                        last = pe.matmul(PO[:, b * TS:(b + 1) * TS], SH8[:, b, :], QP[:, TP + b * TS:TP + (b + 1) * TS],
                                         start=False, stop=(b == NS - 1), skip_group_check=True)
                last.then_inc(H.o_full, 1)
                if t < NT - 1:
                    pe.matmul(PST[:, 0:P], kv[:, 1, 0:P], kv[:, 0, 0:P], start=True, stop=True).then_inc(H.st_full, 1)
                    return
                pe.wait_ge(H.kz8, 8 * h + 9)
                for b in range(NS):
                    if b == 4:
                        pe.wait_ge(H.w_ok, 3 * h + 3)
                    last = pe.matmul((PST, PRB)[b // 4][:, b % 4 * P:(b % 4 + 1) * P], KM8[b], kv[:, 0, 0:P],
                                     start=True, stop=True, skip_group_check=True)
                    if b % 4 == 3:
                        last.then_inc(H.st_full, 1)

            pe.wait_ge(R.kv, 9 * RH + 1)
            pe.wait_ge(R.kz8, 8 * RH + 1)
            pe.wait_ge(R.att, 9 * RH + 1)
            pe.wait_ge(R.o_ev, 9 * RH + 1)
            pe.wait_ge(R.st_ev, 16 * RH + 1)
            pe.wait_ge(R.w_ok, 3 * RH + 1)
            def hg_pair(i):
                for u in range(2):
                    h = 2 * i + u
                    for s in range(HG_SLOTS):
                        j, c = divmod(s, NC)
                        jj = HG_BLOCKS * u + j
                        gemm(40 + 10 * i + jj, 20 + 5 * i + jj // 2, jj % 2, c)
                        for x in range(NC):
                            if s == H_NORM[x]:
                                head_sum(H, h, x, 1)
                            if s == H_NORM[x] + 1:
                                head_spread(H, h, x)
                        if s >= HA and s - HA < NT:
                            hg_a(h, s - HA)
                        if s > HA and s - HA - 1 < NT:
                            hg_b(h, s - HA - 1)

            with pe.Fori(0, HH // 2) as i:
                hg_pair(i)

            for br in range(2):
                for p in range(2):
                    for c in range(NC):
                        n = NRB + KT * br + p
                        if p == 0:
                            pe.wait_ge(sp_hi, 3 * KT * br + KT * (c + 1))
                            pe.wait_ge(sp_lo, 3 * KT * br + KT * (c + 1))
                        gemm(n, None, p, c, w=w_item(n))
                if br == 0:
                    with pe.Fori(1, KT // 2) as i:
                        for p in range(2):
                            for c in range(NC):
                                gemm(NRB + 2 * i + p, None, p, c)
                else:
                    for n in range(NRB + KT + 2, NB1):
                        for c in range(NC):
                            gemm(n, None, n % 2, c, w=w_item(n))

            def up(g, b, c):
                s = slice(c * CH, (c + 1) * CH)
                for k in range(KT):
                    pe.matmul(psum[c][:, 0:CH], WHI[b % 2][:, k, :], XH[:, k, s], start=(k == 0), stop=False)
                    pe.matmul(psum[c][:, 0:CH], WHI[b % 2][:, k, :], XL[:, k, s], start=False, stop=False)
                    last = pe.matmul(psum[c][:, 0:CH], WLO[b % 2][:, k, :], XH[:, k, s], start=False, stop=(k == KT - 1))
                last.then_inc(mm, 1)

            pe.wait_ge(w_lo, W_OUT + KT)
            pe.wait_ge(H.kv, 9 * HH + 1)
            pe.wait_ge(H.kz8, 8 * HH + 1)
            pe.wait_ge(H.att, 9 * HH + 1)
            pe.wait_ge(H.o_ev, 9 * HH + 1)
            pe.wait_ge(H.st_ev, 16 * HH + 1)
            pe.wait_ge(H.w_ok, 3 * HH + 1)
            for t in range(NT + 2):
                if t < NT:
                    s = slice(t * P, (t + 1) * P)
                    pe.wait_ge(sp_hi, 6 * KT + KT * (t // TPC + 1))
                    pe.wait_ge(sp_lo, 6 * KT + KT * (t // TPC + 1))
                    if t == 1:
                        pe.wait_ge(ev, NC * NB1 - 1)
                    if t == 2:
                        pe.wait_ge(ev, NC * NB1)
                    if t >= 2:
                        pe.wait_ge(d_x1, t - 1)
                    for q in range(2):
                        bank = row_bank(t, q)
                        ns = slice(512 * q, 512 * (q + 1))
                        for k in range(KT):
                            pe.matmul(bank[:, :], XH[:, k, s], WOH[:, k, ns], start=(k == 0), stop=False)
                            pe.matmul(bank[:, :], XH[:, k, s], WOL[:, k, ns], start=False, stop=False)
                            last = pe.matmul(bank[:, :], XL[:, k, s], WOH[:, k, ns], start=False, stop=(k == KT - 1))
                    last.then_inc(d_mm, 1)
                if t >= 2:
                    norm_transpose(NT + t - 2, HR2[(NT + t - 2) % 2])
                if t in (NT - 1, NT):
                    c = t - NT + 1
                    pe.wait_ge(n_xh, 2 * NT + 2 * TPC * (c + 1))
                    pe.wait_ge(n_xl, 2 * NT + 2 * TPC * (c + 1))
                    pe.wait_ge(d_x1, NT - 1)
                    pe.wait_ge(w_lo, W_FFN + 1)
                    up(0, 0, c)

            pe.wait_ge(n_xh, 4 * NT)
            pe.wait_ge(n_xl, 4 * NT)
            pe.wait_ge(d_x1, NT)
            def mlp(g, first):
                for b in range(4):
                    pe.wait_ge(w_lo, W_FFN + 8 * g + 2 * b + 1)
                    for c in range(NC):
                        if b:
                            pe.wait_ge(f_t1, NC * (4 * g + b - 1) + c + 1)
                        if not (first and b == 0 and c < 2):
                            up(g, b, c)
                pe.wait_ge(w_lo, W_FFN + 8 * g + 8)
                for t in range(NT):
                    s = slice(t * P, (t + 1) * P)
                    pe.wait_ge(f_ul, 12 * g + 10 + t // TPC)
                    for q in range(2):
                        x = 2 * t + q
                        bank = psum[3 + x % 5]
                        ns = slice(512 * q, 512 * (q + 1))
                        if x >= 5:
                            pe.wait_ge(dn_ev, 18 * g + x - 5 + 2)
                        else:
                            pe.wait_ge(dn_ev, 18 * g + 1)
                        for k in range(4):
                            pe.matmul(bank[:, :], UH[:, k, s], WDH[:, k, ns], start=(k == 0), stop=False)
                            pe.matmul(bank[:, :], UH[:, k, s], WDL[:, k, ns], start=False, stop=False)
                            last = pe.matmul(bank[:, :], UL[:, k, s], WDH[:, k, ns], start=False, stop=(k == 3))
                        last.then_inc(dn, 1)
            mlp(0, True)
            with pe.Fori(1, FF // 512) as g:
                mlp(g, False)

        @block.scalar
        def _(act):
            ch = Chain(act, act_ch)

            def copy(dst, src):
                return act.activation(dst, src, ACT.Copy)

            def whi(w, p, m, src, dst, free=None):
                act.wait_ge(w_raw[p], 16 * m + 16)
                if free is not None:
                    act.wait_ge(mm, free)
                copy(dst, src).then_inc(w_hi, 1)

            def whi_block(n, m, p, free=True):
                whi(n, p, m, as_block(WRAW[p]), WHI[p][:, :, :], 3 * n - 3 if free else None)

            def evac(n, m, p, c, first=False):
                act.wait_ge(mm, NC * n + c + 1)
                if c == 0 and not first:
                    act.wait_ge(z_st[p], 16 * m)
                copy(ZST[p][:, c * CH:(c + 1) * CH], psum[c][:, 0:CH]).then_inc(ev, 1)

            def norm_sq(tt, src, junk):
                if tt:
                    act.wait_ge(n_ss, tt)
                act.activation(junk[:, :], src[:, :], ACT.Square, accum_out=ssc[:, tt:tt + 1]).then_inc(n_ss, 1)

            def norm_xh(tt, tm, t):
                for g in range(2):
                    act.wait_ge(n_tm, 2 * tt + g + 1)
                    copy(XH[:, 4 * g:4 * g + 4, t * P:(t + 1) * P], tm[g][:, :, :]).then_inc(n_xh, 1)

            def first_sq(tt):
                act.wait_ge(x_in[tt], 16)
                norm_sq(tt, XR[tt], SQJ)

            first_sq(0)
            for tt in range(NT + 1):
                if tt < NT - 1:
                    first_sq(tt + 1)
                if tt < NT:
                    act.wait_ge(n_rs, tt + 1)
                    if tt >= 2:
                        act.wait_ge(n_tp, 2 * (tt - 2) + 2)
                    act.activation(HR[tt % 2][:, :], XR[tt][:, :], ACT.Copy, scale=rsc[:, tt:tt + 1]).then_inc(n_hr, 1)
                if tt == 2:
                    whi_block(0, 0, 0, free=False)
                if tt == 5:
                    whi_block(1, 0, 1, free=False)
                if tt:
                    norm_xh(tt - 1, TM, tt - 1)
            act.wait_ge(lb_ch, 2)
            act.activation(LB[:, :, :], LB[:, :, :], ACT.Exp).then_inc(lb_e, 1)
            for s in (R.kv, R.o_ev, R.kz8, H.kv, H.o_ev, H.kz8):
                act.sem_inc(s, 1)

            def block_slot(n, m, p, c):
                if c == 0:
                    mn, pn = (m, 1) if p == 0 else (m + 1, 0)
                    whi_block(n + 1, mn, pn)
                evac(n, m, p, c)

            act.wait_ge(n_xl, 2 * NT)
            for n in range(2):
                for c in range(NC):
                    if c == 0 and n == 1:
                        whi_block(2, 1, 0)
                    evac(n, 0, n, c, first=True)
            with act.Fori(1, 4) as m:
                for p in range(2):
                    for c in range(NC):
                        block_slot(2 * m + p, m, p, c)

            def kv_ret(h, t):
                act.wait_ge(R.t_full, 9 * h + t + 1)
                act.wait_ge(R.st_full, 16 * h + (t if t >= 2 else 1))
                if t == 0:
                    act.wait_ge(R.in_[3], 16 * h + 16)
                if t < NT - 1:
                    copy(KVT[t % 2][:, 0, :], PT[:, 0:RD])
                    act.activation(KVT[t % 2][:, 1, :], PT[:, RD:2 * RD], ACT.Copy, scale=ZETA).then_inc(R.kv, 1)
                else:
                    copy(KVT[t % 2][:, 0, :], PT[:, 0:RD]).then_inc(R.kv, 1)

            def kz_ret(h, streams):
                for b in streams:
                    if b >= 2:
                        act.wait_ge(R.st_full, 16 * h + 8 + b)
                    act.activation(KZ8[b % 2][:, :], PT[:, RD:2 * RD], ACT.Copy,
                                   scale=HC[:, 4 * P + 3 + b:4 * P + 4 + b]).then_inc(R.kz8, 1)

            def head_sq(K, h, c, ne, src, gate, g_in, g_v):
                act.wait_ge(K.o_ev, 9 * h + TPC * c + TPC + 1)
                act.wait_ge(K.rb, 3 * h + c + 1)
                act.activation(SQ[:, 0:ne, :], src, ACT.Square).then_inc(K.sq, 1)
                act.wait_ge(g_in, g_v)
                act.wait_ge(K.u_ok, 3 * h + c + 1)
                act.activation(SG[:, 0:ne, :], gate, ACT.Sigmoid).then_inc(K.sg, 1)

            with act.Fori(0, RH) as h:
                for s in range(RET_SLOTS):
                    j, c = divmod(s, NC)
                    block_slot(8 + 8 * h + j, 4 + 4 * h + j // 2, j % 2, c)
                    for t in range(NT):
                        if s == RA + t:
                            kv_ret(h, t)
                        if s == RA + 1 + t:
                            if t == NT - 1:
                                kz_ret(h, range(2, NS))
                            act.wait_ge(R.o_full, 9 * h + t + 1)
                            copy(QX[:, :, t * P:(t + 1) * P],
                                 PO[:, 0:RD].rearrange("p (e t) -> p e t", e=2)).then_inc(R.o_ev, 1)
                    if s == RA + NT - 1:
                        kz_ret(h, range(2))
                    for i in range(NC):
                        if s == R_NORM[i] - 1:
                            g_v = 32 * h + (16, 16, 32)[i]
                            if i == 1:
                                g_v = 16 * h + 16
                            head_sq(R, h, i, 2, QX[:, :, i * CH:(i + 1) * CH], ZG[i % 2][:, :, :], R.g_in[i % 2], g_v)

            ret_mixed(act)

            def kv_hg(h, t):
                act.wait_ge(H.t_full, 9 * h + t + 1)
                act.wait_ge(H.st_full, 10 * h + (t if t >= 2 else 1))
                if t < NT - 1:
                    copy(KVT[t % 2][:, :, 0:P], PT[:, 0:2 * P].rearrange("p (a d) -> p a d", a=2)).then_inc(H.kv, 1)
                else:
                    copy(KVT[t % 2][:, 0, 0:P], PT[:, 0:P]).then_inc(H.kv, 1)

            def kz_hg(h):
                for b in range(NS):
                    act.activation(KM8[b], PT[:, P:2 * P], ACT.Copy, scale=RM[:, b:b + 1]).then_inc(H.kz8, 1)

            act.wait_ge(c_in2, 48)

            def forget(h):
                act.wait_ge(H.in_[1], 16 * h + 16)
                act.activation(FG[:, :], HZ[1][:, :], ACT.Sigmoid).then_inc(H.f_ok, 1)

            def piece(i):
                c, k = divmod(i % (3 * KT), KT)
                cs = slice(c * CH, (c + 1) * CH)
                if i < 3 * KT:
                    act.wait_ge(ua_in[c], 32 if c else 64)
                    copy(XH[:, k, cs], UA[c][k]).then_inc(sp_hi, 1)
                else:
                    act.wait_ge(ur1_in[k], 16)
                    copy(XH[:, k, cs], UR1[:, k, cs]).then_inc(sp_hi, 1)

            def hg_pair(i, last):
                for u in range(2):
                    h = 2 * i + u
                    end = last and u == 1
                    for s in range(HG_SLOTS):
                        j, c = divmod(s, NC)
                        jj = HG_BLOCKS * u + j
                        block_slot(40 + 10 * i + jj, 20 + 5 * i + jj // 2, jj % 2, c)
                        if s == HG_SLOTS - 2 and not end:
                            forget(h + 1)
                        if s >= HA and s - HA < NT:
                            kv_hg(h, s - HA)
                            if s - HA == NT - 1:
                                kz_hg(h)
                        if s > HA and s - HA - 1 < NT:
                            t = s - HA - 1
                            act.wait_ge(H.o_full, 9 * h + t + 1)
                            copy(OH[:, t * P:(t + 1) * P], PO[:, 0:P]).then_inc(H.o_ev, 1)
                        for x in range(NC):
                            if s == H_NORM[x] - 1:
                                head_sq(H, h, x, 1, OH[:, x * CH:(x + 1) * CH].unsqueeze(1),
                                        HZ[3][:, x * CH:(x + 1) * CH].unsqueeze(1), H.in_[3], 16 * h + 16)
                        if end and s >= HG_SLOTS - 2:
                            for x in range(KT):
                                piece(KT * (s - HG_SLOTS + 2) + x)
                if last:
                    for x in range(KT):
                        piece(2 * KT + x)

            forget(0)
            with act.Fori(0, HH // 2 - 1) as i:
                hg_pair(i, False)
            hg_pair(HH // 2 - 1, True)

            def split_next(n):
                w = w_item(n + 1)
                whi(w, w % 2, w // 2, as_block(WRAW[w % 2]), WHI[(n + 1) % 2][:, :, :], 3 * n)

            split_next(NRB)
            for k in range(2 * KT):
                n = NRB + k
                act.wait_ge(mg_in[k % 2], 16 * (k // 2 + 1))
                act.activation(MG[k % 2][:, :], MG[k % 2][:, :], ACT.Sigmoid).then_inc(mg_ok, 1)
                if k >= KT:
                    if k == KT:
                        act.wait_ge(sp_lo, 6 * KT)
                    w = w_row(k - KT)
                    whi(w, w % 2, w // 2, WRAW[w % 2][:, :], WOH[:, k - KT, :])
                if 0 < k < 2 * KT - 1:
                    split_next(n)
                if k == KT - 1:
                    for c in range(NC):
                        act.wait_ge(mm, NC * n + c + 1)
                        for x in range(KT):
                            piece(3 * KT + KT * c + x)
            for c in range(NC):
                act.wait_ge(ev, NC * (NB1 - 1) + c + 1)
                for k in range(KT):
                    copy(XH[:, k, c * CH:(c + 1) * CH], MIX[:, k, c * CH:(c + 1) * CH]).then_inc(sp_hi, 1)
            act.wait_ge(sp_lo, 9 * KT)
            act.wait_ge(gb_in, 16)
            for t in range(NT + 2):
                if t < NT:
                    act.wait_ge(d_mm, t + 1)
                    act.wait_ge(n_ss, NT + t)
                    if t:
                        act.wait_ge(d_ss, t)
                    for q in range(2):
                        last = act.activation(SQJ2[:, 512 * q:512 * (q + 1)], row_bank(t, q)[:, :], ACT.Square,
                                              accum_out=dss[:, 2 * t + q:2 * t + q + 1])
                    last.then_inc(d_ss, 1)
                if t == 3:
                    whi(W_FFN, 0, W_FFN // 2, as_block(WRAW[0]), WHI[0][:, :, :])
                if t >= 2:
                    norm_xh(NT + t - 2, TM2, t - 2)
                if t < NT:
                    act.wait_ge(d_x1, t + 1)
                    act.wait_ge(d_ss, t + 1)
                    act.activation(SQJ2[:, :], X1R[t % 2][:, :], ACT.Square, accum_out=ssc[:, NT + t:NT + t + 1]).then_inc(n_ss, 1)
            NG = FF // 512
            act.wait_ge(n_xl, 4 * NT)
            act.wait_ge(w_lo, W_FFN + 1)

            def mlp(g, last):
                w0 = W_FFN + 1 + 8 * g

                def split(i):
                    q = (W_FFN + 1 + i) % 2
                    m = (W_FFN + 1 + i) // 2 + 4 * g
                    if i % 2 == 0:
                        if i == 0:
                            act.wait_ge(dn, 18 * g + 1)
                        whi(w0 + i, q, m, WRAW[q][:, :], WDH[:, i // 2, :])
                    else:
                        b = (i // 2 + 1) % 4
                        whi(w0 + i, q, m, as_block(WRAW[q]), WHI[b % 2][:, :, :],
                            NC * (NB1 + 4 * g + i // 2))
                for b in range(4):
                    for c in range(NC):
                        if c == 0:
                            split(2 * b)
                        if c == 1 and b < 3:
                            split(2 * b + 1)
                        x = NC * b + c
                        act.wait_ge(mm, NC * NB1 + 12 * g + x + 1)
                        if x >= 2:
                            act.wait_ge(f_t2, 12 * g + x - 1)
                        act.activation(T1[x % 2][:, :], psum[c][:, 0:CH], ACT.Relu).then_inc(f_t1, 1)
                        act.wait_ge(f_t2, 12 * g + x + 1)
                        copy(UH[:, b, c * CH:(c + 1) * CH], T2[x % 2][:, :]).then_inc(f_uh, 1)
                if not last:
                    split(7)
            act.sem_inc(dn, 1)
            with act.Fori(0, NG - 1) as g:
                mlp(g, False)
            mlp(NG - 1, True)
            act.wait_ge(mm, NC * NB1 + 12 * NG)
            for t in range(NT):
                act.wait_ge(dn_ev, 18 * (NG - 1) + 2 * t + 3)
                if t:
                    act.wait_ge(y_ss, t)
                act.activation(SQJ3[:, :], ACC[:, t, :], ACT.Square, accum_out=yss[:, t:t + 1]).then_inc(y_ss, 1)

        @block.vector
        def _(dve):
            ch = Chain(dve, dve_ch)

            def wlo(w, src, hi, lo):
                dve.wait_ge(w_hi, w + 1)
                dve.tensor_tensor(lo, src, plain(hi), ALU.subtract).then_inc(w_lo, 1)

            def wlo_block(n, p):
                wlo(n, as_block(WRAW[p]), WHI[p][:, :, :], WLO[p][:, :, :])

            def norm_ms(tt):
                dve.wait_ge(n_ss, tt + 1)
                dve.tensor_scalar(msc[:, tt:tt + 1], ssc[:, tt:tt + 1], 1.0 / D, EPS, ALU.mult, ALU.add).then_inc(n_ms, 1)

            def norm_row(tt, src, dst):
                dve.wait_ge(n_rs, tt + 1)
                if tt >= 2:
                    dve.wait_ge(n_tp, 2 * (tt - 2) + 2)
                dve.tensor_scalar(dst[:, :], src[:, :], rsc[:, tt:tt + 1], None, ALU.mult).then_inc(n_hr, 1)

            def norm_cols(tt, tm, which, t):
                b = 3 + 2 * (tt % 2)
                for g in range(2):
                    dve.wait_ge(n_tp, 2 * tt + g + 1)
                    if tt:
                        dve.wait_ge(n_xh, 2 * (tt - 1) + g + 1)
                        dve.wait_ge(n_xl, 2 * (tt - 1) + g + 1)
                    gain = gcol[:, which, 4 * g:4 * g + 4].unsqueeze(2).to_broadcast([P, 4, P])
                    dve.tensor_tensor(tm[g][:, :, :], psum[b + g][:, :].rearrange("p (k t) -> p k t", k=4),
                                      gain, ALU.mult).then_inc(n_tm, 1)
                for g in range(2):
                    dve.wait_ge(n_xh, 2 * tt + g + 1)
                    ks, ts = slice(4 * g, 4 * g + 4), slice(t * P, (t + 1) * P)
                    dve.tensor_tensor(XL[:, ks, ts], tm[g][:, :, :], plain(XH[:, ks, ts]), ALU.subtract).then_inc(n_xl, 1)

            dve.wait_ge(c_in, 48)
            dve.tensor_tensor(LBM[:, :], LB[:, 0, :], LB[:, 1, :], ALU.max).then_inc(lb_ch, 1)
            dve.wait_ge(lb_ch, 1)
            dve.tensor_tensor(LB[:, :, :], LB[:, :, :], LBM[:, :].unsqueeze(1).to_broadcast([P, 2, HH]),
                              ALU.subtract).then_inc(lb_ch, 1)
            norm_ms(0)
            for tt in range(NT + 1):
                if tt < NT - 1:
                    norm_ms(tt + 1)
                if tt == 3:
                    wlo_block(0, 0)
                if tt == 6:
                    wlo_block(1, 1)
                if tt:
                    norm_cols(tt - 1, TM, 0, tt - 1)
            dve.wait_ge(lb_e, 1)
            ch(dve.tensor_tensor(LBM[:, :], LB[:, 0, :], LB[:, 1, :], ALU.add))
            ch(dve.reciprocal(LBM[:, :], LBM[:, :]))
            ch(dve.tensor_tensor(LBC[:, 0, :], LB[:, 0, :], LBM[:, :], ALU.mult))
            ch(dve.tensor_scalar(LBC[:, 1, :], LBC[:, 0, :], -1.0, 1.0, ALU.mult, ALU.add))
            ch(dve.memset(ones[:, :], 1.0))
            ch.reset()
            for s in (R.att, R.st_ev, R.ms, R.u_ok, R.w_ok, H.att, H.st_ev, H.ms, H.u_ok, H.w_ok):
                dve.sem_inc(s, 1)

            wlo_block(2, 0)
            with dve.Fori(1, 4) as m:
                for p in range(2):
                    wlo_block(2 * m + p + 1, (p + 1) % 2)

            def norm_sum(K, h, c, width):
                dve.wait_ge(K.rb, 3 * h + c + 2)
                dve.tensor_scalar(MS[:, :], PRB[:, 0:TPC], 1.0 / width, EPS, ALU.mult, ALU.add).then_inc(K.ms, 1)
                dve.wait_ge(K.rs, 3 * h + c + 1)
                dve.tensor_tensor(DG[:, :, :], ident[:, :].unsqueeze(1).to_broadcast([P, TPC, P]),
                                  RST[:, :].unsqueeze(2).to_broadcast([P, TPC, P]), ALU.mult).then_inc(K.dg, 1)

            def gated(K, h, c, ne, src):
                dve.wait_ge(K.gt, 3 * h + c + 1)
                dve.wait_ge(K.rbb, 3 * h + c + 1)
                dve.tensor_tensor(SG[:, 0:ne, :], SG[:, 0:ne, :],
                                  PRB[:, 0:CH].unsqueeze(1).to_broadcast([P, ne, CH]), ALU.mult).then_inc(K.w_ok, 1)
                dve.wait_ge(K.w_ok, 3 * h + c + 2)
                dve.wait_ge(K.u_st, 48 * h + 16 * c + 16)
                dve.tensor_tensor(UB[:, 0:ne, :], SG[:, 0:ne, :], src, ALU.mult).then_inc(K.u_ok, 1)

            def rotate_q(h, c):
                s = slice(c * CH, (c + 1) * CH)
                cs, sn = CS[:, 0, s], CS[:, 1, s]
                dve.tensor_tensor(RTMP[:, 0, :], ZQ[:, 0, s], cs, ALU.mult)
                ch(dve.tensor_tensor(RTMP[:, 1, :], ZQ[:, 1, s], sn, ALU.mult))
                ch(dve.tensor_tensor(QR[:, 0, s], RTMP[:, 0, :], RTMP[:, 1, :], ALU.subtract))
                dve.tensor_tensor(RTMP[:, 0, :], ZQ[:, 0, s], sn, ALU.mult)
                ch(dve.tensor_tensor(RTMP[:, 1, :], ZQ[:, 1, s], cs, ALU.mult))
                ch(dve.tensor_tensor(QR[:, 1, s], RTMP[:, 0, :], RTMP[:, 1, :], ALU.add))
                n = TPC if c < NC - 1 else TPC - 1
                for d in range(2):
                    v = lambda x: x[:, d, c * CH:c * CH + n * P].rearrange("p (a t) -> p a t", t=P)
                    last = dve.tensor_tensor(v(QX), v(QR), XI[:, 0, :].unsqueeze(1).to_broadcast([P, n, P]), ALU.mult)
                    if c == NC - 1:
                        last = dve.tensor_tensor(QX[:, d, TP:T], QR[:, d, TP:T], XI[:, 1, :], ALU.mult)
                ch(last)

            def rotate_k0(c):
                s = slice(c * CH, (c + 1) * CH)
                dve.tensor_tensor(RTMP[:, 0, :], ZK[:, 0, s], CS[:, 0, s], ALU.mult)
                ch(dve.tensor_tensor(RTMP[:, 1, :], ZK[:, 1, s], CS[:, 1, s], ALU.mult))
                ch(dve.tensor_tensor(KR[:, 0, s], RTMP[:, 0, :], RTMP[:, 1, :], ALU.subtract))

            dve.wait_ge(c_in2, 48)
            with dve.Fori(0, RH) as h:
                for s in range(RET_SLOTS):
                    j, c = divmod(s, NC)
                    n = 8 + 8 * h + j
                    if c == 0:
                        wlo_block(n + 1, (j + 1) % 2)
                    for i in range(NC):
                        if s == R_NORM[i]:
                            norm_sum(R, h, i, RD)
                        if s == R_NORM[i] + 1:
                            gated(R, h, i, 2, QX[:, :, i * CH:(i + 1) * CH])
                    if s in (0, 1, 3):
                        if s == 0:
                            dve.wait_ge(R.in_[0], 16 * h + 16)
                            dve.wait_ge(R.in_[3], 16 * h + 16)
                        rotate_q(h, min(s, 2))
                    if s == 4:
                        dve.wait_ge(R.in_[1], 16 * h + 16)
                        for c in range(NC):
                            rotate_k0(c)
                        dve.sem_inc(R.q_ok, 1)
                    for t in range(NT):
                        if s == RA + t:
                            dve.wait_ge(R.sc, 9 * h + t + 1)
                            dve.wait_ge(R.st_full, 16 * h + (t if t >= 2 else 1))
                            dve.tensor_tensor(ATT[t % 2][:, :], PSC[:, 0:P], DM[:, t // NTP, :], ALU.mult).then_inc(R.att, 1)
                        if s == RA + 1 + t and t < NT - 1:
                            dve.wait_ge(R.st_full, 16 * h + t + 2)
                            pst = PST[:, :].rearrange("p (d e) -> p d e", d=2)
                            if t == 0:
                                dve.wait_ge(R.sr_st, 16 * h + 16)
                                dve.tensor_copy(SR[:, :, :], pst).then_inc(R.st_ev, 1)
                            else:
                                dve.wait_ge(R.st_ev, 16 * h + t + 1)
                                dve.scalar_tensor_tensor(SR[:, :, :], SR[:, :, :], G128, pst, ALU.mult, ALU.add)\
                                   .then_inc(R.st_ev, 1)
                        if s == RA + 1 + t and t == NT - 1:
                            dve.wait_ge(R.s8_in[0], 32 * h + 32)
                            dve.wait_ge(R.s8_in[1], 32 * h + 32)
                            for b in range(NS):
                                st = S8A[:, b, :, :] if b < 4 else S8B[:, b - 4, :, :]
                                dve.wait_ge(R.st_full, 16 * h + b + 10)
                                dve.scalar_tensor_tensor(st, st, G16, (PST, PRB)[b % 2][:, :].rearrange(
                                    "p (d e) -> p d e", d=2), ALU.mult, ALU.add).then_inc(R.st_ev, 1)
                ch.reset()

            def prep_q(h, c, part):
                s = slice(c * CH, (c + 1) * CH)
                if part == 0:
                    ch(dve.tensor_copy(PP[:, s], FG[:, s]))
                for l in (range(0, 3), range(3, LEV))[part]:
                    w = 1 << l
                    n = CH if l < LEVS or c < NC - 1 else CH - P
                    v = lambda x: x[:, c * CH:c * CH + n].rearrange("p (g a w) -> p g a w", a=2, w=w)
                    q = QE[c % 2][:, l, 0:n // 2].rearrange("p (g w) -> p g w", w=w)
                    pp = v(PP)
                    dve.tensor_tensor(q, v(HZ[0])[:, :, 1, :], pp[:, :, 1, :], ALU.mult)
                    ch(dve.tensor_tensor(pp[:, :, 1, :], pp[:, :, 1, :],
                                         pp[:, :, 0, w - 1:w].to_broadcast([P, n // (2 * w), w]), ALU.mult))
                if part == 1:
                    ch(dve.tensor_tensor(QP[:, s], HZ[0][:, s], PP[:, s], ALU.mult))
                    dve.sem_inc(H.q_ok, 1)

            def weights(h, t):
                dve.wait_ge(H.sc, 9 * h + t + 1)
                dve.wait_ge(H.st_full, 10 * h + (t if t >= 2 else 1))
                dve.wait_ge(H.kv, 9 * h + t + 2)
                at = ATT[t % 2]
                ch(dve.tensor_tensor(at[:, :], PSC[:, 0:P], ident[:, :], ALU.mult))
                for l in range(LEV if t < NT - 1 else LEVS):
                    w = 1 << l
                    src = PSC[:, P + 64 * l:P + 64 * (l + 1)] if l < 6 else PT[:, 2 * P:2 * P + 64]
                    g = lambda x: x.rearrange("p (g w) -> p g w", w=w)
                    last = dve.copy_predicated(at[:, :].rearrange("p (g a w) -> p g a w", a=2, w=w)[:, :, 1, :],
                                               g(MK[:, l, :]), g(src))
                    if l < (LEV if t < NT - 1 else LEVS) - 1:
                        ch(last)
                last.then_inc(H.att, 1)

            def forget(h):
                dve.wait_ge(H.f_ok, h + 1)
                ch(dve.tensor_scalar(FG[:, :], FG[:, :], LBC[:, 1, bass.ds(h, 1)], LBC[:, 0, bass.ds(h, 1)],
                                     ALU.mult, ALU.add))
                ch(dve.tensor_scalar(KK[:, :], FG[:, :], -1.0, 1.0, ALU.mult, ALU.add))
                dve.sem_inc(H.fk, 1)
                dve.wait_ge(H.in_[0], 16 * h + 16)

            def piece(i):
                dve.wait_ge(sp_hi, i + 1)
                c, k = divmod(i % (3 * KT), KT)
                cs = slice(c * CH, (c + 1) * CH)
                src = UA[c][k] if i < 3 * KT else UR1[:, k, cs]
                dve.tensor_tensor(XL[:, k, cs], src, plain(XH[:, k, cs]), ALU.subtract).then_inc(sp_lo, 1)

            def hg_pair(i, final):
                for u in range(2):
                    h = 2 * i + u
                    end = final and u == 1
                    for s in range(HG_SLOTS):
                        j, c = divmod(s, NC)
                        jj = HG_BLOCKS * u + j
                        n = 40 + 10 * i + jj
                        if c == 0 and jj:
                            wlo_block(n + 1, (jj + 1) % 2)
                        for x in range(NC):
                            if s == H_NORM[x]:
                                norm_sum(H, h, x, HD)
                            if s == H_NORM[x] + 1:
                                gated(H, h, x, 1, OH[:, x * CH:(x + 1) * CH].unsqueeze(1))
                        if s in (0, 1, 6, 7):
                            if s == 6:
                                dve.wait_ge(H.sc, 9 * h + 3)
                            prep_q(h, 1 + s // 6, s % 6)
                        if s >= HA and s - HA < NT:
                            weights(h, s - HA)
                        if s > HA and s - HA - 1 < NT:
                            t = s - HA - 1
                            if t < NT - 1:
                                dve.wait_ge(H.st_full, 10 * h + t + 2)
                                if t == 0:
                                    dve.wait_ge(H.sr_st, 16 * h + 16)
                                    dve.tensor_copy(SH[:, :], PST[:, 0:P]).then_inc(H.st_ev, 1)
                                else:
                                    dve.wait_ge(H.st_ev, 16 * h + t + 1)
                                    e = (t + 1) * P - 1
                                    dve.scalar_tensor_tensor(SH[:, :], SH[:, :], PP[:, e:e + 1], PST[:, 0:P],
                                                             ALU.mult, ALU.add).then_inc(H.st_ev, 1)
                            else:
                                dve.wait_ge(H.s8_in[0], 16 * h + 16)
                                for b in range(NS):
                                    e = TP + (b + 1) * TS - 1
                                    if b % 4 == 0:
                                        dve.wait_ge(H.st_full, 10 * h + b // 4 + 10)
                                    dve.scalar_tensor_tensor(SH8[:, b, :], SH8[:, b, :], PP[:, e:e + 1],
                                                             (PST, PRB)[b // 4][:, b % 4 * P:(b % 4 + 1) * P], ALU.mult, ALU.add).then_inc(H.st_ev, 1)
                        if s >= HG_SLOTS - 2 and not end:
                            if s == HG_SLOTS - 2:
                                forget(h + 1)
                            prep_q(h + 1, 0, s - HG_SLOTS + 2)
                        if end and s >= HG_SLOTS - 2:
                            for x in range(KT):
                                piece(KT * (s - HG_SLOTS + 2) + x)
                    ch.reset()
                if final:
                    for x in range(KT):
                        piece(2 * KT + x)
                else:
                    wlo_block(51 + 10 * i, 1)

            ret_done(dve)
            wlo_block(41, 1)
            forget(0)
            prep_q(0, 0, 0)
            prep_q(0, 0, 1)
            ch.reset()
            with dve.Fori(0, HH // 2 - 1) as i:
                hg_pair(i, False)
            hg_pair(HH // 2 - 1, True)

            def split_next(n):
                w, p = w_item(n + 1), (n + 1) % 2
                wlo(w, as_block(WRAW[w % 2]), WHI[p][:, :, :], WLO[p][:, :, :])

            split_next(NRB)
            hg_done(dve)
            for k in range(2 * KT):
                n = NRB + k
                dve.wait_ge(mg_ok, k + 1)
                if k >= KT:
                    w = w_row(k - KT)
                    wlo(w, WRAW[w % 2][:, :], WOH[:, k - KT, :], WOL[:, k - KT, :])
                if 0 < k < 2 * KT - 1:
                    split_next(n)
                for c in range(NC):
                    s = slice(c * CH, (c + 1) * CH)
                    dve.wait_ge(mm, NC * n + c + 1)
                    if k < KT:
                        dve.tensor_tensor(MIX[:, k, s], psum[c][:, 0:CH], MG[k % 2][:, s], ALU.mult).then_inc(ev, 1)
                    else:
                        ch(dve.tensor_tensor(MG[k % 2][:, s], psum[c][:, 0:CH], MG[k % 2][:, s], ALU.mult))
                        dve.tensor_tensor(MIX[:, k - KT, s], MIX[:, k - KT, s], MG[k % 2][:, s], ALU.add).then_inc(ev, 1)
                    if k == KT - 1:
                        for x in range(KT):
                            piece(3 * KT + KT * c + x)
                    if k == 2 * KT - 1:
                        for x in range(KT):
                            dve.wait_ge(sp_hi, 6 * KT + KT * c + x + 1)
                            dve.tensor_tensor(XL[:, x, s], MIX[:, x, s], plain(XH[:, x, s]), ALU.subtract).then_inc(sp_lo, 1)
            dve.wait_ge(gb_in, 16)
            for t in range(NT + 2):
                if t < NT:
                    dve.wait_ge(d_ss, t + 1)
                    ch(dve.tensor_tensor(dss[:, 2 * t:2 * t + 1], dss[:, 2 * t:2 * t + 1], dss[:, 2 * t + 1:2 * t + 2], ALU.add))
                    dve.tensor_scalar(dms[:, t:t + 1], dss[:, 2 * t:2 * t + 1], 1.0 / D, EPS, ALU.mult, ALU.add).then_inc(d_ms, 1)
                    dve.wait_ge(d_rs, t + 1)
                    if t >= 2:
                        dve.wait_ge(x1_st[t % 2], 16 * (t // 2))
                    dve.wait_ge(xi_in[t % 2], 16 * (t // 2 + 1))
                    for q in range(2):
                        ns = slice(512 * q, 512 * (q + 1))
                        ch(dve.scalar_tensor_tensor(X1R[t % 2][:, ns], row_bank(t, q)[:, :], drs[:, t:t + 1],
                                                    GB[:, ns], ALU.mult, ALU.mult))
                    dve.tensor_tensor(X1R[t % 2][:, :], X1R[t % 2][:, :], XI2[t % 2][:, :], ALU.add).then_inc(d_x1, 1)
                if 1 <= t <= NT:
                    tt = NT + t - 1
                    norm_ms(tt)
                    norm_row(tt, X1R[(t - 1) % 2], HR2[tt % 2])
                if t == 3:
                    wlo_block(W_FFN, 0)
                if t >= 2:
                    norm_cols(NT + t - 2, TM2, 1, t - 2)
            ch.reset()
            NG = FF // 512
            dve.sem_inc(dn_ev, 1)

            def finish(t):
                dve.wait_ge(y_ss, t + 1)
                dve.tensor_scalar(yms[:, t:t + 1], yss[:, t:t + 1], 1.0 / D, EPS, ALU.mult, ALU.add).then_inc(y_ms, 1)
                dve.wait_ge(y_rs, t + 1)
                if t >= 2:
                    dve.wait_ge(y_st[t % 2], 16 * (t // 2))
                dve.wait_ge(x1_in[t % 2], 16 * (t // 2 + 1))
                dve.wait_ge(gb_in, 32)
                ch(dve.scalar_tensor_tensor(OF[t % 2][:, :], ACC[:, t, :], yrs[:, t:t + 1], GF[:, :], ALU.mult, ALU.mult))
                dve.tensor_tensor(OF[t % 2][:, :], OF[t % 2][:, :], X1F[t % 2][:, :], ALU.add).then_inc(y_ok, 1)

            def mlp(g, last):
                w0 = W_FFN + 1 + 8 * g

                def split(i):
                    q = (W_FFN + 1 + i) % 2
                    if i % 2 == 0:
                        wlo(w0 + i, WRAW[q][:, :], WDH[:, i // 2, :], WDL[:, i // 2, :])
                    else:
                        b = (i // 2 + 1) % 4
                        wlo(w0 + i, as_block(WRAW[q]), WHI[b % 2][:, :, :], WLO[b % 2][:, :, :])
                for b in range(4):
                    for c in range(NC):
                        if c == 0:
                            split(2 * b)
                        if c == 1 and b < 3:
                            split(2 * b + 1)
                        x = NC * b + c
                        dve.wait_ge(f_t1, 12 * g + x + 1)
                        if x >= 2:
                            dve.wait_ge(f_ul, 12 * g + x - 1)
                        dve.tensor_tensor(T2[x % 2][:, :], T1[x % 2][:, :], T1[x % 2][:, :], ALU.mult).then_inc(f_t2, 1)
                        dve.wait_ge(f_uh, 12 * g + x + 1)
                        us_ = slice(c * CH, (c + 1) * CH)
                        dve.tensor_tensor(UL[:, b, us_], T2[x % 2][:, :], plain(UH[:, b, us_]), ALU.subtract).then_inc(f_ul, 1)
                if not last:
                    split(7)
                dve.wait_ge(acc0, 1)
                for x in range(2 * NT):
                    t, q = divmod(x, 2)
                    ns = slice(512 * q, 512 * (q + 1))
                    dve.wait_ge(dn, 18 * g + x + 2)
                    dve.tensor_tensor(ACC[:, t, ns], ACC[:, t, ns], psum[3 + x % 5][:, :], ALU.add).then_inc(dn_ev, 1)
                    if last and q and t:
                        finish(t - 1)
            with dve.Fori(0, NG - 1) as g:
                mlp(g, False)
            mlp(NG - 1, True)
            finish(NT - 1)

        @block.gpsimd
        def _(pool):
            ch = Chain(pool, pool_ch)
            ch(pool.memset(mhalf[:, :], -0.5))

            def rsqrt(dst, src, n=1):
                e = mhalf[:, :] if n == 1 else mhalf[:, :].to_broadcast([P, n])
                return pool.tensor_tensor(dst, src, e, ALU.pow)

            for tt in range(NT):
                pool.wait_ge(n_ms, tt + 1)
                rsqrt(rsc[:, tt:tt + 1], msc[:, tt:tt + 1]).then_inc(n_rs, 1)
            ch.reset()

            def gate(K, h, c, ne, g):
                pool.wait_ge(K.sg, 3 * h + c + 1)
                pool.tensor_tensor(SG[:, 0:ne, :], SG[:, 0:ne, :], g, ALU.mult).then_inc(K.gt, 1)
                pool.wait_ge(K.ms, 3 * h + c + 2)
                if c:
                    pool.wait_ge(K.dg, 3 * h + c)
                rsqrt(RST[:, :], MS[:, :], TPC).then_inc(K.rs, 1)

            pool.wait_ge(c_in2, 48)
            with pool.Fori(0, RH) as h:
                pool.wait_ge(R.in_[1], 16 * h + 16)
                pool.wait_ge(R.att, 9 * h + 1)
                for c in range(NC):
                    s = slice(c * CH, (c + 1) * CH)
                    cs, sn = CS[:, 0, s], CS[:, 1, s]
                    pool.tensor_tensor(PTMP[:, 0, :], ZK[:, 0, s], sn, ALU.mult)
                    ch(pool.tensor_tensor(PTMP[:, 1, :], ZK[:, 1, s], cs, ALU.mult))
                    last = pool.tensor_tensor(KR[:, 1, s], PTMP[:, 0, :], PTMP[:, 1, :], ALU.add)
                    if c < NC - 1:
                        ch(last)
                last.then_inc(R.k_ok, 1)
                for c in range(NC):
                    gate(R, h, c, 2, ZG[c % 2][:, :, :])
                ch.reset()

            ret_mixed(pool)
            for i in range(2):
                ch(pool.memset(KE[i][:, :, :], 0.0))
            ret_done(pool)
            ch.reset()

            def prep_k(h, c):
                s = slice(c * CH, (c + 1) * CH)
                off, tot = 0, FG[:, s]
                pool.tensor_tensor(FT[:, 0:CH // 2], FG[:, c * CH:(c + 1) * CH:2], FG[:, c * CH + 1:(c + 1) * CH:2], ALU.mult)
                ch(pool.memset(RR[:, s], 1.0))
                for l in range(LEV):
                    w = 1 << l
                    n = CH if l < LEVS or c < NC - 1 else CH - P
                    v = lambda x: x[:, 0:n].rearrange("p (g a w) -> p g a w", a=2, w=w)
                    pairs = tot[:, 0:n // w].rearrange("p (g a) -> p g a", a=2)
                    rr = v(RR[:, s])
                    pool.tensor_tensor(v(KE[c % 2][:, l, :])[:, :, 0, :], v(KK[:, s])[:, :, 0, :], rr[:, :, 0, :], ALU.mult)
                    if l < LEV - 1:
                        nxt = FT[:, off:off + n // (2 * w)]
                        if l:
                            pool.tensor_tensor(nxt, pairs[:, :, 0], pairs[:, :, 1], ALU.mult)
                        off += n // (2 * w)
                    ch(pool.tensor_tensor(rr[:, :, 0, :], rr[:, :, 0, :],
                                          pairs[:, :, 1:2].to_broadcast([P, n // (2 * w), w]), ALU.mult))
                    tot = nxt
                ch(pool.tensor_tensor(KRH[:, s], KK[:, s], RR[:, s], ALU.mult))
                pool.sem_inc(H.k_ok, 1)

            def hg_head(h, last):
                prep_k(h, 1)
                pool.wait_ge(H.att, 9 * h + 4)
                prep_k(h, 2)
                for c in range(NC):
                    gate(H, h, c, 1, HZ[3][:, c * CH:(c + 1) * CH].unsqueeze(1))
                if not last:
                    pool.wait_ge(H.fk, h + 2)
                    pool.wait_ge(H.att, 9 * h + 10)
                    prep_k(h + 1, 0)
                ch.reset()

            pool.wait_ge(H.fk, 1)
            prep_k(0, 0)
            ch.reset()
            with pool.Fori(0, HH - 1) as h:
                hg_head(h, False)
            hg_head(HH - 1, True)

            for t in range(NT + 1):
                if t < NT:
                    pool.wait_ge(d_ms, t + 1)
                    rsqrt(drs[:, t:t + 1], dms[:, t:t + 1]).then_inc(d_rs, 1)
                if t >= 1:
                    tt = NT + t - 1
                    pool.wait_ge(n_ms, tt + 1)
                    rsqrt(rsc[:, tt:tt + 1], msc[:, tt:tt + 1]).then_inc(n_rs, 1)
            pool.wait_ge(n_xl, 4 * NT)
            pool.wait_ge(n_xh, 4 * NT)
            for i in range(2):
                pool.wait_ge(x1_st[i], 16 * ((NT + 1 - i) // 2))
            pool.memset(ACC[:, :, :], 0.0).then_inc(acc0, 1)
            for t in range(NT):
                pool.wait_ge(y_ms, t + 1)
                rsqrt(yrs[:, t:t + 1], yms[:, t:t + 1]).then_inc(y_rs, 1)


_INS = ["x_prompt", "x_sample", "state_ret", "state_hgrn", "w_in", "w_a", "w_b", "w_out", "w_up", "w_down",
        "g_post_mix", "g_post_ffn"]
_OUTS = [("y_p", (1, TP, D)), ("y_s", (NS, TS, D)), ("ret_p", (1, 1, RH, RD, RD)), ("hg_p", (1, 1, HH, HD, HD)),
         ("ret_s", (1, NS, RH, RD, RD)), ("hg_s", (1, NS, HH, HD, HD))]


def shape_tables(np):
    f = np.float32
    inv = (f(10000.0) ** (-np.arange(0, RD, 2, dtype=f) / f(RD))).astype(f)
    pos = np.concatenate([np.arange(TP), PAST + np.arange(NS * TS) % TS]).astype(f)
    ang = (inv[:, None] * pos[None, :]).astype(f)
    rope = np.stack([np.cos(ang), np.sin(ang)], axis=1).astype(f)
    gam = np.log(1.0 - np.exp(np.linspace(np.log(1.0 / 32), np.log(1.0 / 512), RH))).astype(f).astype(np.float64)
    i = np.arange(P)
    ret = np.zeros((RH, P, 4 * P + 12), f)
    for h in range(RH):
        lg = gam[h]
        ret[h, :, 0:P] = np.exp((i + 1) * lg)[None]
        ret[h, :, P:2 * P] = np.exp((i % TS + 1) * lg)[None]
        m, n = i[:, None], i[None, :]
        ret[h, :, 2 * P:3 * P] = np.where(m // 64 <= n // 64, np.exp(np.abs(n - m) * lg), 0) * RD ** -0.5
        ret[h, :, 3 * P:4 * P] = np.where(m // TS == n // TS, np.exp(np.abs(n - m) * lg), 0) * RD ** -0.5
        ret[h, :, 4 * P] = np.exp((P - 1 - i) * lg) * RD ** -0.5
        ret[h, :, 4 * P + 1] = np.exp(P * lg)
        ret[h, :, 4 * P + 2] = np.exp(TS * lg)
        for b in range(NS):
            ret[h, :, 4 * P + 3 + b] = np.where(i // TS == b, np.exp((TS - 1 - i % TS) * lg), 0) * RD ** -0.5
    mask = np.zeros((P, LEV, 64), np.uint32)
    for l in range(LEV):
        w = 1 << l
        t = np.arange(64) // w * 2 * w + w + np.arange(64) % w
        mask[:, l] = (i[:, None] // w == t[None, :] // w - 1)
    rows = (i[:, None] // TS == np.arange(NS)[None]).astype(f)
    return {"c_rope": rope, "c_ret": ret, "c_mask": mask, "c_rows": rows, "c_ident": np.eye(P, dtype=f)}


def kernel(**inputs):
    import numpy as _np
    import concourse.bacc as _bacc
    from concourse import mybir as _mybir
    from concourse.bass_utils import run_bass_kernel_spmd as _run

    nc = _bacc.Bacc("TRN2", target_bir_lowering=False, num_devices=1)
    data = {n: _np.ascontiguousarray(inputs[n]) for n in _INS}
    data["g_pre_cols"] = _np.ascontiguousarray(
        _np.stack([inputs["g_pre_mix"], inputs["g_pre_ffn"]]).reshape(2, KT, P).transpose(2, 0, 1))
    data["lb_cols"] = _np.ascontiguousarray(_np.asarray(inputs["lb_logits"]).reshape(2, HH, P).transpose(2, 0, 1))
    data.update(shape_tables(_np))
    arrays, a, o = {}, {}, {}
    for name, x in data.items():
        arrays[f"in_{name}"] = x
        a[name] = nc.dram_tensor(f"in_{name}", x.shape, _mybir.dt.from_np(x.dtype), kind="ExternalInput").ap()
    for name, shape in _OUTS:
        o[name] = nc.dram_tensor(f"out_{name}", shape, _mybir.dt.float32, kind="ExternalOutput").ap()
    scr = {n: nc.dram_tensor(f"scratch_{n}", s, _mybir.dt.float32, kind="Internal").ap()
           for n, s in (("z", (80, P, T)), ("u", (16, P, T)), ("x1", (T, D)))}
    program(nc, a, o, scr)
    r = _run(nc, [arrays], core_ids=[0])
    return tuple(r.results[0][f"out_{name}"] for name, _ in _OUTS)
```
